# Optimizing a Trainium2 kernel written in Bass

```python
import math
import jax, jax.numpy as jnp
from jax import lax
import numpy as np

D_MODEL = 2048
BATCH = 1
SEQ = 512
DEPTH = 1

GRID_W = 64
CTX_LEN = 256
EPS = 1e-6
N_MOD = 6

ATTN_HEADS = 8
ATTN_KV_HEADS = 2
HEAD_DIM = 128
ATTN_GROUP = ATTN_HEADS // ATTN_KV_HEADS
Q_BLOCK = 128
ROPE_THETA = 10000.0
ROPE_AXIS_DIM = HEAD_DIM // 2
ROPE_FREQS = ROPE_AXIS_DIM // 2

DN_HEADS = 8
DN_KEY_DIM = 128
DN_VAL_DIM = 128
DN_CONV = 5
DN_CHUNK = 64

ATTN_Q_W = ATTN_HEADS * HEAD_DIM
ATTN_KV_W = ATTN_KV_HEADS * HEAD_DIM
DN_QK_W = DN_HEADS * DN_KEY_DIM
DN_V_W = DN_HEADS * DN_VAL_DIM
DN_CONV_W = 2 * DN_QK_W + DN_V_W
N_BRANCH = 2
IN_SIZES = (ATTN_Q_W, ATTN_KV_W, ATTN_KV_W, DN_CONV_W, DN_V_W, 2 * DN_HEADS, 2 * DN_HEADS, N_BRANCH * D_MODEL)
IN_W = sum(IN_SIZES)

PEER_HEADS = 8
PEER_N_KEYS = 128
PEER_EXPERTS = PEER_N_KEYS * PEER_N_KEYS
PEER_KEY_DIM = 256
PEER_HALF = PEER_KEY_DIM // 2
PEER_TOPK = 16
PEER_BLOCK = 128

kernel_name = 'hybrid_gqa_gdn_peer_dit_block'

def rms_norm(x, w):
    xf = x.astype(jnp.float32)
    y = xf * lax.rsqrt(jnp.mean(xf * xf, axis=-1, keepdims=True) + EPS)
    return (y * w.astype(jnp.float32)).astype(x.dtype)

def split_cols(t, sizes):
    out, start = [], 0
    for s in sizes:
        out.append(t[..., start:start + s])
        start += s
    return out

def l2_normalize(t):
    tf = t.astype(jnp.float32)
    return tf * lax.rsqrt(jnp.sum(tf * tf, axis=-1, keepdims=True) + EPS)

def axial_rope_angles(rows):
    row = jnp.repeat(jnp.arange(rows), GRID_W)
    col = jnp.tile(jnp.arange(GRID_W), rows)
    inv = ROPE_THETA ** (-jnp.arange(ROPE_FREQS, dtype=jnp.float32) / ROPE_FREQS)
    pos = jnp.stack([row, col], axis=-1).astype(jnp.float32)
    ang = pos[:, :, None] * inv
    return jnp.cos(ang), jnp.sin(ang)

def apply_axial_rope(t, cos, sin):
    B, T, H, D = t.shape
    tf = t.astype(jnp.float32).reshape(B, T, H, 2, 2, ROPE_FREQS)
    x1, x2 = tf[..., 0, :], tf[..., 1, :]
    cs, sn = cos[None, :, None], sin[None, :, None]
    out = jnp.stack([x1 * cs - x2 * sn, x2 * cs + x1 * sn], axis=-2)
    return out.reshape(B, T, H, D).astype(t.dtype)

def short_conv(t, w):
    C = t.shape[-1]
    y = lax.conv_general_dilated(t, w[:, None, :].astype(t.dtype), window_strides=(1,), padding='SAME',
                                 dimension_numbers=('NWC', 'WIO', 'NWC'), feature_group_count=C)
    return jax.nn.silu(y)

def block_attention(q, k, v):
    B, T, _, D = q.shape
    n_blk = T // Q_BLOCK
    qb = q.reshape(B, n_blk, Q_BLOCK, ATTN_KV_HEADS, ATTN_GROUP, D).transpose(1, 0, 2, 3, 4, 5)
    scale = D ** -0.5

    def one_block(q_blk):
        s = jnp.einsum('bqhgd,bkhd->bhgqk', q_blk, k, preferred_element_type=jnp.float32) * scale
        p = jax.nn.softmax(s, axis=-1).astype(v.dtype)
        return jnp.einsum('bhgqk,bkhd->bqhgd', p, v)

    o = lax.map(one_block, qb)
    return o.transpose(1, 0, 2, 3, 4, 5).reshape(B, T, ATTN_HEADS * D)

def gated_delta_rule(q, k, v, log_a, beta, state0):
    B, T, H, Dk = q.shape
    C = DN_CHUNK
    N = T // C
    q = q * (Dk ** -0.5)

    def chunks(t):
        return t.reshape(B, N, C, H, -1).transpose(0, 3, 1, 2, 4)

    q, k, v = chunks(q), chunks(k), chunks(v)
    g = jnp.cumsum(log_a.reshape(B, N, C, H).transpose(0, 3, 1, 2), axis=-1)
    bt = beta.reshape(B, N, C, H).transpose(0, 3, 1, 2)
    tri_incl = jnp.tril(jnp.ones((C, C), dtype=bool))
    tri_strict = jnp.tril(jnp.ones((C, C), dtype=bool), -1)
    decay = jnp.exp(jnp.where(tri_incl, g[..., :, None] - g[..., None, :], -jnp.inf))
    kb = k * bt[..., None]
    vb = v * bt[..., None]
    a_mat = jnp.where(tri_strict, jnp.einsum('bhncd,bhnsd->bhncs', kb, k) * decay, 0.0)
    t_mat = a_mat + jnp.eye(C, dtype=a_mat.dtype)
    u = lax.linalg.triangular_solve(t_mat, vb, left_side=True, lower=True, unit_diagonal=True)
    w = lax.linalg.triangular_solve(t_mat, kb * jnp.exp(g)[..., None], left_side=True, lower=True,
                                    unit_diagonal=True)
    qk = jnp.where(tri_incl, jnp.einsum('bhncd,bhnsd->bhncs', q, k) * decay, 0.0)

    def step(S, xs):
        q_c, k_c, u_c, w_c, qk_c, g_c = xs
        v_new = u_c - jnp.einsum('bhcd,bhde->bhce', w_c, S)
        o = jnp.einsum('bhcd,bhde->bhce', q_c * jnp.exp(g_c)[..., None], S) + jnp.einsum('bhcs,bhse->bhce', qk_c, v_new)
        g_last = g_c[..., -1]
        S = S * jnp.exp(g_last)[..., None, None] + jnp.einsum(
            'bhcd,bhce->bhde', k_c * jnp.exp(g_last[..., None] - g_c)[..., None], v_new)
        return S, o

    xs = tuple(jnp.moveaxis(t, 2, 0) for t in (q, k, u, w, qk, g))
    S, o = lax.scan(step, state0, xs)
    o = o.transpose(1, 0, 3, 2, 4).reshape(B, T, H, -1)
    return o, S

def stream_features(h, w_in, q_norm_w, k_norm_w, conv_w, a_log, dt_bias, rope):
    B, T, _ = h.shape
    proj = h @ w_in
    aq, ak, av, dn_qkv, dn_z, dn_b, dn_a, gate_logits = split_cols(proj, IN_SIZES)
    aq = rms_norm(aq.reshape(B, T, ATTN_HEADS, HEAD_DIM), q_norm_w)
    ak = rms_norm(ak.reshape(B, T, ATTN_KV_HEADS, HEAD_DIM), k_norm_w)
    av = av.reshape(B, T, ATTN_KV_HEADS, HEAD_DIM)
    if rope is not None:
        aq = apply_axial_rope(aq, *rope)
        ak = apply_axial_rope(ak, *rope)
    dq, dk, dv = split_cols(short_conv(dn_qkv, conv_w), (DN_QK_W, DN_QK_W, DN_V_W))
    dq = l2_normalize(dq.reshape(B, T, DN_HEADS, DN_KEY_DIM))
    dk = l2_normalize(dk.reshape(B, T, DN_HEADS, DN_KEY_DIM))
    dv = dv.reshape(B, T, DN_HEADS, DN_VAL_DIM).astype(jnp.float32)
    beta = jax.nn.sigmoid(dn_b.astype(jnp.float32)).reshape(B, T, 2, DN_HEADS)
    log_a = -jnp.exp(a_log) * jax.nn.softplus(dn_a.astype(jnp.float32).reshape(B, T, 2, DN_HEADS) + dt_bias)
    return {'aq': aq, 'ak': ak, 'av': av, 'dq': dq, 'dk': dk, 'dv': dv, 'z': dn_z,
            'beta': beta, 'log_a': log_a, 'gates': gate_logits}

def bidirectional_delta(lat, ctx):
    B, _, H, Dk = lat['dq'].shape
    Dv = lat['dv'].shape[-1]
    outs_lat, outs_ctx = [], []
    for d in range(2):
        rev = d == 1

        def prep(f):
            ts = (f['dq'], f['dk'], f['dv'], f['log_a'][:, :, d], f['beta'][:, :, d])
            return tuple(jnp.flip(t, axis=1) for t in ts) if rev else ts

        zero = jnp.zeros((B, H, Dk, Dv), jnp.float32)
        o_c, s_c = gated_delta_rule(*prep(ctx), zero)
        o_l, _ = gated_delta_rule(*prep(lat), s_c)
        outs_lat.append(jnp.flip(o_l, axis=1) if rev else o_l)
        outs_ctx.append(jnp.flip(o_c, axis=1) if rev else o_c)
    return outs_lat[0] + outs_lat[1], outs_ctx[0] + outs_ctx[1]

def merge_branches(o_attn, o_dn, z, gate_logits, dn_norm_w, w_b_attn, w_b_dn, w_out):
    B, T, _ = z.shape
    zf = z.reshape(B, T, DN_HEADS, DN_VAL_DIM).astype(jnp.float32)
    o_dn = (rms_norm(o_dn, dn_norm_w) * jax.nn.silu(zf)).reshape(B, T, DN_V_W).astype(z.dtype)
    g_attn, g_dn = split_cols(jax.nn.sigmoid(gate_logits), (D_MODEL, D_MODEL))
    y = g_attn * (o_attn @ w_b_attn) + g_dn * (o_dn @ w_b_dn)
    return y @ w_out

def peer_ffn(h, w_q, sub_keys, u, v):
    B, T, D = h.shape
    tokens = h.reshape(-1, D)
    n_blk = tokens.shape[0] // PEER_BLOCK

    def one_block(xb):
        nt = xb.shape[0]
        q = (xb @ w_q).reshape(nt, PEER_HEADS, 2, PEER_HALF)
        s = jnp.einsum('thpd,hpkd->thpk', q, sub_keys, preferred_element_type=jnp.float32)
        s_top, i_top = lax.top_k(s, PEER_TOPK)
        cand_s = (s_top[..., 0, :, None] + s_top[..., 1, None, :]).reshape(nt, PEER_HEADS, PEER_TOPK * PEER_TOPK)
        cand_i = (i_top[..., 0, :, None] * PEER_N_KEYS + i_top[..., 1, None, :]).reshape(nt, PEER_HEADS, PEER_TOPK * PEER_TOPK)
        best_s, pos = lax.top_k(cand_s, PEER_TOPK)
        experts = jnp.take_along_axis(cand_i, pos, axis=-1).reshape(nt, PEER_HEADS * PEER_TOPK)
        gates = jax.nn.softmax(best_s, axis=-1).reshape(nt, PEER_HEADS * PEER_TOPK)
        hid = jnp.einsum('ted,td->te', u[experts], xb, preferred_element_type=jnp.float32)
        act = (jax.nn.gelu(hid, approximate=False) * gates).astype(xb.dtype)
        return jnp.einsum('te,ted->td', act, v[experts])

    y = lax.map(one_block, tokens.reshape(n_blk, PEER_BLOCK, D))
    return y.reshape(B, T, D)

def setup_inputs(seed: int = 0) -> dict:
    key = jax.random.key(seed)
    ks = jax.random.split(key, 23)
    f32 = jnp.float32
    D = D_MODEL

    def nrm(k, shape, scale):
        return jax.random.normal(k, shape, f32) * scale

    dt = jnp.exp(jax.random.uniform(ks[13], (DEPTH, 2, DN_HEADS), f32, math.log(1e-3), math.log(1e-1)))
    return {
        'x': nrm(ks[0], (BATCH, SEQ, D), 1.0),
        'c': nrm(ks[1], (BATCH, D), 1.0),
        'ctx': nrm(ks[2], (BATCH, CTX_LEN, D), 1.0),
        'c_ctx': nrm(ks[3], (D,), 1.0),
        'ada_w': nrm(ks[4], (DEPTH, D, N_MOD * D), D ** -0.5),
        'ada_b': nrm(ks[5], (DEPTH, N_MOD * D), 0.02),
        'norm1_w': 1.0 + nrm(ks[6], (DEPTH, D), 0.02),
        'norm2_w': 1.0 + nrm(ks[7], (DEPTH, D), 0.02),
        'w_in': nrm(ks[8], (DEPTH, D, IN_W), D ** -0.5),
        'attn_q_norm': 1.0 + nrm(ks[9], (DEPTH, HEAD_DIM), 0.02),
        'attn_k_norm': 1.0 + nrm(ks[10], (DEPTH, HEAD_DIM), 0.02),
        'dn_conv_w': nrm(ks[11], (DEPTH, DN_CONV, DN_CONV_W), DN_CONV ** -0.5),
        'dn_a_log': jnp.log(jax.random.uniform(ks[12], (DEPTH, 2, DN_HEADS), f32, 1.0, 16.0)),
        'dn_dt_bias': dt + jnp.log(-jnp.expm1(-dt)),
        'dn_norm_w': 1.0 + nrm(ks[14], (DEPTH, DN_VAL_DIM), 0.02),
        'w_branch_attn': nrm(ks[15], (DEPTH, ATTN_Q_W, D), ATTN_Q_W ** -0.5),
        'w_branch_dn': nrm(ks[16], (DEPTH, DN_V_W, D), DN_V_W ** -0.5),
        'w_out': nrm(ks[17], (DEPTH, D, D), D ** -0.5),
        'peer_w_q': nrm(ks[18], (DEPTH, D, PEER_HEADS * PEER_KEY_DIM), D ** -0.5),
        'peer_sub_keys': nrm(ks[19], (DEPTH, PEER_HEADS, 2, PEER_N_KEYS, PEER_HALF), PEER_HALF ** -0.5),
        'peer_u': nrm(ks[20], (DEPTH, PEER_EXPERTS, D), D ** -0.5),
        'peer_v': nrm(ks[21], (DEPTH, PEER_EXPERTS, D), 0.5),
        'final_norm_w': 1.0 + nrm(ks[22], (D,), 0.02),
    }

def reference(x, c, ctx, c_ctx, ada_w, ada_b, norm1_w, norm2_w, w_in, attn_q_norm, attn_k_norm,
              dn_conv_w, dn_a_log, dn_dt_bias, dn_norm_w, w_branch_attn, w_branch_dn, w_out,
              peer_w_q, peer_sub_keys, peer_u, peer_v, final_norm_w):
    ROWS = x.shape[1] // GRID_W
    rope = axial_rope_angles(ROWS)
    silu_c = jax.nn.silu(c)
    silu_cc = jax.nn.silu(c_ctx)
    mod_sizes = (D_MODEL,) * N_MOD
    for layer in range(DEPTH):
        update_ctx = layer < DEPTH - 1
        sh1, sc1, g1, sh2, sc2, g2 = [m[:, None, :] for m in split_cols(silu_c @ ada_w[layer] + ada_b[layer], mod_sizes)]
        csh1, csc1, cg1, csh2, csc2, cg2 = split_cols(silu_cc @ ada_w[layer] + ada_b[layer], mod_sizes)

        h = rms_norm(x, norm1_w[layer]) * (1.0 + sc1) + sh1
        hc = rms_norm(ctx, norm1_w[layer]) * (1.0 + csc1) + csh1
        lat = stream_features(h, w_in[layer], attn_q_norm[layer], attn_k_norm[layer], dn_conv_w[layer],
                              dn_a_log[layer], dn_dt_bias[layer], rope)
        cf = stream_features(hc, w_in[layer], attn_q_norm[layer], attn_k_norm[layer], dn_conv_w[layer],
                             dn_a_log[layer], dn_dt_bias[layer], None)
        k_all = jnp.concatenate([lat['ak'], cf['ak']], axis=1)
        v_all = jnp.concatenate([lat['av'], cf['av']], axis=1)
        o_attn = block_attention(lat['aq'], k_all, v_all)
        o_dn_lat, o_dn_ctx = bidirectional_delta(lat, cf)
        mix = merge_branches(o_attn, o_dn_lat, lat['z'], lat['gates'], dn_norm_w[layer],
                             w_branch_attn[layer], w_branch_dn[layer], w_out[layer])
        x = x + g1 * mix
        if update_ctx:
            o_attn_c = block_attention(cf['aq'], cf['ak'], cf['av'])
            mix_c = merge_branches(o_attn_c, o_dn_ctx, cf['z'], cf['gates'], dn_norm_w[layer],
                                   w_branch_attn[layer], w_branch_dn[layer], w_out[layer])
            ctx = ctx + cg1 * mix_c

        h2 = rms_norm(x, norm2_w[layer]) * (1.0 + sc2) + sh2
        x = x + g2 * peer_ffn(h2, peer_w_q[layer], peer_sub_keys[layer], peer_u[layer], peer_v[layer])
        if update_ctx:
            hc2 = rms_norm(ctx, norm2_w[layer]) * (1.0 + csc2) + csh2
            ctx = ctx + cg2 * peer_ffn(hc2, peer_w_q[layer], peer_sub_keys[layer], peer_u[layer], peer_v[layer])
    return rms_norm(x, final_norm_w)


_drawn_inputs = setup_inputs


def setup_inputs(seed=0):
    import zlib

    import numpy as np

    out = dict(_drawn_inputs(seed))
    spreads = {}
    factors = {'norm1_w': 3.219,
     'attn_q_norm': 8.0,
     'attn_k_norm': 8.0,
     'dn_norm_w': 11.713,
     'final_norm_w': 8.075,
     'norm2_w': 8.0}
    for name, (base, spread) in spreads.items():
        noise = np.random.default_rng([zlib.crc32(name.encode()), seed]).standard_normal(out[name].shape)
        drawn = base * np.exp(spread * noise) if base else spread * noise
        out[name] = __import__('jax').numpy.asarray(drawn.astype(out[name].dtype))
    for name, factor in factors.items():
        out[name] = (out[name] * factor).astype(out[name].dtype)
    return out
```

```python
from contextlib import ExitStack

import numpy as np

import concourse.bass as bass
from concourse import mybir

P = 128
D = 2048
KD = D // P
LAT, CTX = 512, 256
T = LAT + CTX
NT = T // P
CT = CTX // P
LT = LAT // P
N_MOD = 6
EPS = 1e-6
HD = 128
QH, KVH = 8, 2
QGROUP = QH // KVH
GRID_W = 64
ROPE_THETA = 10000.0
DH = 8
CONV = 5
CHUNK = 64
PH = 8
NKEYS = 128
TOPK = 16
CW = 512
G_AQ, G_AK, G_AV = 0, 8, 10
G_DQ, G_DK, G_DV, G_Z = 12, 20, 28, 36
BA0 = 44 * P
G_GATE = 44
GATE0 = BA0 + 32
IN_W = GATE0 + 2 * D
NG = G_GATE + 2 * D // P

F32 = mybir.dt.float32
U32 = mybir.dt.uint32
I32 = mybir.dt.int32
ALU = mybir.AluOpType
ACT = mybir.ActivationFunctionType
AX_X = mybir.AxisListType.X
ds = bass.ds


def constants():
    p = np.arange(P)
    same = p[:, None] // CHUNK == p[None, :] // CHUNK
    row, col = p[:, None], p[None, :]
    c = {"ident": np.eye(P), "ones": np.ones((P, P))}
    c["incl_f"] = same & (col >= row)
    c["incl_b"] = same & (col <= row)
    c["strict_f"] = same & (col < row)
    c["strict_b"] = same & (col > row)
    c["chunk"] = same
    c["half0"] = np.broadcast_to(row < CHUNK, (P, P))
    c["half1"] = np.broadcast_to(row >= CHUNK, (P, P))
    for n in range(6):
        b = 1 << n
        low = (row // b == col // b + 1) & ((row // b) % 2 == 1)
        c[f"level_b{n}"] = low
        c[f"level_f{n}"] = low.T
    half = HD // 4
    rot = np.zeros((P, P))
    for d in range(P):
        if (d // half) % 2 == 0:
            rot[d + half, d] = -1.0
        else:
            rot[d - half, d] = 1.0
    c["rot"] = rot
    t = np.arange(LAT)
    inv = (np.float32(ROPE_THETA) ** (-np.arange(half, dtype=np.float32) / np.float32(half))).astype(np.float32)
    pos = np.stack([t // GRID_W, t % GRID_W]).astype(np.float32)
    ang = pos[p // (2 * half)] * inv[p % half][:, None]
    c["cos"] = np.cos(ang.astype(np.float32))
    c["sin"] = np.sin(ang.astype(np.float32))
    pick = np.zeros((P, 19))
    pick[:, 9] = 1.0
    c["pick"] = pick
    rows = np.zeros((P, 10 * P))
    for h in range(10):
        rows[h, h * P:(h + 1) * P] = 1.0
    c["rows"] = rows
    c["iota16"] = np.broadcast_to(np.arange(16), (P, 16))
    return {k: np.ascontiguousarray(v, dtype=np.float32) for k, v in c.items()}


ATTENTION_ONLY = ("rot", "cos", "sin", "pick", "rows")
CONST_AT = {}
_widths = {n: a.shape[1] for n, a in constants().items()}
_at = 0
for _name in [n for n in _widths if n not in ATTENTION_ONLY] + list(ATTENTION_ONLY):
    CONST_AT[_name] = (_at, _widths[_name])
    _at += _widths[_name]
CONST_ALL = _at
CONST_W = CONST_AT[ATTENTION_ONLY[0]][0]


class Count:

    def __init__(self):
        self.n, self.over = 0, 0

    def up(self, k=1):
        self.n += k
        return self.over + self.n

    def enter(self, i, per_turn):
        self.start, self.per, self.over = self.n, per_turn, self.over + i * per_turn

    def leave(self, turns):
        assert self.n - self.start == self.per, (self.n - self.start, self.per)
        self.n, self.over = self.start + turns * self.per, 0


class Kernel:

    def __init__(self, nc, stack, inputs, consts, out):
        self.nc, self.stack, self.inp, self.consts, self.out = nc, stack, inputs, consts, out
        self.held = stack.enter_context(nc.semaphore("held"))
        self.sems = []
        dram = lambda name, shape: nc.dram_tensor(name, shape, F32, kind="Internal").ap()
        self.mod_d = dram("mod_rows", (2, N_MOD * D))
        self.feat_d = dram("features", (NG, P, T))
        self.h2_d = dram("h2_rows", (LT, P, D))
        self.psum = stack.enter_context(nc.psum_tensor("psum", [P, 8, 512], F32))

    def sem(self, name):
        self.sems.append(self.nc.alloc_semaphore(name))
        return self.sems[-1]

    def give_back_semaphores(self):
        self.nc.clear_and_free_semaphores(self.sems)
        self.nc.all_engine_barrier()
        self.sems = []


def sbuf(k, stack, name, shape, dtype=F32):
    return stack.enter_context(k.nc.sbuf_tensor(name, shape, dtype))


def load_consts(k):
    k.c = {}
    nc = k.nc
    names = list(CONST_AT)
    k.const_sb = sbuf(k, k.stack, "const_sb", [P, CONST_W])
    for name in names:
        a, n = CONST_AT[name]
        if name in ATTENTION_ONLY:
            continue
        k.c[name] = k.const_sb[:, a:a + n]


def turns(eng, n, body):
    body(0)
    if n > 1:
        with eng.Fori(1, n) as i:
            body(i)


def hold(k, eng, sem, value):
    eng.wait_ge(sem, value)
    eng.sem_inc(k.held, 1)


def rsqrt_steps(k, dve, act, ms, tmp, r, ms_ready, root_ready, step, st):
    if act is not None:
        act.wait_ge(*ms_ready)
        k.nc.scalar.activation(tmp, ms, ACT.Sqrt).then_inc(root_ready[0], 1)
    if dve is not None:
        dve.wait_ge(*root_ready)
        k.nc.vector.reciprocal(r, tmp).then_inc(step, 1)
        dve.wait_ge(step, st.up())
        k.nc.vector.tensor_tensor(tmp, r, r, ALU.mult).then_inc(step, 1)
        dve.wait_ge(step, st.up())
        k.nc.vector.scalar_tensor_tensor(out=tmp, in0=ms, scalar=-0.5, in1=tmp, op0=ALU.mult, op1=ALU.mult).then_inc(step, 1)
        dve.wait_ge(step, st.up())
        k.nc.vector.scalar_tensor_tensor(out=r, in0=tmp, scalar=1.5, in1=r, op0=ALU.add, op1=ALU.mult).then_inc(step, 1)
        dve.wait_ge(step, st.up())


def modulation(k, xn):
    nc, ps = k.nc, k.psum
    NCH = N_MOD * D // CW
    with ExitStack() as s:
        w = sbuf(k, s, "ada_chunk", [P, 2, KD, CW])
        bias = sbuf(k, s, "ada_bias", [2, 2, CW])
        row = sbuf(k, s, "mod_row", [2, 2, CW])
        raw = sbuf(k, s, "cond_raw", [P, 2, KD])
        sc = sbuf(k, s, "cond_silu", [P, KD, 2])
        junk = sbuf(k, s, "norm_squares", [P, D])
        ss = sbuf(k, s, "norm_sums", [P, 3, NT])
        cond_in, x_in, consts_in = k.sem("cond_in"), k.sem("x_in"), k.sem("consts_in")
        w_in = [k.sem("ada_in0"), k.sem("ada_in1")]
        silu_done, mod_done, row_done = k.sem("silu_done"), k.sem("mod_done"), k.sem("row_done")
        row_out = [k.sem("row_out0"), k.sem("row_out1")]
        sums_done, ms_done, root_done = k.sem("sums_done"), k.sem("ms_done"), k.sem("root_done")
        step = k.sem("mod_dve_step")
        aw = k.inp["ada_w"].rearrange("a (p k) n -> (a p) k n", k=KD)
        ab = k.inp["ada_b"]
        with nc.Block() as block:

            @block.sync
            def _(sp):
                sp.dma_start(raw[:, 0, :], k.inp["c"].rearrange("a (p k) -> (a p) k", k=KD)).then_inc(cond_in, 16)
                sp.dma_start(raw[:, 1, :], k.inp["c_ctx"].rearrange("(p k) -> p k", k=KD)).then_inc(cond_in, 16)

                def load(b, j):
                    sp.dma_start(w[:, b], aw[:, :, ds(j * CW, CW)]).then_inc(w_in[b], 16)
                    sp.dma_start(bias[:, b], ab[:, ds(j * CW, CW)].to_broadcast([2, CW])).then_inc(w_in[b], 16)

                for b in range(2):
                    load(b, b)
                with sp.Fori(0, NCH // 2 - 1) as i:
                    for b in range(2):
                        sp.wait_ge(row_done, 2 * i + b + 1)
                        load(b, 2 * i + b + 2)

            @block.tensor
            def _(pe):
                pe.wait_ge(silu_done, 1)

                def products(i):
                    for b in range(2):
                        pe.wait_ge(w_in[b], 32 * i + 32)
                        if not isinstance(i, int):
                            pe.wait_ge(row_done, 2 * i + b - 1)
                        for kk in range(KD):
                            mm = nc.tensor.matmul(ps[0:2, b, :], sc[:, kk, :], w[:, b, kk, :], start=kk == 0, stop=kk == KD - 1)
                        mm.then_inc(mod_done, 1)

                turns(pe, NCH // 2, products)

            @block.scalar
            def _(act):
                act.wait_ge(cond_in, 32)
                nc.scalar.activation(sc[:, :, :].rearrange("p k a -> p a k"), raw[:, :, :], ACT.Silu).then_inc(silu_done, 1)
                act.dma_start(k.const_sb[:, :], k.consts[:, 0:CONST_W]).then_inc(consts_in, 16)
                act.dma_start(xn[:, 0:CT, :], k.inp["ctx"].rearrange("a (t p) d -> p (a t) d", p=P)).then_inc(x_in, 16)
                act.dma_start(xn[:, CT:NT, :], k.inp["x"].rearrange("a (t p) d -> p (a t) d", p=P)).then_inc(x_in, 16)
                act.wait_ge(x_in, 32)
                for t in range(NT):
                    if t:
                        act.wait_ge(sums_done, t)
                    nc.scalar.activation(junk[:, :], xn[:, t, :], ACT.Square, accum_out=ss[:, 0, t:t + 1]).then_inc(sums_done, 1)
                rsqrt_steps(k, None, act, ss[:, 0, :], ss[:, 1, :], None, (ms_done, 1), (root_done, 1), None, None)
                act.wait_ge(consts_in, 16)

            @block.vector
            def _(dve):
                st = Count()
                dve.wait_ge(sums_done, NT)
                nc.vector.tensor_scalar(ss[:, 0, :], ss[:, 0, :], 1.0 / D, EPS, ALU.mult, ALU.add).then_inc(ms_done, 1)
                rsqrt_steps(k, dve, None, ss[:, 0, :], ss[:, 1, :], ss[:, 2, :], None, (root_done, 1), step, st)
                for t in range(NT):
                    nc.vector.tensor_scalar(xn[:, t, :], xn[:, t, :], ss[:, 2, t:t + 1], None, ALU.mult)

                def add_bias(i):
                    for b in range(2):
                        dve.wait_ge(mod_done, 2 * i + b + 1)
                        if not isinstance(i, int):
                            dve.wait_ge(row_out[b], 16 * i)
                        nc.vector.tensor_tensor(row[:, b, :], ps[0:2, b, :], bias[:, b, :], ALU.add).then_inc(row_done, 1)

                turns(dve, NCH // 2, add_bias)

            @block.gpsimd
            def _(pool):
                with pool.Fori(0, NCH // 2) as i:
                    for b in range(2):
                        pool.wait_ge(row_done, 2 * i + b + 1)
                        pool.dma_start(k.mod_d[:, ds((2 * i + b) * CW, CW)], row[:, b, :]).then_inc(row_out[b], 16)
                for b in range(2):
                    pool.wait_ge(row_out[b], 16 * NCH // 2)


def turn(k, xn, hT):
    nc, ps = k.nc, k.psum
    with ExitStack() as s:
        modc = sbuf(k, s, "mod_cols", [P, 2, 2, KD])
        nw = sbuf(k, s, "norm1_cols", [P, KD])
        scale = sbuf(k, s, "scale_cols", [P, 2, KD])
        mod_in, scale_done, turned, taken = k.sem("mod_cols_in"), k.sem("scale_done"), k.sem("turned"), k.sem("taken")
        with nc.Block() as block:

            @block.sync
            def _(sp):
                for a in range(2):
                    sp.dma_start(modc[:, a], k.mod_d[a:a + 1, 0:2 * D].rearrange("a (s p k) -> (a p) s k", s=2, k=KD)).then_inc(mod_in, 16)
                sp.dma_start(nw[:, :], k.inp["norm1_w"].rearrange("a (p k) -> (a p) k", k=KD)).then_inc(mod_in, 16)

            @block.tensor
            def _(pe):
                for kk in range(KD):
                    slot = kk % 4
                    if kk >= 4:
                        pe.wait_ge(taken, 2 * (kk - 3))
                    for t in range(NT):
                        bank, col = (2 * slot, t * P) if t < CT else (2 * slot + 1, (t - CT) * P)
                        tr = nc.tensor.transpose(ps[:, bank, col:col + P], xn[:, t, kk:D:KD], k.c["ident"])
                    tr.then_inc(turned, 1)

            @block.vector
            def _(dve):
                dve.wait_ge(mod_in, 48)
                for a in range(2):
                    nc.vector.scalar_tensor_tensor(out=scale[:, a, :], in0=modc[:, a, 1, :], scalar=1.0, in1=nw[:, :], op0=ALU.add, op1=ALU.mult).then_inc(scale_done, 1)
                dve.wait_ge(scale_done, 2)
                for kk in range(KD):
                    slot = kk % 4
                    dve.wait_ge(turned, kk + 1)
                    for a, cols, bank, n in ((1, slice(0, CTX), 2 * slot, CTX), (0, slice(CTX, T), 2 * slot + 1, LAT)):
                        nc.vector.tensor_scalar(hT[:, kk, cols], ps[:, bank, 0:n], scale[:, a, kk:kk + 1], modc[:, a, 0, kk:kk + 1], ALU.mult, ALU.add).then_inc(taken, 1)


def project(k, hT, ba):
    nc, ps = k.nc, k.psum
    segments = [
        (0, G_AQ, 2, False, "copy"),
        (G_Z * P, G_Z, 2, False, "silu"),
        (G_DQ * P, G_DQ, 2, False, "conv"),
        (G_AK * P, G_AK, 1, True, "copy"),
        (G_DK * P, G_DK, 4, True, "conv"),
        (GATE0, G_GATE, 8, False, "sigmoid"),
    ]
    GC = CW // P
    PADW = 2 + CTX + 4 + LAT + 2
    L0 = CTX + 4
    with ExitStack() as s:
        w = sbuf(k, s, "w_chunk", [P, 2, KD, CW])
        wba = sbuf(k, s, "w_ba", [P, KD, 32])
        pad = sbuf(k, s, "conv_in", [P, 2, PADW])
        y = sbuf(k, s, "conv_out", [P, 2, PADW - 4])
        stage = sbuf(k, s, "stage", [P, 2, T])
        taps_r = sbuf(k, s, "taps_rows", [CONV * 24, P])
        taps = sbuf(k, s, "taps", [P, CONV * 24])
        w_in = [k.sem("w_in0"), k.sem("w_in1")]
        out_st = [k.sem("feat_out0"), k.sem("feat_out1")]
        small_in, group_done, evac_done, conv_done, conv_staged = k.sem("small_in"), k.sem("group_done"), k.sem("evac_done"), k.sem("conv_done"), k.sem("conv_staged")
        pads_zero, taps_turned, taps_done, ba_done, step = k.sem("pads_zero"), k.sem("taps_turned"), k.sem("taps_done"), k.sem("ba_done"), k.sem("proj_dve_step")
        wi = k.inp["w_in"].rearrange("a (p k) n -> (a p) k n", k=KD)

        def walk(eng, body):
            base = 0
            for seg in segments:
                n = seg[2]
                if n >= 4:
                    with eng.Fori(0, n // 2) as i:
                        for b in range(2):
                            body(seg, base + b + 2 * i, b + 2 * i, (base + b) % 2, base + b)
                else:
                    for c in range(n):
                        body(seg, base + c, c, (base + c) % 2, base + c)
                base += n

        def conv_index(seg, cs, j):
            first = sum(GC * x[2] for x in segments[:segments.index(seg)] if x[4] == "conv")
            return first + GC * cs + j

        with nc.Block() as block:

            @block.sync
            def _(sp):
                sp.dma_start(wba[:, :, :], wi[:, :, BA0:BA0 + 32]).then_inc(small_in, 16)
                sp.dma_start(taps_r[:, :], k.inp["dn_conv_w"].rearrange("a j (g p) -> (a j g) p", p=P)).then_inc(small_in, 16)

                def load(seg, c, cs, b, c0):
                    if c0 >= 2:
                        sp.wait_ge(group_done, GC * (c - 1))
                    sp.dma_start(w[:, b], wi[:, :, ds(seg[0] + cs * CW, CW)]).then_inc(w_in[b], 16)

                walk(sp, load)

            @block.tensor
            def _(pe):
                pe.wait_ge(small_in, 32)
                nc.tensor.transpose(ps[:, 4, 0:CONV * 24], taps_r[:, :], k.c["ident"][0:CONV * 24, 0:CONV * 24]).then_inc(taps_turned, 1)
                for t in range(NT):
                    for kk in range(KD):
                        mm = nc.tensor.matmul(ps[:, 5, 32 * t:32 * t + 32], hT[:, kk, t * P:(t + 1) * P], wba[:, kk, :], start=kk == 0, stop=kk == KD - 1)
                mm.then_inc(taps_turned, 1)

                def products(seg, c, cs, b, c0):
                    pe.wait_ge(w_in[b], (c - c0) * 8 + 16 * (c0 // 2 + 1))
                    for j in range(GC):
                        slot = (GC * c0 + j) % 2
                        if GC * c0 + j >= 2:
                            pe.wait_ge(evac_done, GC * c + j - 1)
                        for kk in range(KD):
                            mm = nc.tensor.matmul(ps[:, slot, :], w[:, b, kk, j * P:(j + 1) * P], hT[:, kk, CTX:T], start=kk == 0, stop=kk == KD - 1)
                            if seg[3]:
                                mm = nc.tensor.matmul(ps[:, 2 + slot, 0:CTX], w[:, b, kk, j * P:(j + 1) * P], hT[:, kk, 0:CTX], start=kk == 0, stop=kk == KD - 1)
                        mm.then_inc(group_done, 1)

                walk(pe, products)

            @block.scalar
            def _(act):
                act.wait_ge(pads_zero, 2)
                def evacuate(seg, c, cs, b, c0):
                    func = {"copy": ACT.Copy, "silu": ACT.Silu, "sigmoid": ACT.Sigmoid, "conv": ACT.Copy}[seg[4]]
                    for j in range(GC):
                        g0 = GC * c0 + j
                        slot = g0 % 2
                        act.wait_ge(group_done, GC * c + j + 1)
                        if seg[4] == "conv":
                            cc = conv_index(seg, cs, j)
                            if seg[3]:
                                nc.scalar.activation(pad[:, slot, 2:2 + CTX], ps[:, 2 + slot, 0:CTX], func)
                            nc.scalar.activation(pad[:, slot, L0 + 2:L0 + 2 + LAT], ps[:, slot, :], func).then_inc(evac_done, 1)
                            act.wait_ge(conv_done, cc + 1)
                            if g0 >= 2:
                                act.wait_ge(out_st[slot], 16 * ((g0 // 2)) + (c - c0) * 16 * GC // 2)
                            if seg[3]:
                                nc.scalar.activation(stage[:, slot, 0:CTX], y[:, slot, 0:CTX], ACT.Silu)
                            nc.scalar.activation(stage[:, slot, CTX:T], y[:, slot, L0:L0 + LAT], ACT.Silu).then_inc(conv_staged, 1)
                        else:
                            if g0 >= 2:
                                act.wait_ge(out_st[slot], 16 * ((g0 // 2)) + (c - c0) * 16 * GC // 2)
                            if seg[3]:
                                nc.scalar.activation(stage[:, slot, 0:CTX], ps[:, 2 + slot, 0:CTX], func)
                            nc.scalar.activation(stage[:, slot, CTX:T], ps[:, slot, :], func).then_inc(evac_done, 1)

                walk(act, evacuate)

            @block.vector
            def _(dve):
                for b in range(2):
                    nc.vector.memset(pad[:, b, :], 0.0).then_inc(pads_zero, 1)
                dve.wait_ge(taps_turned, 2)
                nc.vector.tensor_copy(taps[:, :], ps[:, 4, 0:CONV * 24]).then_inc(taps_done, 1)
                nc.vector.tensor_copy(ba[:, :, :], ps[:, 5, 0:32 * NT].rearrange("p (t n) -> p t n", n=32)).then_inc(ba_done, 1)
                dve.wait_ge(taps_done, 1)

                first_conv = GC * sum(x[2] for x in segments[:2])

                def convolve(seg, c, cs, b, c0):
                    if seg[4] != "conv":
                        return
                    lo = 0 if seg[3] else L0
                    for j in range(GC):
                        g0 = GC * c0 + j
                        slot = g0 % 2
                        dve.wait_ge(evac_done, GC * c + j + 1)
                        if conv_index(seg, 0, j) >= 2 or c0 * GC > first_conv:
                            dve.wait_ge(conv_staged, conv_index(seg, cs, j) - 1)
                        out = y[:, slot, lo:PADW - 4]
                        for tap in range(CONV):
                            src = pad[:, slot, lo + tap:PADW - 4 + tap]
                            wt = taps[:, ds(tap * 24 + seg[1] - G_DQ + j + GC * cs, 1)]
                            if tap == 0:
                                ins = nc.vector.tensor_scalar(out, src, wt, None, ALU.mult)
                            else:
                                ins = nc.vector.scalar_tensor_tensor(out=out, in0=src, scalar=wt, in1=out, op0=ALU.mult, op1=ALU.add)
                            if tap < CONV - 1:
                                ins.then_inc(step, 1)
                                dve.wait_ge(step, conv_index(seg, cs, j) * (CONV - 1) + tap + 1)
                            else:
                                ins.then_inc(conv_done, 1)

                walk(dve, convolve)

            @block.gpsimd
            def _(pool):
                def store(seg, c, cs, b, c0):
                    for j in range(GC):
                        slot = (GC * c0 + j) % 2
                        if seg[4] == "conv":
                            pool.wait_ge(conv_staged, conv_index(seg, cs, j) + 1)
                        else:
                            pool.wait_ge(evac_done, GC * c + j + 1)
                        lo = 0 if seg[3] else CTX
                        g = seg[1] + j + GC * cs
                        pool.dma_start(k.feat_d[ds(g, 1), :, lo:T].rearrange("a p t -> (a p) t"), stage[:, slot, lo:T]).then_inc(out_st[slot], 16)

                walk(pool, store)
                chunks = sum(seg[2] for seg in segments)
                for b in range(2):
                    pool.wait_ge(out_st[b], 16 * GC // 2 * chunks)


def attention(k, oT):
    nc, ps = k.nc, k.psum
    NH = QH + KVH
    with ExitStack() as s:
        qk = sbuf(k, s, "qk_raw", [P, NH, T])
        vT = sbuf(k, s, "v_raw", [P, KVH, T])
        vt = sbuf(k, s, "v_tokens", [P, KVH, NT, HD])
        nw = sbuf(k, s, "qk_norm_cols", [P, 2])
        sq = sbuf(k, s, "qk_squares", [P, 2, T])
        ms = sbuf(k, s, "qk_means", [NH, T])
        tmp = sbuf(k, s, "qk_roots", [NH, T])
        rr = sbuf(k, s, "qk_rsqrt", [NH, T])
        side = sbuf(k, s, "rope_cos_part", [P, 2, LAT])
        qs = sbuf(k, s, "q_head", [P, 2, LAT])
        pr = sbuf(k, s, "probs", [P, 2, T])
        pT = sbuf(k, s, "probs_turned", [P, 2, NT, LAT])
        small = sbuf(k, s, "softmax_cols", [P, 2, 4])
        tables = sbuf(k, s, "attention_tables", [P, CONST_ALL - CONST_W])
        for name in ATTENTION_ONLY:
            a, n = CONST_AT[name]
            k.c[name] = tables[:, a - CONST_W:a - CONST_W + n]
        names = ["qkv_in", "squared", "summed", "means_done", "roots_done", "attn_dve_step", "rsqrt_done", "spread", "normed",
                 "rotated", "cos_done", "rope_done", "v_turned", "v_copied", "q_copied", "scores_done", "shift_done", "exp_done",
                 "recip_done", "probs_done", "probs_turned_done", "probs_copied", "o_done", "o_copied", "sin_done"]
        S = {n: k.sem("at_" + n) for n in names}
        with nc.Block() as block:

            @block.sync
            def _(sp):
                for src, dst in (
                    (k.feat_d[G_AQ:G_AQ + QH, :, CTX:T], qk[:, 0:QH, CTX:T]),
                    (k.feat_d[G_AK:G_AK + KVH, :, :], qk[:, QH:NH, :]),
                    (k.feat_d[G_AV:G_AV + KVH, :, :], vT[:, :, :]),
                ):
                    sp.dma_start(dst, src.rearrange("g p t -> p g t")).then_inc(S["qkv_in"], 16)
                sp.dma_start(tables[:, :], k.consts[:, CONST_W:CONST_ALL]).then_inc(S["qkv_in"], 16)
                sp.dma_start(nw[:, 0:1], k.inp["attn_q_norm"].rearrange("a d -> d a")).then_inc(S["qkv_in"], 16)
                sp.dma_start(nw[:, 1:2], k.inp["attn_k_norm"].rearrange("a d -> d a")).then_inc(S["qkv_in"], 16)

            def columns(h):
                return (CTX, T) if h < QH else (0, T)

            def tile_order():
                yield "ahead", 0
                yield "ahead", 1
                for t in range(LT):
                    yield "behind", t
                    if t + 2 < LT:
                        yield "ahead", t + 2

            def heads(eng, body):
                for kv in range(KVH):
                    def turn2(i):
                        for b in range(2):
                            body(kv, kv * QGROUP + 2 * i + b, b)
                    if kv == 0:
                        turns(eng, QGROUP // 2, turn2)
                    else:
                        with eng.Fori(0, QGROUP // 2) as i:
                            turn2(i)

            def first(h):
                return isinstance(h, int) and h < 2

            @block.tensor
            def _(pe):
                pe.wait_ge(S["qkv_in"], 96)
                for h in range(NH):
                    pe.wait_ge(S["squared"], h + 1)
                    pick = k.c["pick"][:, 9 - h:19 - h]
                    mm = nc.tensor.matmul(ps[0:NH, 0, :], pick, sq[:, h % 2, CTX:T], start=h == 0, stop=h == NH - 1)
                    if h >= QH:
                        mm = nc.tensor.matmul(ps[0:NH, 1, 0:CTX], pick, sq[:, h % 2, 0:CTX], start=h == QH, stop=h == NH - 1)
                    mm.then_inc(S["summed"], 1)
                for kv in range(KVH):
                    for t in range(NT):
                        tr = nc.tensor.transpose(ps[:, 2 + 2 * kv + t // 4, (t % 4) * P:(t % 4 + 1) * P], vT[:, kv, t * P:(t + 1) * P], k.c["ident"])
                    tr.then_inc(S["v_turned"], 1)
                pe.wait_ge(S["rsqrt_done"], 1)
                pe.wait_ge(S["v_copied"], KVH)
                for h in range(NH):
                    if h >= 1:
                        pe.wait_ge(S["normed"], h)
                    spread = k.c["rows"][0:NH, h * P:(h + 1) * P]
                    mm = nc.tensor.matmul(ps[:, 2, :], spread, rr[:, CTX:T], start=True, stop=True)
                    if h >= QH:
                        mm = nc.tensor.matmul(ps[:, 3, 0:CTX], spread, rr[:, 0:CTX], start=True, stop=True)
                    mm.then_inc(S["spread"], 1)
                    pe.wait_ge(S["normed"], h + 1)
                    if h >= 2:
                        pe.wait_ge(S["sin_done"], h - 1)
                    nc.tensor.matmul(ps[:, 4 + h % 2, :], k.c["rot"], qk[:, h, CTX:T], start=True, stop=True).then_inc(S["rotated"], 1)
                pe.wait_ge(S["rope_done"], NH)

                def head(kv, h, b):
                    for what, t in tile_order():
                        n = h * LT + t
                        if what == "ahead":
                            if t == 0:
                                pe.wait_ge(S["q_copied"], h + 1)
                            if not (isinstance(n, int) and n < 2):
                                pe.wait_ge(S["exp_done"], n - 1)
                            lhs = qs[:, b, t * P:(t + 1) * P]
                            nc.tensor.matmul(ps[:, 2 * (t % 2), :], lhs, qk[:, QH + kv, 0:512], start=True, stop=True)
                            nc.tensor.matmul(ps[:, 2 * (t % 2) + 1, 0:T - 512], lhs, qk[:, QH + kv, 512:T], start=True, stop=True).then_inc(S["scores_done"], 1)
                        else:
                            pe.wait_ge(S["probs_done"], n + 1)
                            if not (isinstance(n, int) and n < 1):
                                pe.wait_ge(S["probs_copied"], n)
                            for j in range(NT):
                                tr = nc.tensor.transpose(ps[:, 4 + j // 4, (j % 4) * P:(j % 4 + 1) * P], pr[:, t % 2, j * P:(j + 1) * P], k.c["ident"])
                            tr.then_inc(S["probs_turned_done"], 1)
                    pe.wait_ge(S["probs_copied"], h * LT + LT)
                    if not first(h):
                        pe.wait_ge(S["o_copied"], h - 1)
                    for j in range(NT):
                        mm = nc.tensor.matmul(ps[:, 6 + b, :], vt[:, kv, j, :], pT[:, b, j, :], start=j == 0, stop=j == NT - 1)
                    mm.then_inc(S["o_done"], 1)

                heads(pe, head)

            @block.scalar
            def _(act):
                act.wait_ge(S["qkv_in"], 96)
                for h in range(NH):
                    if h >= 2:
                        act.wait_ge(S["summed"], h - 1)
                    a, b = columns(h)
                    nc.scalar.activation(sq[:, h % 2, a:b], qk[:, h, a:b], ACT.Square).then_inc(S["squared"], 1)
                rsqrt_steps(k, None, act, ms[:, :], tmp[:, :], None, (S["means_done"], 2), (S["roots_done"], 1), None, None)
                for kv in range(KVH):
                    act.wait_ge(S["v_turned"], kv + 1)
                    src = ps[:, 2 + 2 * kv:4 + 2 * kv, :].rearrange("p a n -> p (a n)")[:, 0:T]
                    nc.scalar.activation(vt[:, kv].rearrange("p t d -> p (t d)"), src, ACT.Copy).then_inc(S["v_copied"], 1)

                def head(kv, h, b):
                    for what, t in tile_order():
                        if what == "ahead":
                            n = h * LT + t
                            act.wait_ge(S["shift_done"], n + 1)
                            if not (isinstance(n, int) and n < 2):
                                act.wait_ge(S["probs_turned_done"], n - 1)
                            src = ps[:, 2 * (t % 2):2 * (t % 2) + 2, :].rearrange("p a n -> p (a n)")[:, 0:T]
                            nc.scalar.activation(pr[:, t % 2, :], src, ACT.Exp, bias=small[:, t % 2, 1:2], scale=float(HD) ** -0.5,
                                                 accum_out=small[:, t % 2, 2:3]).then_inc(S["exp_done"], 1)
                    act.wait_ge(S["o_done"], h + 1)
                    nc.scalar.activation(oT[:, ds(h, 1), :].rearrange("p a t -> p (a t)"), ps[:, 6 + b, :], ACT.Copy).then_inc(S["o_copied"], 1)

                heads(act, head)

            @block.vector
            def _(dve):
                st = Count()
                dve.wait_ge(S["qkv_in"], 96)
                dve.wait_ge(S["summed"], NH)
                nc.vector.tensor_scalar(ms[:, CTX:T], ps[0:NH, 0, :], 1.0 / HD, EPS, ALU.mult, ALU.add).then_inc(S["means_done"], 1)
                nc.vector.tensor_scalar(ms[:, 0:CTX], ps[0:NH, 1, 0:CTX], 1.0 / HD, EPS, ALU.mult, ALU.add).then_inc(S["means_done"], 1)
                rsqrt_steps(k, dve, None, ms[:, :], tmp[:, :], rr[:, :], None, (S["roots_done"], 1), S["attn_dve_step"], st)
                dve.sem_inc(S["rsqrt_done"], 1)

                def rope_end(h):
                    dve.wait_ge(S["cos_done"], h + 1)
                    dve.wait_ge(S["sin_done"], h + 1)
                    nc.vector.tensor_tensor(qk[:, h, CTX:T], side[:, h % 2, :], qk[:, h, CTX:T], ALU.add).then_inc(S["rope_done"], 1)

                for h in range(NH):
                    dve.wait_ge(S["spread"], h + 1)
                    w = nw[:, 0:1] if h < QH else nw[:, 1:2]
                    if h >= QH:
                        nc.vector.scalar_tensor_tensor(out=qk[:, h, 0:CTX], in0=qk[:, h, 0:CTX], scalar=w, in1=ps[:, 3, 0:CTX], op0=ALU.mult, op1=ALU.mult)
                    nc.vector.scalar_tensor_tensor(out=qk[:, h, CTX:T], in0=qk[:, h, CTX:T], scalar=w, in1=ps[:, 2, :], op0=ALU.mult, op1=ALU.mult).then_inc(S["normed"], 1)
                    dve.wait_ge(S["rotated"], h + 1)
                    dve.wait_ge(S["cos_done"], h + 1)
                    nc.vector.tensor_tensor(qk[:, h, CTX:T], ps[:, 4 + h % 2, :], k.c["sin"], ALU.mult).then_inc(S["sin_done"], 1)
                    rope_end(h)

                def head(kv, h, b):
                    for what, t in tile_order():
                        n = h * LT + t
                        col = small[:, t % 2]
                        if what == "ahead":
                            dve.wait_ge(S["scores_done"], n + 1)
                            src = ps[:, 2 * (t % 2):2 * (t % 2) + 2, :].rearrange("p a n -> p (a n)")[:, 0:T]
                            nc.vector.tensor_reduce(col[:, 0:1], src, AX_X, ALU.max).then_inc(S["attn_dve_step"], 1)
                            dve.wait_ge(S["attn_dve_step"], base_steps + n + 1)
                            nc.vector.tensor_scalar(col[:, 1:2], col[:, 0:1], -float(HD) ** -0.5, None, ALU.mult).then_inc(S["shift_done"], 1)
                        else:
                            dve.wait_ge(S["exp_done"], n + 1)
                            if not (isinstance(n, int) and n < 2):
                                dve.wait_ge(S["probs_done"], n - 1)
                            nc.vector.reciprocal(col[:, 3:4], col[:, 2:3]).then_inc(S["recip_done"], 1)
                            dve.wait_ge(S["probs_turned_done"], n + 1)
                            if t == 0 and not first(h):
                                dve.wait_ge(S["o_done"], h - 1)
                            src = ps[:, 4:6, :].rearrange("p a n -> p (a n)")[:, 0:T].rearrange("p (j q) -> p j q", q=P)
                            nc.vector.tensor_copy(pT[:, b, :, t * P:(t + 1) * P], src).then_inc(S["probs_copied"], 1)

                base_steps = st.n
                heads(dve, head)

            @block.gpsimd
            def _(pool):
                pool.wait_ge(S["qkv_in"], 96)
                for h in range(NH):
                    pool.wait_ge(S["normed"], h + 1)
                    if h >= 2:
                        pool.wait_ge(S["rope_done"], h - 1)
                    nc.gpsimd.tensor_tensor(side[:, h % 2, :], qk[:, h, CTX:T], k.c["cos"], ALU.mult).then_inc(S["cos_done"], 1)
                pool.wait_ge(S["rope_done"], NH)

                def head(kv, h, b):
                    if not first(h):
                        pool.wait_ge(S["scores_done"], (h - 1) * LT)
                    nc.gpsimd.tensor_copy(qs[:, b, :], qk[:, ds(h, 1), CTX:T].rearrange("p a t -> p (a t)")).then_inc(S["q_copied"], 1)
                    for t in range(LT):
                        pool.wait_ge(S["recip_done"], h * LT + t + 1)
                        nc.gpsimd.tensor_tensor(pr[:, t % 2, :], pr[:, t % 2, :], small[:, t % 2, 3:4].to_broadcast([P, T]), ALU.mult).then_inc(S["probs_done"], 1)

                heads(pool, head)


def decay_columns(k, ba, cols):
    nc, ps = k.nc, k.psum
    W = 2 * DH * NT
    with ExitStack() as s:
        rates = sbuf(k, s, "rates", [P, 2, 2 * DH])
        a = sbuf(k, s, "decay_work", [P, 4, NT, 2 * DH])
        rates_in, act_step, dve_step, sums_done = k.sem("rates_in"), k.sem("decay_act"), k.sem("decay_dve"), k.sem("decay_sums")
        by_tile = lambda x: x.rearrange("p (t n) -> p t n", n=2 * DH)
        kind = lambda j: cols[:, :, j, :, :].rearrange("p h d t -> p t d h")
        split = lambda x: x.rearrange("p t (d h) -> p t d h", d=2)
        with nc.Block() as block:

            @block.sync
            def _(sp):
                for j, name in enumerate(("dn_a_log", "dn_dt_bias")):
                    sp.dma_start(rates[:, j, :], k.inp[name].rearrange("a d h -> a (d h)").to_broadcast([P, 2 * DH])).then_inc(rates_in, 16)

            @block.scalar
            def _(act):
                act.wait_ge(rates_in, 32)
                nc.scalar.activation(rates[:, 0, :], rates[:, 0, :], ACT.Exp).then_inc(act_step, 1)
                act.wait_ge(dve_step, 1)
                nc.scalar.activation(a[:, 1], a[:, 0], ACT.Abs).then_inc(act_step, 1)
                act.wait_ge(act_step, 2)
                nc.scalar.activation(a[:, 1], a[:, 1], ACT.Exp, scale=-1.0).then_inc(act_step, 1)
                act.wait_ge(act_step, 3)
                nc.scalar.activation(a[:, 1], a[:, 1], ACT.Ln, bias=1.0).then_inc(act_step, 1)
                nc.scalar.activation(a[:, 2], ba[:, :, 0:2 * DH], ACT.Sigmoid).then_inc(act_step, 1)
                act.wait_ge(dve_step, 6)
                nc.scalar.activation(kind(3), split(a[:, 0]), ACT.Exp).then_inc(act_step, 1)
                nc.scalar.activation(kind(4), split(a[:, 3]), ACT.Exp).then_inc(act_step, 1)
                for half in range(2):
                    nc.scalar.activation(kind(6 + half), split(by_tile(ps[:, 2 + half, 0:W])), ACT.Exp).then_inc(act_step, 1)

            @block.vector
            def _(dve):
                dve.wait_ge(rates_in, 32)
                nc.vector.tensor_tensor(a[:, 0], ba[:, :, 2 * DH:4 * DH], rates[:, 1:2, :].to_broadcast([P, NT, 2 * DH]), ALU.add).then_inc(dve_step, 1)
                dve.wait_ge(act_step, 5)
                nc.vector.scalar_tensor_tensor(out=a[:, 1], in0=a[:, 0], scalar=0.0, in1=a[:, 1], op0=ALU.max, op1=ALU.add).then_inc(dve_step, 1)
                dve.wait_ge(dve_step, 2)
                nc.vector.scalar_tensor_tensor(out=a[:, 1], in0=a[:, 1], scalar=-1.0, in1=rates[:, 0:1, :].to_broadcast([P, NT, 2 * DH]), op0=ALU.mult, op1=ALU.mult).then_inc(dve_step, 1)
                dve.wait_ge(sums_done, 1)
                nc.vector.tensor_copy(a[:, 0].rearrange("p t (d h) -> p d t h", d=2), ps[:, 0, 0:W].rearrange("p (d t h) -> p d t h", d=2, t=NT)).then_inc(dve_step, 1)
                dve.wait_ge(dve_step, 4)
                nc.vector.tensor_tensor(a[:, 3], by_tile(ps[:, 1, 0:W]), a[:, 0], ALU.subtract).then_inc(dve_step, 1)
                nc.vector.tensor_copy(kind(0), split(a[:, 2])).then_inc(dve_step, 1)
                nc.vector.tensor_copy(kind(1), split(a[:, 0])).then_inc(dve_step, 1)
                nc.vector.tensor_copy(kind(5), split(a[:, 1])).then_inc(dve_step, 1)
                dve.wait_ge(act_step, 9)
                nc.vector.tensor_tensor(kind(2), kind(3), split(a[:, 2]), ALU.mult).then_inc(dve_step, 1)

            @block.tensor
            def _(pe):
                pe.wait_ge(dve_step, 3)
                la = a[:, 1]
                for d, mask in enumerate(("incl_f", "incl_b")):
                    dst = ps[:, 0, d * W // 2:(d + 1) * W // 2].rearrange("p (t h) -> p t h", h=DH)
                    nc.tensor.matmul(dst, k.c[mask], la[:, :, d * DH:(d + 1) * DH], start=True, stop=True)
                for bank, mask in ((1, "chunk"), (2, "half0"), (3, "half1")):
                    mm = nc.tensor.matmul(by_tile(ps[:, bank, 0:W]), k.c[mask], la, start=True, stop=True)
                mm.then_inc(sums_done, 1)


def delta(k, cols, odT):
    nc, ps = k.nc, k.psum
    M = 2 * NT
    NK = 8
    with ExitStack() as s:
        raw = sbuf(k, s, "dn_raw", [P, 3, T])
        z = sbuf(k, s, "dn_z", [P, LAT])
        kt = sbuf(k, s, "dn_tokens", [P, NT + LT, P])
        vt = sbuf(k, s, "dn_v", [P, NT, P])
        sq = sbuf(k, s, "dn_squares", [P, NT + LT, P])
        cs = sbuf(k, s, "dn_head_cols", [P, NK, M])
        nrm = sbuf(k, s, "dn_norms", [P, 3, NT + LT])
        kT = sbuf(k, s, "dn_kT", [P, T])
        qT = sbuf(k, s, "dn_qT", [P, LAT])
        dec = sbuf(k, s, "dn_decay", [P, M, P])
        fs = sbuf(k, s, "dn_decay_strict", [P, M, P])
        fi = sbuf(k, s, "dn_decay_incl", [P, 2, LT, P])
        A = sbuf(k, s, "dn_A", [P, M, P])
        QK = sbuf(k, s, "dn_QK", [P, 2, LT, P])
        R = sbuf(k, s, "dn_inverse_turned", [P, M, P])
        Ti = sbuf(k, s, "dn_inverse", [P, M, P])
        Y = sbuf(k, s, "dn_product", [P, M, P])
        kbg = sbuf(k, s, "dn_k_beta_g", [P, M, P])
        kdec = sbuf(k, s, "dn_k_decayed", [P, M, P])
        vb = sbuf(k, s, "dn_v_beta", [P, M, P])
        qg = sbuf(k, s, "dn_q_g", [P, 2, LT, P])
        qgT = sbuf(k, s, "dn_q_g_turned", [P, 2, LT, P])
        state = sbuf(k, s, "dn_state", [P, 2, P])
        vn = sbuf(k, s, "dn_v_new", [P, 2, P])
        o = sbuf(k, s, "dn_o", [P, LT, P])
        onr = sbuf(k, s, "dn_o_norms", [P, 3, LT])
        nw = sbuf(k, s, "dn_norm_col", [P, 1])
        per = {
            "raw_in": 48, "z_in": 16, "raw_turned": 3, "k_tok": 1, "v_tok": 1, "q_tok": 1, "squares": 1, "norm_ms": 1, "norm_root": 1,
            "normed": 2, "turned_back": 2, "copied_back": 2, "head_cols": 1, "rates_spread": 2, "g_rows": 1, "diffs": 3, "decay_done": 2,
            "strict_done": 4, "incl_done": 2, "kk_done": 2, "a_done": 2, "qk_done": 2, "scaled": 8, "inv_pe": 48, "inv_dve": 68,
            "w_done": 1, "u_done": 1, "w_copied": 3, "u_copied": 3, "qg_turned": 1, "qg_copied": 1, "ws_done": 22, "kv_done": 22,
            "o_mm": 16, "vn_done": 22, "s_done": 22, "o_added": 16, "o_squares": 1, "o_ms": 1, "o_root": 1, "o_normed": 1,
            "o_turned": 1, "dn_step": 10, "o_zero": 1,
        }
        S = {n: k.sem("dn_" + n) for n in per}
        head_free, nw_in = k.sem("head_free"), k.sem("nw_in")
        order = [list(range(2 * NT)), [3, 2, 1, 0] + list(range(2 * NT - 1, 3, -1))]
        GROUPS = [(0, 0, 3), (0, 3, 6), (1, 0, 3), (1, 3, 6)]
        flat = lambda x: x.rearrange("p a b -> p (a b)")

        def at(h, name, j):
            return h * per[name] + j + 1

        def scan_steps():
            for i in range(2 * NT):
                for d in range(2):
                    c = order[d][i]
                    yield i, d, c // 2, (c % 2) * CHUNK

        with nc.Block() as block:

            @block.sync
            def _(sp):
                sp.dma_start(nw[:, :], k.inp["dn_norm_w"].rearrange("a d -> d a")).then_inc(nw_in, 16)

                def load(h):
                    row = lambda g, a: k.feat_d[ds(g + h, 1), :, a:T].rearrange("a p t -> (a p) t")
                    sp.dma_start(raw[:, 0, :], row(G_DK, 0)).then_inc(S["raw_in"], 16)
                    sp.dma_start(raw[:, 1, :], row(G_DV, 0)).then_inc(S["raw_in"], 16)
                    sp.dma_start(raw[:, 2, CTX:T], row(G_DQ, CTX)).then_inc(S["raw_in"], 16)

                def load_z(h):
                    sp.dma_start(z[:, :], k.feat_d[ds(G_Z + h, 1), :, CTX:T].rearrange("a p t -> (a p) t")).then_inc(S["z_in"], 16)

                load(0)
                load_z(0)
                with sp.Fori(1, DH) as h:
                    sp.wait_ge(S["raw_turned"], 3 * h)
                    load(h)
                    sp.wait_ge(head_free, h + 1)
                    load_z(h)

            @block.tensor
            def _(pe):
                w = lambda name, h, j: pe.wait_ge(S[name], at(h, name, j))
                ident = k.c["ident"]
                col = lambda j: slice((j % 4) * P, (j % 4 + 1) * P)
                with pe.Fori(0, DH) as h:
                    pe.wait_ge(head_free, h + 1)
                    pe.wait_ge(S["raw_in"], 48 * h + 48)
                    for j, (bank, lo) in enumerate(((0, 0), (2, 0), (4, CT))):
                        for t in range(lo, NT):
                            tr = nc.tensor.transpose(ps[:, bank + (t - lo) // 4, col(t - lo)], raw[:, j, t * P:(t + 1) * P], ident)
                        tr.then_inc(S["raw_turned"], 1)
                    w("rates_spread", h, 1)
                    for b in range(3):
                        mm = nc.tensor.matmul(ps[:, 5 + b, :], k.c["ones"], flat(A[:, 4 * b:4 * b + 4, :]), start=True, stop=True)
                    mm.then_inc(S["g_rows"], 1)
                    w("k_tok", h, 0)
                    w("normed", h, 0)
                    for t in range(NT):
                        tr = nc.tensor.transpose(ps[:, t // 4, col(t)], kt[:, t, :], ident)
                    tr.then_inc(S["turned_back"], 1)
                    w("q_tok", h, 0)
                    w("normed", h, 1)
                    for t in range(LT):
                        tr = nc.tensor.transpose(ps[:, 4, col(t)], kt[:, NT + t, :], ident)
                    tr.then_inc(S["turned_back"], 1)
                    w("copied_back", h, 1)
                    w("v_tok", h, 0)
                    for t in range(NT):
                        mm = nc.tensor.matmul(ps[:, 2 + t // 4, col(t)], kT[:, t * P:(t + 1) * P], kT[:, t * P:(t + 1) * P], start=True, stop=True)
                    mm.then_inc(S["kk_done"], 1)
                    for t in range(LT):
                        mm = nc.tensor.matmul(ps[:, 4, col(t)], kT[:, (CT + t) * P:(CT + t + 1) * P], qT[:, t * P:(t + 1) * P], start=True, stop=True)
                    mm.then_inc(S["kk_done"], 1)
                    w("diffs", h, 2)
                    w("qk_done", h, 1)
                    for n in range(6):
                        for g, (d, a, b) in enumerate(GROUPS):
                            if n == 0:
                                w("a_done", h, d)
                            else:
                                w("inv_dve", h, 12 * (n - 1) + 4 + 2 * g + 1)
                            for j in range(a, b):
                                m = d * NT + j
                                mm = nc.tensor.matmul(ps[:, g, (j - a) * P:(j - a + 1) * P], A[:, m, :], ident if n == 0 else R[:, m, :], start=True, stop=True)
                            mm.then_inc(S["inv_pe"], 1)
                        for g, (d, a, b) in enumerate(GROUPS):
                            w("inv_dve", h, 12 * n + g)
                            for j in range(a, b):
                                m = d * NT + j
                                c = slice((j - a) * P, (j - a + 1) * P)
                                if n < 5:
                                    mm = nc.tensor.matmul(ps[:, g, c], Y[:, m, :], ident if n == 0 else Ti[:, m, :], start=True, stop=True)
                                if n > 0:
                                    mm = nc.tensor.matmul(ps[:, 4 + g, c], Ti[:, m, :], Y[:, m, :], start=True, stop=True)
                            mm.then_inc(S["inv_pe"], 1)
                    w("scaled", h, 7)
                    w("inv_dve", h, 67)
                    for m in range(M):
                        mm = nc.tensor.matmul(ps[:, m // 4, col(m)], kbg[:, m, :], R[:, m, :], start=True, stop=True)
                    mm.then_inc(S["w_done"], 1)
                    for m in range(M):
                        mm = nc.tensor.matmul(ps[:, 3 + m // 4, col(m)], R[:, m, :], vb[:, m, :], start=True, stop=True)
                    mm.then_inc(S["u_done"], 1)
                    w("w_copied", h, 2)
                    for d in range(2):
                        for t in range(LT):
                            tr = nc.tensor.transpose(ps[:, d, col(t)], qg[:, d, t, :], ident)
                    tr.then_inc(S["qg_turned"], 1)
                    w("qg_copied", h, 0)
                    w("u_copied", h, 2)
                    for i, d, t, lo in scan_steps():
                        m = d * NT + t
                        rows = slice(lo, lo + CHUNK)
                        if i > 0:
                            w("s_done", h, 2 * (i - 1) + d)
                            nc.tensor.matmul(ps[rows, d, 0:P], Y[:, m, lo:lo + CHUNK], state[:, d, :], start=True, stop=True).then_inc(S["ws_done"], 1)
                        if d == 0:
                            continue
                        for e in range(2):
                            c = order[e][i]
                            t, lo = c // 2, (c % 2) * CHUNK
                            m, rows = e * NT + t, slice(lo, lo + CHUNK)
                            if i > 0:
                                w("vn_done", h, 2 * (i - 1) + e)
                            new = vn[rows, e, :] if i > 0 else Ti[rows, m, :]
                            if i >= 4:
                                if i > 4:
                                    w("o_added", h, 2 * (i - 5) + e)
                                nc.tensor.matmul(ps[rows, 2 + e, 0:P], qgT[:, e, t - CT, lo:lo + CHUNK], state[:, e, :], start=True, stop=False)
                                nc.tensor.matmul(ps[rows, 2 + e, 0:P], QK[rows, e, t - CT, lo:lo + CHUNK], new, start=False, stop=True).then_inc(S["o_mm"], 1)
                            if i < 2 * NT - 1:
                                nc.tensor.matmul(ps[:, 4 + e, 0:P], kdec[rows, m, :], new, start=True, stop=True).then_inc(S["kv_done"], 1)
                    w("o_normed", h, 0)
                    for t in range(LT):
                        tr = nc.tensor.transpose(ps[:, 6, col(t)], o[:, t, :], ident)
                    tr.then_inc(S["o_turned"], 1)

            @block.scalar
            def _(act):
                w = lambda name, h, j: act.wait_ge(S[name], at(h, name, j))
                copy = lambda dst, src: nc.scalar.activation(dst, src, ACT.Copy)
                with act.Fori(0, DH) as h:
                    w("raw_turned", h, 0)
                    copy(flat(kt[:, 0:NT, :]), flat(ps[:, 0:2, :])[:, 0:T]).then_inc(S["k_tok"], 1)
                    w("raw_turned", h, 1)
                    copy(flat(vt[:, :, :]), flat(ps[:, 2:4, :])[:, 0:T]).then_inc(S["v_tok"], 1)
                    w("raw_turned", h, 2)
                    copy(flat(kt[:, NT:NT + LT, :]), ps[:, 4, :]).then_inc(S["q_tok"], 1)
                    rsqrt_steps(k, None, act, nrm[:, 0, :], nrm[:, 1, :], None, (S["norm_ms"], at(h, "norm_ms", 0)), (S["norm_root"], 1), None, None)
                    w("diffs", h, 2)
                    nc.scalar.activation(dec[:, :, :], dec[:, :, :], ACT.Abs).then_inc(S["decay_done"], 1)
                    w("decay_done", h, 0)
                    nc.scalar.activation(dec[:, :, :], dec[:, :, :], ACT.Exp, scale=-1.0).then_inc(S["decay_done"], 1)
                    w("turned_back", h, 0)
                    copy(kT[:, :], flat(ps[:, 0:2, :])[:, 0:T]).then_inc(S["copied_back"], 1)
                    w("turned_back", h, 1)
                    copy(qT[:, :], ps[:, 4, :]).then_inc(S["copied_back"], 1)
                    w("w_done", h, 0)
                    for b in range(3):
                        copy(flat(Y[:, 4 * b:4 * b + 4, :]), ps[:, b, :]).then_inc(S["w_copied"], 1)
                    w("u_done", h, 0)
                    for b in range(3):
                        copy(flat(Ti[:, 4 * b:4 * b + 4, :]), ps[:, 3 + b, :]).then_inc(S["u_copied"], 1)
                    w("qg_turned", h, 0)
                    copy(qgT[:, :, :, :].rearrange("p d t c -> p (d t c)"), flat(ps[:, 0:2, :])).then_inc(S["qg_copied"], 1)
                    rsqrt_steps(k, None, act, onr[:, 0, :], onr[:, 1, :], None, (S["o_ms"], at(h, "o_ms", 0)), (S["o_root"], 1), None, None)

            @block.vector
            def _(dve):
                st = Count()
                v = nc.vector
                w = lambda name, h, j: dve.wait_ge(S[name], at(h, name, j))
                dve.sem_inc(head_free, 1)
                with dve.Fori(0, DH) as h:
                    st.enter(h, per["dn_step"])
                    w("squares", h, 0)
                    v.tensor_reduce(nrm[:, 0, :], sq[:, :, :], AX_X, ALU.add).then_inc(S["dn_step"], 1)
                    dve.wait_ge(S["dn_step"], st.up())
                    v.tensor_scalar(nrm[:, 0, :], nrm[:, 0, :], EPS, None, ALU.add).then_inc(S["norm_ms"], 1)
                    rsqrt_steps(k, dve, None, nrm[:, 0, :], nrm[:, 1, :], nrm[:, 2, :], None, (S["norm_root"], at(h, "norm_root", 0)), S["dn_step"], st)
                    v.tensor_tensor(kt[:, 0:NT, :], kt[:, 0:NT, :], nrm[:, 2, 0:NT, None].to_broadcast([P, NT, P]), ALU.mult).then_inc(S["normed"], 1)
                    v.scalar_tensor_tensor(out=kt[:, NT:NT + LT, :], in0=kt[:, NT:NT + LT, :], scalar=float(HD) ** -0.5,
                                           in1=nrm[:, 2, NT:NT + LT, None].to_broadcast([P, LT, P]), op0=ALU.mult, op1=ALU.mult).then_inc(S["normed"], 1)
                    w("g_rows", h, 0)
                    w("head_cols", h, 0)
                    for b in range(3):
                        v.tensor_tensor(dec[:, 4 * b:4 * b + 4, :], ps[:, 5 + b, :].rearrange("p (a c) -> p a c", c=P),
                                        cs[:, 1, 4 * b:4 * b + 4, None].to_broadcast([P, 4, P]), ALU.subtract).then_inc(S["diffs"], 1)
                    v.memset(o[:, :, :], 0.0).then_inc(S["o_zero"], 1)
                    w("kk_done", h, 0)
                    for d in range(2):
                        w("strict_done", h, 2 * d + 1)
                        v.tensor_tensor(A[:, d * NT:(d + 1) * NT, :], flat(ps[:, 2:4, :])[:, 0:T].rearrange("p (a c) -> p a c", c=P), fs[:, d * NT:(d + 1) * NT, :], ALU.mult).then_inc(S["a_done"], 1)
                    w("kk_done", h, 1)
                    for d in range(2):
                        w("incl_done", h, d)
                        v.tensor_tensor(QK[:, d], ps[:, 4, :].rearrange("p (a c) -> p a c", c=P), fi[:, d], ALU.mult).then_inc(S["qk_done"], 1)
                    for n in range(6):
                        for g, (d, a, b) in enumerate(GROUPS):
                            w("inv_pe", h, 8 * n + g)
                            mask = k.c[f"level_{'fb'[d]}{n}"]
                            v.tensor_tensor(Y[:, d * NT + a:d * NT + b, :], ps[:, g, 0:3 * P].rearrange("p (a c) -> p a c", c=P),
                                            mask[:, None, :].to_broadcast([P, 3, P]), ALU.mult).then_inc(S["inv_dve"], 1)
                        for g, (d, a, b) in enumerate(GROUPS):
                            ms = slice(d * NT + a, d * NT + b)
                            one = k.c["ident"][:, None, :].to_broadcast([P, 3, P])
                            w("inv_pe", h, 8 * n + 4 + g)
                            if n == 0:
                                v.tensor_tensor(R[:, ms, :], one, Y[:, ms, :], ALU.subtract).then_inc(S["inv_dve"], 1)
                                v.tensor_tensor(Ti[:, ms, :], one, ps[:, g, 0:3 * P].rearrange("p (a c) -> p a c", c=P), ALU.subtract).then_inc(S["inv_dve"], 1)
                            else:
                                v.tensor_tensor(R[:, ms, :], R[:, ms, :], ps[:, 4 + g, 0:3 * P].rearrange("p (a c) -> p a c", c=P), ALU.subtract).then_inc(S["inv_dve"], 1)
                                if n < 5:
                                    v.tensor_tensor(Ti[:, ms, :], Ti[:, ms, :], ps[:, g, 0:3 * P].rearrange("p (a c) -> p a c", c=P), ALU.subtract).then_inc(S["inv_dve"], 1)
                    w("u_copied", h, 2)
                    w("o_zero", h, 0)
                    for i in range(2 * NT):
                        for d in range(2):
                            c = order[d][i]
                            t, lo = c // 2, (c % 2) * CHUNK
                            m, rows = d * NT + t, slice(lo, lo + CHUNK)
                            if i > 0:
                                w("ws_done", h, 2 * (i - 1) + d)
                                v.tensor_tensor(vn[rows, d, :], Ti[rows, m, :], ps[rows, d, 0:P], ALU.subtract).then_inc(S["vn_done"], 1)
                        for d in range(2):
                            c = order[d][i]
                            t, half = c // 2, c % 2
                            m = d * NT + t
                            if i < 2 * NT - 1:
                                w("kv_done", h, 2 * i + d)
                            if i == 0:
                                v.tensor_copy(state[:, d, :], ps[:, 4 + d, 0:P]).then_inc(S["s_done"], 1)
                            elif i < 2 * NT - 1:
                                v.scalar_tensor_tensor(out=state[:, d, :], in0=state[:, d, :], scalar=cs[:, 6 + half, m:m + 1], in1=ps[:, 4 + d, 0:P], op0=ALU.mult, op1=ALU.add).then_inc(S["s_done"], 1)
                        for d in range(2):
                            c = order[d][i]
                            t, lo = c // 2, (c % 2) * CHUNK
                            rows = slice(lo, lo + CHUNK)
                            if i >= 4:
                                w("o_mm", h, 2 * (i - 4) + d)
                                if i > 4:
                                    w("o_added", h, 2 * (i - 5) + 1)
                                v.tensor_tensor(o[rows, t - CT, :], o[rows, t - CT, :], ps[rows, 2 + d, 0:P], ALU.add).then_inc(S["o_added"], 1)
                    w("o_squares", h, 0)
                    v.tensor_reduce(onr[:, 0, :], sq[:, 0:LT, :], AX_X, ALU.add).then_inc(S["dn_step"], 1)
                    dve.wait_ge(S["dn_step"], st.up())
                    v.tensor_scalar(onr[:, 0, :], onr[:, 0, :], 1.0 / HD, EPS, ALU.mult, ALU.add).then_inc(S["o_ms"], 1)
                    rsqrt_steps(k, dve, None, onr[:, 0, :], onr[:, 1, :], onr[:, 2, :], None, (S["o_root"], at(h, "o_root", 0)), S["dn_step"], st)
                    v.tensor_tensor(o[:, :, :], o[:, :, :], onr[:, 2, :, None].to_broadcast([P, LT, P]), ALU.mult).then_inc(S["o_normed"], 1)
                    w("o_turned", h, 0)
                    dve.wait_ge(S["z_in"], 16 * h + 16)
                    dve.wait_ge(nw_in, 16)
                    v.scalar_tensor_tensor(out=odT[:, ds(h, 1), :].rearrange("p a t -> p (a t)"), in0=ps[:, 6, :], scalar=nw[:, 0:1], in1=z[:, :], op0=ALU.mult, op1=ALU.mult).then_inc(head_free, 1)
                st.leave(DH)

            @block.gpsimd
            def _(pool):
                g = nc.gpsimd
                w = lambda name, h, j: pool.wait_ge(S[name], at(h, name, j))
                spread = lambda x, n: x[:, :, None].to_broadcast([P, n, P])
                with pool.Fori(0, DH) as h:
                    pool.wait_ge(head_free, h + 1)
                    g.tensor_copy(cs[:, :, :], cols[:, ds(h, 1)].rearrange("p a k d t -> p (a k) (d t)")).then_inc(S["head_cols"], 1)
                    w("head_cols", h, 0)
                    for d, mask in enumerate(("incl_f", "incl_b")):
                        g.tensor_tensor(A[:, d * NT:(d + 1) * NT, :], k.c[mask][:, None, :].to_broadcast([P, NT, P]), spread(cs[:, 5, d * NT:(d + 1) * NT], NT), ALU.mult).then_inc(S["rates_spread"], 1)
                    w("k_tok", h, 0)
                    w("q_tok", h, 0)
                    g.tensor_tensor(sq[:, :, :], kt[:, :, :], kt[:, :, :], ALU.mult).then_inc(S["squares"], 1)
                    w("decay_done", h, 1)
                    for d in range(2):
                        ms = slice(d * NT, (d + 1) * NT)
                        strict, incl = k.c[f"strict_{'fb'[d]}"], k.c[f"incl_{'fb'[d]}"]
                        g.tensor_tensor(fs[:, ms, :], dec[:, ms, :], strict[:, None, :].to_broadcast([P, NT, P]), ALU.mult).then_inc(S["strict_done"], 1)
                        w("strict_done", h, 2 * d)
                        g.tensor_tensor(fs[:, ms, :], fs[:, ms, :], spread(cs[:, 0, ms], NT), ALU.mult).then_inc(S["strict_done"], 1)
                    for d in range(2):
                        g.tensor_tensor(fi[:, d], dec[:, d * NT + CT:(d + 1) * NT, :], k.c[f"incl_{'fb'[d]}"][:, None, :].to_broadcast([P, LT, P]), ALU.mult).then_inc(S["incl_done"], 1)
                    w("normed", h, 1)
                    w("v_tok", h, 0)
                    for d in range(2):
                        ms = slice(d * NT, (d + 1) * NT)
                        g.tensor_tensor(kbg[:, ms, :], kt[:, 0:NT, :], spread(cs[:, 2, ms], NT), ALU.mult).then_inc(S["scaled"], 1)
                        g.tensor_tensor(vb[:, ms, :], vt[:, :, :], spread(cs[:, 0, ms], NT), ALU.mult).then_inc(S["scaled"], 1)
                        g.tensor_tensor(kdec[:, ms, :], kt[:, 0:NT, :], spread(cs[:, 4, ms], NT), ALU.mult).then_inc(S["scaled"], 1)
                        g.tensor_tensor(qg[:, d], kt[:, NT:NT + LT, :], spread(cs[:, 3, d * NT + CT:(d + 1) * NT], LT), ALU.mult).then_inc(S["scaled"], 1)
                    w("o_added", h, 15)
                    g.tensor_tensor(sq[:, 0:LT, :], o[:, :, :], o[:, :, :], ALU.mult).then_inc(S["o_squares"], 1)


def merge(k, oT, odT, yT, x1):
    nc, ps = k.nc, k.psum
    NCH, GC = D // CW, CW // P
    with ExitStack() as s:
        w = sbuf(k, s, "branch_chunk", [P, 2, 2, QH, CW])
        gate = sbuf(k, s, "gate_chunk", [P, 2, 2, GC, LAT])
        part = x1[:, 0, :].rearrange("p (a b t) -> p a b t", a=2, b=2)
        w_in = [k.sem("branch_in0"), k.sem("branch_in1")]
        products_done, parts_done, y_done = k.sem("branch_done"), k.sem("parts_done"), k.sem("y_done")
        sources = [k.inp[n].rearrange("a (h p) n -> (a p) h n", p=P) for n in ("w_branch_attn", "w_branch_dn")]
        with nc.Block() as block:

            @block.sync
            def _(sp):
                def load(c, b):
                    for j in range(2):
                        sp.dma_start(w[:, b, j], sources[j][:, :, ds(c * CW, CW)]).then_inc(w_in[b], 16)
                        g = G_GATE + j * (D // P) + c * GC
                        sp.dma_start(gate[:, b, j], k.feat_d[ds(g, GC), :, CTX:T].rearrange("g p t -> p g t")).then_inc(w_in[b], 16)

                for b in range(2):
                    load(b, b)
                with sp.Fori(1, NCH // 2) as i:
                    for b in range(2):
                        sp.wait_ge(y_done, GC * (2 * i + b - 1))
                        load(2 * i + b, b)

            @block.tensor
            def _(pe):
                def chunks(i):
                    for b in range(2):
                        pe.wait_ge(w_in[b], 64 * i + 64)
                        for j in range(GC):
                            g = GC * (2 * i + b) + j
                            if not (isinstance(g, int) and g < 2):
                                pe.wait_ge(y_done, g - 1)
                            for branch, src in enumerate((oT, odT)):
                                for h in range(QH):
                                    mm = nc.tensor.matmul(ps[:, 2 * (j % 2) + branch, :], w[:, b, branch, h, j * P:(j + 1) * P], src[:, h, :], start=h == 0, stop=h == QH - 1)
                            mm.then_inc(products_done, 1)

                turns(pe, NCH // 2, chunks)

            @block.vector
            def _(dve):
                with dve.Fori(0, NCH // 2) as i:
                    for b in range(2):
                        for j in range(GC):
                            g = GC * (2 * i + b) + j
                            dve.wait_ge(products_done, g + 1)
                            for branch in range(2):
                                nc.vector.tensor_tensor(part[:, j % 2, branch, :], ps[:, 2 * (j % 2) + branch, :], gate[:, b, branch, j, :], ALU.mult).then_inc(parts_done, 1)
                            dve.wait_ge(parts_done, 2 * g + 2)
                            nc.vector.tensor_tensor(yT[:, ds(g, 1), :].rearrange("p a t -> p (a t)"), part[:, j % 2, 0, :], part[:, j % 2, 1, :], ALU.add).then_inc(y_done, 1)


def residual(k, yT, x1):
    nc, ps = k.nc, k.psum
    NCH, NGR = D // CW, D // P
    with ExitStack() as s:
        w = sbuf(k, s, "w_out_chunk", [P, 2, NGR, CW])
        g1 = sbuf(k, s, "g1_rows", [P, D])
        part = sbuf(k, s, "mix_part", [P, 2, CW])
        w_in = [k.sem("w_out_in0"), k.sem("w_out_in1")]
        x_in, mix_done, gated, added = k.sem("x1_in"), k.sem("mix_done"), k.sem("mix_gated"), k.sem("mix_added")
        wo = k.inp["w_out"].rearrange("a (g p) n -> (a p) g n", p=P)
        with nc.Block() as block:

            @block.sync
            def _(sp):
                def load(c, b):
                    sp.dma_start(w[:, b], wo[:, :, ds(c * CW, CW)]).then_inc(w_in[b], 16)

                load(0, 0)
                sp.dma_start(g1[:, :], k.mod_d[0:1, 2 * D:3 * D].to_broadcast([P, D])).then_inc(x_in, 16)
                sp.dma_start(x1[:, :, :], k.inp["x"].rearrange("a (t p) d -> (a p) t d", p=P)).then_inc(x_in, 16)
                load(1, 1)
                with sp.Fori(1, NCH // 2) as i:
                    for b in range(2):
                        sp.wait_ge(mix_done, LT * (2 * i + b - 1))
                        load(2 * i + b, b)

            @block.tensor
            def _(pe):
                def chunks(i):
                    for b in range(2):
                        pe.wait_ge(w_in[b], 16 * i + 16)
                        for t in range(LT):
                            n = LT * (2 * i + b) + t
                            if not (isinstance(n, int) and n < 4):
                                pe.wait_ge(gated, n - 3)
                            for g in range(NGR):
                                mm = nc.tensor.matmul(ps[:, t, :], yT[:, g, t * P:(t + 1) * P], w[:, b, g, :], start=g == 0, stop=g == NGR - 1)
                            mm.then_inc(mix_done, 1)

                turns(pe, NCH // 2, chunks)

            @block.vector
            def _(dve):
                dve.wait_ge(x_in, 32)

                def chunks(i):
                    for b in range(2):
                        for t in range(LT):
                            c = 2 * i + b
                            n = LT * c + t
                            dve.wait_ge(mix_done, n + 1)
                            nc.vector.tensor_tensor(part[:, t % 2, :], ps[:, t, :], g1[:, ds(c * CW, CW)], ALU.mult).then_inc(gated, 1)
                            dve.wait_ge(gated, n + 1)
                            xs = x1[:, t, ds(c * CW, CW)]
                            nc.vector.tensor_tensor(xs, xs, part[:, t % 2, :], ALU.add).then_inc(added, 1)

                turns(dve, NCH // 2, chunks)


def second_norm(k, x1, h2T):
    nc, ps = k.nc, k.psum
    with ExitStack() as s:
        h2 = sbuf(k, s, "h2", [P, LT, D])
        rows = sbuf(k, s, "norm2_rows", [P, 3, D])
        h2_out = k.sem("h2_out")
        ss = sbuf(k, s, "norm2_sums", [P, 3, LT])
        rows_in, sums, ms_done, root_done, step = k.sem("norm2_rows_in"), k.sem("norm2_sums_done"), k.sem("norm2_ms"), k.sem("norm2_root"), k.sem("norm2_step")
        h2_done, turned, taken = k.sem("h2_done"), k.sem("h2_turned"), k.sem("h2_taken")
        with nc.Block() as block:

            @block.sync
            def _(sp):
                sp.dma_start(rows[:, 0, :], k.inp["norm2_w"].to_broadcast([P, D])).then_inc(rows_in, 16)
                sp.dma_start(rows[:, 1, :], k.mod_d[0:1, 4 * D:5 * D].to_broadcast([P, D])).then_inc(rows_in, 16)
                sp.dma_start(rows[:, 2, :], k.mod_d[0:1, 3 * D:4 * D].to_broadcast([P, D])).then_inc(rows_in, 16)
                for t in range(LT):
                    sp.wait_ge(h2_done, t + 1)
                    sp.dma_start(k.h2_d[t], h2[:, t, :]).then_inc(h2_out, 16)
                sp.wait_ge(h2_out, 16 * LT)

            @block.scalar
            def _(act):
                for t in range(LT):
                    nc.scalar.activation(h2[:, t, :], x1[:, t, :], ACT.Square, accum_out=ss[:, 0, t:t + 1]).then_inc(sums, 1)
                rsqrt_steps(k, None, act, ss[:, 0, :], ss[:, 1, :], None, (ms_done, 1), (root_done, 1), None, None)
                for kk in range(1, KD, 2):
                    act.wait_ge(turned, kk + 1)
                    nc.scalar.activation(h2T[:, kk, :], ps[:, kk % 8, :], ACT.Copy).then_inc(taken, 1)

            @block.vector
            def _(dve):
                st = Count()
                dve.wait_ge(rows_in, 48)
                nc.vector.scalar_tensor_tensor(out=rows[:, 0, :], in0=rows[:, 1, :], scalar=1.0, in1=rows[:, 0, :], op0=ALU.add, op1=ALU.mult).then_inc(step, 1)
                st.up()
                dve.wait_ge(sums, LT)
                nc.vector.tensor_scalar(ss[:, 0, :], ss[:, 0, :], 1.0 / D, EPS, ALU.mult, ALU.add).then_inc(ms_done, 1)
                rsqrt_steps(k, dve, None, ss[:, 0, :], ss[:, 1, :], ss[:, 2, :], None, (root_done, 1), step, st)
                for t in range(LT):
                    nc.vector.scalar_tensor_tensor(out=h2[:, t, :], in0=x1[:, t, :], scalar=ss[:, 2, t:t + 1], in1=rows[:, 0, :], op0=ALU.mult, op1=ALU.mult).then_inc(step, 1)
                    dve.wait_ge(step, st.up())
                    nc.vector.tensor_tensor(h2[:, t, :], h2[:, t, :], rows[:, 2, :], ALU.add).then_inc(h2_done, 1)
                for kk in range(0, KD, 2):
                    dve.wait_ge(turned, kk + 1)
                    nc.vector.tensor_copy(h2T[:, kk, :], ps[:, kk % 8, :]).then_inc(step, 1)
                    st.up()
                k.norm2_steps = st.n

            @block.tensor
            def _(pe):
                pe.wait_ge(h2_done, LT)
                for kk in range(KD):
                    if kk >= 8:
                        if kk % 2:
                            pe.wait_ge(taken, (kk - 8) // 2 + 1)
                        else:
                            pe.wait_ge(step, k.norm2_steps - KD // 2 + (kk - 8) // 2 + 1)
                    for t in range(LT):
                        tr = nc.tensor.transpose(ps[:, kk % 8, t * P:(t + 1) * P], h2[:, t, kk:D:KD], k.c["ident"])
                    tr.then_inc(turned, 1)


def routes(k, h2T, experts, weights):
    nc, ps = k.nc, k.psum
    QW = 256
    NCH, GC, NF = D // QW, QW // P, 2 * PH
    K2 = TOPK * TOPK
    with ExitStack() as s:
        w = sbuf(k, s, "w_q_chunk", [P, 2, KD, QW])
        qT = sbuf(k, s, "queries", [P, NF, LAT])
        sk = sbuf(k, s, "sub_keys", [P, NF, P])
        skT = sbuf(k, s, "sub_keys_turned", [P, NF, P])
        sc = sbuf(k, s, "key_scores", [P, NF, NKEYS])
        top = sbuf(k, s, "top_scores", [P, NF, TOPK])
        topi = sbuf(k, s, "top_index", [P, NF, TOPK], U32)
        topf = sbuf(k, s, "top_index_f", [P, NF, TOPK])
        cand = sbuf(k, s, "candidates", [P, PH, K2])
        best = sbuf(k, s, "best_scores", [P, PH, TOPK])
        pos = sbuf(k, s, "best_places", [P, PH, TOPK], U32)
        half = sbuf(k, s, "best_halves", [P, 2, PH, TOPK], U32)
        halff = sbuf(k, s, "best_halves_f", [P, 2, PH, TOPK])
        hit = sbuf(k, s, "place_hits", [P, PH, TOPK, TOPK])
        keyf = sbuf(k, s, "best_keys", [P, 2, PH, TOPK])
        sums = sbuf(k, s, "weight_sums", [P, 2, PH])
        expd = sbuf(k, s, "best_exp", [P, PH, TOPK])
        w_in = [k.sem("w_q_in0"), k.sem("w_q_in1")]
        sk_in, sk_turned, sk_taken, q_done, q_taken = k.sem("sk_in"), k.sem("sk_turned"), k.sem("sk_taken"), k.sem("q_done"), k.sem("q_taken")
        scores, scores_taken, step, shifted, exps, tile_done = k.sem("key_scores_done"), k.sem("key_scores_taken"), k.sem("route_step"), k.sem("shifted"), k.sem("route_exp"), k.sem("tile_routed")
        wq = k.inp["peer_w_q"].rearrange("a (p k) n -> (a p) k n", k=KD)
        LOW = -3.0e38
        with nc.Block() as block:

            @block.sync
            def _(sp):
                sp.dma_start(sk[:, :, :], k.inp["peer_sub_keys"].rearrange("a h c k d -> k (a h c) d")).then_inc(sk_in, 16)

                def load(c, b):
                    sp.dma_start(w[:, b], wq[:, :, ds(c * QW, QW)]).then_inc(w_in[b], 16)

                for b in range(2):
                    load(b, b)
                with sp.Fori(1, NCH // 2) as i:
                    for b in range(2):
                        sp.wait_ge(q_done, GC * (2 * i + b - 1))
                        load(2 * i + b, b)

            @block.tensor
            def _(pe):
                pe.wait_ge(sk_in, 16)
                for f in range(NF):
                    tr = nc.tensor.transpose(ps[:, 4 + f // 4, (f % 4) * P:(f % 4 + 1) * P], sk[:, f, :], k.c["ident"])
                tr.then_inc(sk_turned, 1)

                def chunks(i):
                    for b in range(2):
                        pe.wait_ge(w_in[b], 16 * i + 16)
                        for j in range(GC):
                            g = GC * (2 * i + b) + j
                            slot = GC * b + j
                            if not isinstance(i, int):
                                pe.wait_ge(q_taken, g - 3)
                            for kk in range(KD):
                                mm = nc.tensor.matmul(ps[:, slot, :], w[:, b, kk, j * P:(j + 1) * P], h2T[:, kk, :], start=kk == 0, stop=kk == KD - 1)
                            mm.then_inc(q_done, 1)

                turns(pe, NCH // 2, chunks)
                pe.wait_ge(q_taken, NF)
                pe.wait_ge(sk_taken, 1)
                for t in range(LT):
                    if t:
                        pe.wait_ge(scores_taken, t)
                    for f in range(NF):
                        mm = nc.tensor.matmul(ps[:, f // 4, (f % 4) * P:(f % 4 + 1) * P], qT[:, f, t * P:(t + 1) * P], skT[:, f, :], start=True, stop=True)
                    mm.then_inc(scores, 1)

            @block.scalar
            def _(act):
                act.wait_ge(sk_turned, 1)
                nc.scalar.activation(skT[:, :, :].rearrange("p f n -> p (f n)"), ps[:, 4:8, :].rearrange("p b n -> p (b n)"), ACT.Copy).then_inc(sk_taken, 1)

                def chunks(i):
                    for b in range(2):
                        for j in range(GC):
                            g = GC * (2 * i + b) + j
                            act.wait_ge(q_done, g + 1)
                            nc.scalar.activation(qT[:, ds(g, 1), :].rearrange("p a t -> p (a t)"), ps[:, GC * b + j, :], ACT.Copy).then_inc(q_taken, 1)

                turns(act, NCH // 2, chunks)
                for t in range(LT):
                    act.wait_ge(scores, t + 1)
                    if t:
                        act.wait_ge(shifted, t)
                    nc.scalar.activation(sc[:, :, :].rearrange("p f n -> p (f n)"), ps[:, 0:4, :].rearrange("p b n -> p (b n)"), ACT.Copy).then_inc(scores_taken, 1)
                    act.wait_ge(shifted, t + 1)
                    nc.scalar.activation(expd[:, :, :], expd[:, :, :], ACT.Exp).then_inc(exps, 1)

            @block.vector
            def _(dve):
                st = Count()
                v = nc.vector

                def top16(values, places, data):
                    v.max(values[:, 0:8], data).then_inc(step, 1)
                    hold(k, dve, step, st.up())
                    v.max_index(places[:, 0:8], values[:, 0:8], data).then_inc(step, 1)
                    st.up()
                    v.match_replace(data, values[:, 0:8], data, LOW).then_inc(step, 1)
                    hold(k, dve, step, st.up())
                    v.max(values[:, 8:16], data).then_inc(step, 1)
                    hold(k, dve, step, st.up())
                    v.max_index(places[:, 8:16], values[:, 8:16], data).then_inc(step, 1)
                    st.up()

                with dve.Fori(0, LT) as t:
                    st.enter(t, 170)
                    hold(k, dve, scores_taken, t + 1)
                    for f in range(NF):
                        top16(top[:, f], topi[:, f], sc[:, f])
                    dve.wait_ge(step, st.up(0))
                    v.tensor_copy(topf[:, :, :], topi[:, :, :]).then_inc(step, 1)
                    st.up()
                    for h in range(PH):
                        v.tensor_tensor(cand[:, h, :].rearrange("p (a b) -> p a b", b=TOPK), top[:, 2 * h, :, None].to_broadcast([P, TOPK, TOPK]),
                                        top[:, 2 * h + 1, None, :].to_broadcast([P, TOPK, TOPK]), ALU.add).then_inc(step, 1)
                        hold(k, dve, step, st.up())
                        top16(best[:, h], pos[:, h], cand[:, h])
                    dve.wait_ge(step, st.up(0))
                    v.tensor_single_scalar(half[:, 0], pos[:, :, :], 4, ALU.logical_shift_right).then_inc(step, 1)
                    v.tensor_single_scalar(half[:, 1], pos[:, :, :], TOPK - 1, ALU.bitwise_and).then_inc(step, 1)
                    dve.wait_ge(step, st.up(2))
                    v.tensor_copy(halff[:, :, :, :], half[:, :, :, :]).then_inc(step, 1)
                    dve.wait_ge(step, st.up())
                    for c in range(2):
                        for h in range(PH):
                            v.tensor_tensor(hit[:, h], halff[:, c, h, :, None].to_broadcast([P, TOPK, TOPK]), k.c["iota16"][:, None, :].to_broadcast([P, TOPK, TOPK]), ALU.is_equal).then_inc(step, 1)
                        dve.wait_ge(step, st.up(PH))
                        for h in range(PH):
                            v.tensor_tensor(hit[:, h], hit[:, h], topf[:, 2 * h + c, None, :].to_broadcast([P, TOPK, TOPK]), ALU.mult).then_inc(step, 1)
                        dve.wait_ge(step, st.up(PH))
                        v.tensor_reduce(keyf[:, c], hit[:, :, :, :], AX_X, ALU.add).then_inc(step, 1)
                        dve.wait_ge(step, st.up())
                    v.tensor_tensor(expd[:, :, :], best[:, :, :], best[:, :, 0:1].to_broadcast([P, PH, TOPK]), ALU.subtract).then_inc(shifted, 1)
                    v.scalar_tensor_tensor(out=experts[:, ds(t, 1), :].rearrange("p a (h n) -> p (a h) n", n=TOPK), in0=keyf[:, 0], scalar=float(NKEYS), in1=keyf[:, 1], op0=ALU.mult, op1=ALU.add).then_inc(step, 1)
                    st.up()
                    dve.wait_ge(exps, t + 1)
                    v.tensor_reduce(sums[:, 0], expd[:, :, :], AX_X, ALU.add).then_inc(step, 1)
                    dve.wait_ge(step, st.up())
                    v.reciprocal(sums[:, 1], sums[:, 0]).then_inc(step, 1)
                    dve.wait_ge(step, st.up())
                    v.tensor_tensor(weights[:, ds(t, 1), :].rearrange("p a (h n) -> p (a h) n", n=TOPK), expd[:, :, :], sums[:, 1, :, None].to_broadcast([P, PH, TOPK]), ALU.mult).then_inc(step, 1)
                    dve.wait_ge(step, st.up())
                st.leave(LT)


def expert_layer(k, x1, experts, weights):
    nc = k.nc
    RING, TURN = 8, 16
    PER = PH * TOPK
    with ExitStack() as s:
        ring = sbuf(k, s, "expert_rows", [P, RING, D])
        idx = sbuf(k, s, "gather_index", [P, 2, RING], I32)
        h2s = sbuf(k, s, "h2_tile", [P, D])
        y = sbuf(k, s, "expert_sum", [P, D])
        rows = sbuf(k, s, "final_rows", [P, 2, D])
        hid16 = sbuf(k, s, "hidden_turn", [P, TURN])
        hid = sbuf(k, s, "hidden", [P, PER])
        acts = sbuf(k, s, "expert_acts", [P, PER])
        ss = sbuf(k, s, "final_sums", [P, 4])
        rows_in, used, h2_in = k.sem("final_rows_in"), k.sem("rows_used"), k.sem("h2_tile_in")
        row_in = [k.sem(f"row_in{b}") for b in range(RING)]
        idx_ready, hid_done, gelu_done, step = k.sem("idx_ready"), k.sem("hidden_done"), k.sem("gelu_done"), k.sem("expert_step")
        x2_done, sq_done, ms_done, root_done, out_done, y_free = k.sem("x2_done"), k.sem("x2_squares"), k.sem("x2_ms"), k.sem("x2_root"), k.sem("out_done"), k.sem("y_free")
        tables = [k.inp[n].rearrange("a e d -> (a e) d") for n in ("peer_u", "peer_v")]
        HALF = PER // TURN

        def number(t, phase, i, b):
            return t * 2 * PER + phase * PER + i * TURN + b

        with nc.Block() as block:

            @block.sync
            def _(sp):
                sp.dma_start(rows[:, 0, :], k.mod_d[0:1, 5 * D:6 * D].to_broadcast([P, D])).then_inc(rows_in, 16)
                sp.dma_start(rows[:, 1, :], k.inp["final_norm_w"][None, :].to_broadcast([P, D])).then_inc(rows_in, 16)

                def load_h2(t):
                    sp.dma_start(h2s[:, :], k.h2_d[ds(t, 1)].rearrange("a p d -> (a p) d")).then_inc(h2_in, 16)

                def store(t):
                    sp.wait_ge(out_done, t + 1)
                    sp.dma_start(k.out[:, ds(t * P, P), :].rearrange("a p d -> (a p) d"), y[:, :]).then_inc(y_free, 16)

                load_h2(0)
                with sp.Fori(1, LT) as t:
                    sp.wait_ge(hid_done, t * HALF)
                    load_h2(t)
                    store(t - 1)
                store(LT - 1)
                sp.wait_ge(y_free, 16 * LT + 16)

            @block.gpsimd
            def _(pool):
                with pool.Fori(0, LT) as t:
                    for phase in range(2):
                        with pool.Fori(0, HALF) as i:
                            for b in range(TURN):
                                slot, bank = b % RING, b // RING
                                hold(k, pool, used, number(t, phase, i, b) + 1)
                                if slot == 0:
                                    src = experts[:, ds(t, 1), ds(i * TURN + b, RING)].rearrange("p a n -> p (a n)")
                                    nc.gpsimd.tensor_copy(idx[:, bank, :], src).then_inc(idx_ready, 1)
                                    hold(k, pool, idx_ready, (t * 2 + phase) * (2 * HALF) + 2 * i + bank + 1)
                                nc.gpsimd.indirect_dma_start(out=ring[:, slot, :], out_offset=None, in_=tables[phase],
                                                             in_offset=bass.IndirectOffsetOnAxis(ap=idx[:, bank, slot:slot + 1], axis=0)).then_inc(row_in[slot], 16)

            @block.scalar
            def _(act):
                with act.Fori(0, LT) as t:
                    act.wait_ge(hid_done, (t + 1) * HALF)
                    nc.scalar.activation(acts[:, :], hid[:, :], ACT.Gelu).then_inc(gelu_done, 1)
                    act.wait_ge(x2_done, t + 1)
                    nc.scalar.activation(y[:, :], x1[:, ds(t, 1), :].rearrange("p a d -> p (a d)"), ACT.Square, accum_out=ss[:, 0:1]).then_inc(sq_done, 1)
                    rsqrt_steps(k, None, act, ss[:, 1:2], ss[:, 2:3], None, (ms_done, t + 1), (root_done, 1), None, None)

            @block.vector
            def _(dve):
                st = Count()
                v = nc.vector
                dve.sem_inc(used, RING)
                dve.sem_inc(y_free, 16)
                dve.wait_ge(rows_in, 32)
                with dve.Fori(0, LT) as t:
                    st.enter(t, 7)
                    xt = x1[:, ds(t, 1), :].rearrange("p a d -> p (a d)")
                    hold(k, dve, h2_in, 16 * t + 16)
                    with dve.Fori(0, HALF) as i:
                        for b in range(TURN):
                            n = number(t, 0, i, b)
                            dve.wait_ge(row_in[b % RING], 16 * ((t * 2 * HALF + i) * (TURN // RING) + b // RING + 1))
                            v.tensor_tensor_reduce(ring[:, b % RING, :], ring[:, b % RING, :], h2s[:, :], 1.0, 0.0, ALU.mult, ALU.add, hid16[:, b:b + 1]).then_inc(used, 1)
                        dve.wait_ge(used, RING + number(t, 0, i, TURN))
                        v.tensor_copy(hid[:, ds(i * TURN, TURN)], hid16[:, :]).then_inc(hid_done, 1)
                        hold(k, dve, hid_done, t * HALF + i + 1)
                    dve.wait_ge(y_free, 16 * t + 16)
                    v.memset(y[:, :], 0.0).then_inc(step, 1)
                    st.up()
                    dve.wait_ge(gelu_done, t + 1)
                    v.tensor_tensor(acts[:, :], acts[:, :], weights[:, ds(t, 1), :].rearrange("p a n -> p (a n)"), ALU.mult).then_inc(step, 1)
                    hold(k, dve, step, st.up())
                    with dve.Fori(0, HALF) as i:
                        for b in range(TURN):
                            n = number(t, 1, i, b)
                            dve.wait_ge(row_in[b % RING], 16 * ((t * 2 * HALF + HALF + i) * (TURN // RING) + b // RING + 1))
                            dve.wait_ge(used, RING + n)
                            v.scalar_tensor_tensor(out=y[:, :], in0=ring[:, b % RING, :], scalar=acts[:, ds(i * TURN + b, 1)], in1=y[:, :], op0=ALU.mult, op1=ALU.add).then_inc(used, 1)
                    dve.wait_ge(used, RING + number(t, 1, HALF, 0))
                    v.tensor_tensor(y[:, :], y[:, :], rows[:, 0, :], ALU.mult).then_inc(step, 1)
                    dve.wait_ge(step, st.up())
                    v.tensor_tensor(xt, xt, y[:, :], ALU.add).then_inc(x2_done, 1)
                    dve.wait_ge(sq_done, t + 1)
                    v.tensor_scalar(ss[:, 1:2], ss[:, 0:1], 1.0 / D, EPS, ALU.mult, ALU.add).then_inc(ms_done, 1)
                    rsqrt_steps(k, dve, None, ss[:, 1:2], ss[:, 2:3], ss[:, 3:4], None, (root_done, t + 1), step, st)
                    v.scalar_tensor_tensor(out=y[:, :], in0=xt, scalar=ss[:, 3:4], in1=rows[:, 1, :], op0=ALU.mult, op1=ALU.mult).then_inc(out_done, 1)
                st.leave(LT)


def build(nc, inputs, consts, out):
    with ExitStack() as stack:
        k = Kernel(nc, stack, inputs, consts, out)
        load_consts(k)
        ba = sbuf(k, stack, "beta_decay_cols", [P, NT, 4 * DH])
        with ExitStack() as s:
            hT = sbuf(k, s, "hT", [P, KD, T])
            with ExitStack() as s2:
                xn = sbuf(k, s2, "xn", [P, NT, D])
                modulation(k, xn)
                turn(k, xn, hT)
            project(k, hT, ba)
        k.give_back_semaphores()
        x1 = sbuf(k, stack, "x1", [P, LT, D])
        with ExitStack() as mixers:
            oT = sbuf(k, mixers, "attn_out_turned", [P, QH, LAT])
            attention(k, oT)
            odT = sbuf(k, mixers, "delta_out_turned", [P, DH, LAT])
            with ExitStack() as s:
                cols = sbuf(k, s, "decay_cols", [P, DH, 8, 2, NT])
                decay_columns(k, ba, cols)
                delta(k, cols, odT)
            k.give_back_semaphores()
            yT = sbuf(k, mixers, "yT", [P, D // P, LAT])
            merge(k, oT, odT, yT, x1)
            residual(k, yT, x1)
        experts = sbuf(k, stack, "experts", [P, LT, PH * TOPK], I32)
        weights = sbuf(k, stack, "expert_weights", [P, LT, PH * TOPK])
        with ExitStack() as s:
            h2T = sbuf(k, s, "h2T", [P, KD, LAT])
            second_norm(k, x1, h2T)
            routes(k, h2T, experts, weights)
        expert_layer(k, x1, experts, weights)


_INS = ["x", "c", "ctx", "c_ctx", "ada_w", "ada_b", "norm1_w", "norm2_w", "w_in", "attn_q_norm", "attn_k_norm",
        "dn_conv_w", "dn_a_log", "dn_dt_bias", "dn_norm_w", "w_branch_attn", "w_branch_dn", "w_out", "peer_w_q",
        "peer_sub_keys", "peer_u", "peer_v", "final_norm_w"]


def kernel(**inputs):
    import concourse.bacc as bacc
    from concourse.bass_utils import run_bass_kernel_spmd

    nc = bacc.Bacc("TRN2", target_bir_lowering=False, num_devices=1)
    arrays, aps = {}, {}
    for name in _INS:
        a = np.ascontiguousarray(inputs[name])
        arrays[f"in_{name}"] = a
        aps[name] = nc.dram_tensor(f"in_{name}", a.shape, F32, kind="ExternalInput").ap()
    tables = constants()
    table = np.concatenate([tables[name] for name in CONST_AT], axis=1)
    arrays["shape_tables"] = table
    consts = nc.dram_tensor("shape_tables", table.shape, F32, kind="ExternalInput").ap()
    out = nc.dram_tensor("out", (1, LAT, D), F32, kind="ExternalOutput").ap()
    build(nc, aps, consts, out)
    r = run_bass_kernel_spmd(nc, [arrays], core_ids=[0])
    return r.results[0]["out"]
```

```python
from contextlib import ExitStack

import numpy as np

import concourse.bass as bass
from concourse import mybir

P = 128
D = 2048
KD = D // P
LAT, CTX = 512, 256
T = LAT + CTX
NT = T // P
CT = CTX // P
LT = LAT // P
N_MOD = 6
EPS = 1e-6
HD = 128
QH, KVH = 8, 2
QGROUP = QH // KVH
GRID_W = 64
ROPE_THETA = 10000.0
DH = 8
CONV = 5
CHUNK = 64
PH = 8
NKEYS = 128
TOPK = 16
CW = 512
G_AQ, G_AK, G_AV = 0, 8, 10
G_DQ, G_DK, G_DV, G_Z = 12, 20, 28, 36
BA0 = 44 * P
G_GATE = 44
GATE0 = BA0 + 32
IN_W = GATE0 + 2 * D
NG = G_GATE + 2 * D // P

F32 = mybir.dt.float32
U32 = mybir.dt.uint32
I32 = mybir.dt.int32
F32R = mybir.dt.float32r
ALU = mybir.AluOpType
ACT = mybir.ActivationFunctionType
AX_X = mybir.AxisListType.X
ds = bass.ds


def constants():
    p = np.arange(P)
    same = p[:, None] // CHUNK == p[None, :] // CHUNK
    row, col = p[:, None], p[None, :]
    c = {"ident": np.eye(P), "ones": np.ones((P, P))}
    c["incl_f"] = same & (col >= row)
    c["incl_b"] = same & (col <= row)
    c["strict_f"] = same & (col < row)
    c["strict_b"] = same & (col > row)
    c["chunk"] = same
    c["half0"] = np.broadcast_to(row < CHUNK, (P, P))
    c["half1"] = np.broadcast_to(row >= CHUNK, (P, P))
    for n in range(6):
        b = 1 << n
        low = (row // b == col // b + 1) & ((row // b) % 2 == 1)
        c[f"level_b{n}"] = low
        c[f"level_f{n}"] = low.T
    half = HD // 4
    rot = np.zeros((P, P))
    for d in range(P):
        if (d // half) % 2 == 0:
            rot[d + half, d] = -1.0
        else:
            rot[d - half, d] = 1.0
    c["rot"] = rot
    t = np.arange(LAT)
    inv = (np.float32(ROPE_THETA) ** (-np.arange(half, dtype=np.float32) / np.float32(half))).astype(np.float32)
    pos = np.stack([t // GRID_W, t % GRID_W]).astype(np.float32)
    ang = pos[p // (2 * half)] * inv[p % half][:, None]
    c["cos"] = np.cos(ang.astype(np.float32))
    c["sin"] = np.sin(ang.astype(np.float32))
    pick = np.zeros((P, 19))
    pick[:, 9] = 1.0
    c["pick"] = pick
    rows = np.zeros((P, 10 * P))
    for h in range(10):
        rows[h, h * P:(h + 1) * P] = 1.0
    c["rows"] = rows
    c["iota16"] = np.broadcast_to(np.arange(16), (P, 16))
    return {k: np.ascontiguousarray(v, dtype=np.float32) for k, v in c.items()}


ALWAYS = ("ident", "ones", "iota16")
ATTENTION_ONLY = ("rot", "cos", "sin", "pick", "rows")
CONST_AT = {}
_widths = {n: a.shape[1] for n, a in constants().items()}
MASKS = tuple(n for n in _widths if n not in ALWAYS + ATTENTION_ONLY)
_at = 0
for _name in ALWAYS + MASKS + ATTENTION_ONLY:
    CONST_AT[_name] = (_at, _widths[_name])
    _at += _widths[_name]
MASKS_AT, ATTENTION_AT, CONST_ALL = CONST_AT[MASKS[0]][0], CONST_AT[ATTENTION_ONLY[0]][0], _at


class Count:

    def __init__(self):
        self.n, self.over, self.loops = 0, 0, []

    def up(self, k=1):
        self.n += k
        return self.over + self.n

    def enter(self, i, per_turn):
        self.loops.append((self.n, per_turn, self.over))
        self.over = self.over + i * per_turn

    def leave(self, turns):
        start, per, self.over = self.loops.pop()
        assert self.n - start == per, (self.n - start, per)
        self.n = start + turns * per


class Kernel:

    def __init__(self, nc, stack, inputs, consts, out):
        self.nc, self.stack, self.inp, self.consts, self.out = nc, stack, inputs, consts, out
        self.held = stack.enter_context(nc.semaphore("held"))
        self.sems = []
        self.c = {}
        dram = lambda name, shape: nc.dram_tensor(name, shape, F32, kind="Internal").ap()
        self.mod_d = dram("mod_rows", (2, N_MOD * D))
        self.feat_d = dram("features", (NG, P, T))
        self.h2_d = dram("h2_rows", (LT, P, D))
        self.psum = stack.enter_context(nc.psum_tensor("psum", [P, 8, 512], F32))

    def sem(self, name):
        self.sems.append(self.nc.alloc_semaphore(name))
        return self.sems[-1]

    def give_back_semaphores(self):
        self.nc.clear_and_free_semaphores(self.sems)
        self.nc.all_engine_barrier()
        self.sems = []


def sbuf(k, stack, name, shape, dtype=F32, side="left"):
    return stack.enter_context(k.nc.sbuf_tensor(name, shape, dtype, side=side))


def const_tables(k, stack, title, names):
    start = CONST_AT[names[0]][0]
    end = sum(CONST_AT[names[-1]])
    tile = sbuf(k, stack, title, [P, end - start])
    for name in names:
        a, n = CONST_AT[name]
        k.c[name] = tile[:, a - start:a - start + n]
    return tile


def turns(eng, n, body):
    body(0)
    if n > 1:
        with eng.Fori(1, n) as i:
            body(i)


def hold(k, eng, sem, value):
    eng.wait_ge(sem, value)
    eng.sem_inc(k.held, 1)


def rsqrt_steps(k, dve, act, ms, tmp, r, ms_ready, root_ready, step, st):
    if act is not None:
        act.wait_ge(*ms_ready)
        k.nc.scalar.activation(tmp, ms, ACT.Sqrt).then_inc(root_ready[0], 1)
    if dve is not None:
        dve.wait_ge(*root_ready)
        k.nc.vector.reciprocal(r, tmp).then_inc(step, 1)
        dve.wait_ge(step, st.up())
        k.nc.vector.tensor_tensor(tmp, r, r, ALU.mult).then_inc(step, 1)
        dve.wait_ge(step, st.up())
        k.nc.vector.scalar_tensor_tensor(out=tmp, in0=ms, scalar=-0.5, in1=tmp, op0=ALU.mult, op1=ALU.mult).then_inc(step, 1)
        dve.wait_ge(step, st.up())
        k.nc.vector.scalar_tensor_tensor(out=r, in0=tmp, scalar=1.5, in1=r, op0=ALU.add, op1=ALU.mult).then_inc(step, 1)
        dve.wait_ge(step, st.up())


def exact(x):
    return x.bitcast(F32)


def split_products(nc, out, lhs, rhs, first, last):
    outs, rhss = (out, rhs) if isinstance(out, list) else ([out], [rhs])
    for o, r in zip(outs, rhss):
        nc.tensor.matmul(o, lhs[0], r[0], start=first, stop=False)
        nc.tensor.matmul(o, lhs[0], r[1], start=False, stop=False)
    for o, r in zip(outs, rhss):
        mm = nc.tensor.matmul(o, lhs[1], r[0], start=False, stop=last)
    return mm


def modulation(k, xn, sc):
    nc, ps = k.nc, k.psum
    MW = 256
    NCH = 2 * D // MW
    with ExitStack() as s:
        w = sbuf(k, s, "ada_chunk", [P, 2, KD, MW])
        bias = sbuf(k, s, "ada_bias", [2, 2, MW])
        row = sbuf(k, s, "mod_row", [2, 2, MW])
        raw = sbuf(k, s, "cond_raw", [P, 2, KD])
        junk = sbuf(k, s, "norm_squares", [P, D])
        ss = sbuf(k, s, "norm_sums", [P, 3, NT])
        cond_in, x_in, consts_in = k.sem("cond_in"), k.sem("x_in"), k.sem("consts_in")
        w_in = [k.sem("ada_in0"), k.sem("ada_in1")]
        silu_done, mod_done, row_done = k.sem("silu_done"), k.sem("mod_done"), k.sem("row_done")
        row_out = [k.sem("row_out0"), k.sem("row_out1")]
        sums_done, ms_done, root_done = k.sem("sums_done"), k.sem("ms_done"), k.sem("root_done")
        step = k.sem("mod_dve_step")
        aw = k.inp["ada_w"].rearrange("a (p k) n -> (a p) k n", k=KD)
        ab = k.inp["ada_b"]
        with nc.Block() as block:

            @block.sync
            def _(sp):
                sp.dma_start(raw[:, 0, :], k.inp["c"].rearrange("a (p k) -> (a p) k", k=KD)).then_inc(cond_in, 16)
                sp.dma_start(raw[:, 1, :], k.inp["c_ctx"].rearrange("(p k) -> p k", k=KD)).then_inc(cond_in, 16)

                def load(b, j):
                    sp.dma_start(w[:, b], aw[:, :, ds(j * MW, MW)]).then_inc(w_in[b], 16)
                    sp.dma_start(bias[:, b], ab[:, ds(j * MW, MW)].to_broadcast([2, MW])).then_inc(w_in[b], 16)

                for b in range(2):
                    load(b, b)
                with sp.Fori(0, NCH // 2 - 1) as i:
                    for b in range(2):
                        sp.wait_ge(row_done, 2 * i + b + 1)
                        load(b, 2 * i + b + 2)

            @block.tensor
            def _(pe):
                pe.wait_ge(silu_done, 1)

                def products(i):
                    for b in range(2):
                        pe.wait_ge(w_in[b], 32 * i + 32)
                        if not isinstance(i, int):
                            pe.wait_ge(row_done, 2 * i + b - 1)
                        for kk in range(KD):
                            mm = nc.tensor.matmul(ps[0:2, b, 0:MW], sc[:, kk, :], w[:, b, kk, :], start=kk == 0, stop=kk == KD - 1)
                        mm.then_inc(mod_done, 1)

                turns(pe, NCH // 2, products)

            @block.scalar
            def _(act):
                act.wait_ge(cond_in, 32)
                nc.scalar.activation(sc[:, :, :].rearrange("p k a -> p a k"), raw[:, :, :], ACT.Silu).then_inc(silu_done, 1)
                act.dma_start(k.const_sb[:, :], k.consts[:, 0:MASKS_AT]).then_inc(consts_in, 16)
                act.dma_start(xn[:, 0:CT, :], k.inp["ctx"].rearrange("a (t p) d -> p (a t) d", p=P)).then_inc(x_in, 16)
                act.dma_start(xn[:, CT:NT, :], k.inp["x"].rearrange("a (t p) d -> p (a t) d", p=P)).then_inc(x_in, 16)
                act.wait_ge(x_in, 32)
                for t in range(NT):
                    if t:
                        act.wait_ge(sums_done, t)
                    nc.scalar.activation(junk[:, :], xn[:, t, :], ACT.Square, accum_out=ss[:, 0, t:t + 1]).then_inc(sums_done, 1)
                rsqrt_steps(k, None, act, ss[:, 0, :], ss[:, 1, :], None, (ms_done, 1), (root_done, 1), None, None)
                act.wait_ge(consts_in, 16)

            @block.vector
            def _(dve):
                st = Count()
                dve.wait_ge(sums_done, NT)
                nc.vector.tensor_scalar(ss[:, 0, :], ss[:, 0, :], 1.0 / D, EPS, ALU.mult, ALU.add).then_inc(ms_done, 1)
                rsqrt_steps(k, dve, None, ss[:, 0, :], ss[:, 1, :], ss[:, 2, :], None, (root_done, 1), step, st)
                for t in range(NT):
                    nc.vector.tensor_scalar(xn[:, t, :], xn[:, t, :], ss[:, 2, t:t + 1], None, ALU.mult)

                def add_bias(i):
                    for b in range(2):
                        dve.wait_ge(mod_done, 2 * i + b + 1)
                        if not isinstance(i, int):
                            dve.wait_ge(row_out[b], 16 * i)
                        nc.vector.tensor_tensor(row[:, b, :], ps[0:2, b, 0:MW], bias[:, b, :], ALU.add).then_inc(row_done, 1)

                turns(dve, NCH // 2, add_bias)

            @block.gpsimd
            def _(pool):
                with pool.Fori(0, NCH // 2) as i:
                    for b in range(2):
                        pool.wait_ge(row_done, 2 * i + b + 1)
                        pool.dma_start(k.mod_d[:, ds((2 * i + b) * MW, MW)], row[:, b, :]).then_inc(row_out[b], 16)
                for b in range(2):
                    pool.wait_ge(row_out[b], 16 * NCH // 2)


def turn(k, xn, hT):
    nc, ps = k.nc, k.psum
    with ExitStack() as s:
        modc = sbuf(k, s, "mod_cols", [P, 2, 2, KD])
        nw = sbuf(k, s, "norm1_cols", [P, KD])
        scale = sbuf(k, s, "scale_cols", [P, 2, KD])
        whole = sbuf(k, s, "h_whole", [P, 2, T])
        high_done, low_done = k.sem("h_high_done"), k.sem("h_low_done")
        mod_in, scale_done, turned, taken = k.sem("mod_cols_in"), k.sem("scale_done"), k.sem("turned"), k.sem("taken")
        with nc.Block() as block:

            @block.sync
            def _(sp):
                for a in range(2):
                    sp.dma_start(modc[:, a], k.mod_d[a:a + 1, 0:2 * D].rearrange("a (s p k) -> (a p) s k", s=2, k=KD)).then_inc(mod_in, 16)
                sp.dma_start(nw[:, :], k.inp["norm1_w"].rearrange("a (p k) -> (a p) k", k=KD)).then_inc(mod_in, 16)

            @block.tensor
            def _(pe):
                for kk in range(KD):
                    slot = kk % 4
                    if kk >= 4:
                        pe.wait_ge(taken, 2 * (kk - 3))
                    for t in range(NT):
                        bank, col = (2 * slot, t * P) if t < CT else (2 * slot + 1, (t - CT) * P)
                        tr = nc.tensor.transpose(ps[:, bank, col:col + P], xn[:, t, kk:D:KD], k.c["ident"])
                    tr.then_inc(turned, 1)

            @block.vector
            def _(dve):
                dve.wait_ge(mod_in, 48)
                for a in range(2):
                    nc.vector.scalar_tensor_tensor(out=scale[:, a, :], in0=modc[:, a, 1, :], scalar=1.0, in1=nw[:, :], op0=ALU.add, op1=ALU.mult).then_inc(scale_done, 1)
                dve.wait_ge(scale_done, 2)
                for kk in range(KD):
                    slot = kk % 4
                    dve.wait_ge(turned, kk + 1)
                    if kk >= 2:
                        dve.wait_ge(low_done, kk - 1)
                    for a, cols, bank, n in ((1, slice(0, CTX), 2 * slot, CTX), (0, slice(CTX, T), 2 * slot + 1, LAT)):
                        nc.vector.tensor_scalar(whole[:, kk % 2, cols], ps[:, bank, 0:n], scale[:, a, kk:kk + 1], modc[:, a, 0, kk:kk + 1], ALU.mult, ALU.add).then_inc(taken, 1)

            @block.scalar
            def _(act):
                for kk in range(KD):
                    act.wait_ge(taken, 2 * kk + 2)
                    nc.scalar.activation(hT[0][:, kk, :], whole[:, kk % 2, :], ACT.Copy).then_inc(high_done, 1)

            @block.gpsimd
            def _(pool):
                for kk in range(KD):
                    pool.wait_ge(high_done, kk + 1)
                    nc.gpsimd.tensor_tensor(hT[1][:, kk, :], whole[:, kk % 2, :], exact(hT[0][:, kk, :]), ALU.subtract).then_inc(low_done, 1)


def project(k, hT, ba, sc):
    nc, ps = k.nc, k.psum
    segments = [
        (0, G_AQ, 2, False, "copy"),
        (G_Z * P, G_Z, 2, False, "silu"),
        (G_DQ * P, G_DQ, 2, False, "conv"),
        (G_AK * P, G_AK, 1, True, "copy"),
        (G_DK * P, G_DK, 4, True, "conv"),
        (GATE0, G_GATE, 8, False, "sigmoid"),
    ]
    GC = CW // P
    PADW = 2 + CTX + 4 + LAT + 2
    L0 = CTX + 4
    with ExitStack() as s:
        raw = sbuf(k, s, "w_raw", [P, 2, KD, CW // 2])
        wh = sbuf(k, s, "w_high", [P, 2, KD, P], F32R)
        wl = sbuf(k, s, "w_low", [P, 2, KD, P], F32R)
        wba = sbuf(k, s, "w_ba", [P, KD, 32])
        wbah = sbuf(k, s, "w_ba_high", [P, KD, 32], F32R)
        wbal = sbuf(k, s, "w_ba_low", [P, KD, 32], F32R)
        high_done, low_done, ba_high, ba_split = k.sem("w_high_done"), k.sem("w_low_done"), k.sem("ba_high"), k.sem("ba_split")
        pad = sbuf(k, s, "conv_in", [P, 2, PADW])
        y = sbuf(k, s, "conv_out", [P, 2, PADW - 4])
        stage = sbuf(k, s, "stage", [P, 2, T])
        LW = D // 2
        aw = sbuf(k, s, "ada_rows", [P, 4, LW])
        acc = sbuf(k, s, "mod_sums", [P, LW])
        late_in = [k.sem(f"late_in{b}") for b in range(4)]
        late_step, bias_in, late_summed, late_row, late_out = k.sem("late_step"), k.sem("ada_bias_in"), k.sem("late_summed"), k.sem("late_row"), k.sem("late_out")
        taps_r = sbuf(k, s, "taps_rows", [CONV * 24, P])
        taps = sbuf(k, s, "taps", [P, CONV * 24])
        w_in = [k.sem("w_in0"), k.sem("w_in1")]
        out_st = [k.sem("feat_out0"), k.sem("feat_out1")]
        small_in, group_done, evac_done, conv_done, conv_staged = k.sem("small_in"), k.sem("group_done"), k.sem("evac_done"), k.sem("conv_done"), k.sem("conv_staged")
        pads_zero, taps_turned, taps_done, ba_done, step = k.sem("pads_zero"), k.sem("taps_turned"), k.sem("taps_done"), k.sem("ba_done"), k.sem("proj_dve_step")
        wi = k.inp["w_in"].rearrange("a (p k) n -> (a p) k n", k=KD)

        LATE, LATE0, WINDOWS = KD + 1, 4, 8
        ada = k.inp["ada_w"].rearrange("a (p k) n -> (a p) k n", k=KD)

        CHUNKS = sum(seg[2] for seg in segments)

        def walk(eng, body, peel=False):
            base = 0
            for seg in segments:
                n = seg[2]
                if n >= 4:
                    off = 2 if peel and seg is segments[-1] else 0
                    with eng.Fori(0, (n - off) // 2) as i:
                        for b in range(2):
                            body(seg, base + b + 2 * i, b + 2 * i, (base + b) % 2, base + b, i)
                    for b in range(off):
                        body(seg, base + n - 2 + b, n - 2 + b, (base + b) % 2, base + b, n // 2 - 1)
                else:
                    for c in range(n):
                        body(seg, base + c, c, (base + c) % 2, base + c, 0)
                base += n

        def window(seg, cs, c0, i):
            n = segments.index(seg)
            if n < 2:
                return n, cs
            if seg[2] >= 4:
                base = sum(x[2] for x in segments[:n])
                return (2 if n == 4 else 4) + i, c0 - base
            return None

        def conv_index(seg, cs, j):
            first = sum(GC * x[2] for x in segments[:segments.index(seg)] if x[4] == "conv")
            return first + GC * cs + j

        with nc.Block() as block:

            @block.sync
            def _(sp):
                sp.dma_start(wba[:, :, :], wi[:, :, BA0:BA0 + 32]).then_inc(small_in, 16)
                sp.dma_start(taps_r[:, :], k.inp["dn_conv_w"].rearrange("a j (g p) -> (a j g) p", p=P)).then_inc(small_in, 16)

                def load(seg, c, cs, b, c0, i):
                    for half in range(2):
                        if c0 >= 1:
                            sp.wait_ge(low_done, GC * c + 2 * half - 2)
                        sp.dma_start(raw[:, half], wi[:, :, ds(seg[0] + cs * CW + half * (CW // 2), CW // 2)]).then_inc(w_in[half], 16)
                        if window(seg, cs, c0, i) is None:
                            continue
                        u, at = window(seg, cs, c0, i)
                        if at == 0 and half == 0:
                            sp.wait_ge(late_step, LATE0 + LATE * u + 1)
                            sp.dma_start(acc[0:1, :], k.inp["ada_b"][:, ds(2 * D + u * LW, LW)]).then_inc(bias_in, 16)
                        for n in range(6 * (2 * at + half), min(6 * (2 * at + half + 1), KD)):
                            sp.wait_ge(late_step, LATE0 + LATE * u + n - (2 if n >= 4 else 3))
                            sp.dma_start(aw[:, n % 4, :], ada[:, n, ds(2 * D + u * LW, LW)]).then_inc(late_in[n % 4], 16)

                walk(sp, load)

            @block.tensor
            def _(pe):
                pe.wait_ge(ba_split, 1)
                nc.tensor.transpose(ps[:, 4, 0:CONV * 24], taps_r[:, :], k.c["ident"][0:CONV * 24, 0:CONV * 24]).then_inc(taps_turned, 1)
                for t in range(NT):
                    for kk in range(KD):
                        tile = [x[:, kk, t * P:(t + 1) * P] for x in hT]
                        mm = split_products(nc, ps[:, 5, 32 * t:32 * t + 32], tile, (wbah[:, kk, :], wbal[:, kk, :]), kk == 0, kk == KD - 1)
                mm.then_inc(taps_turned, 1)

                def products(seg, c, cs, b, c0, i):
                    for j in range(GC):
                        slot = (GC * c0 + j) % 2
                        if GC * c0 + j >= 2:
                            pe.wait_ge(evac_done, GC * c + j - 1)
                        pe.wait_ge(low_done, GC * c + j + 1)
                        for kk in range(KD):
                            outs, cols = [ps[:, slot, :]], [slice(CTX, T)]
                            if seg[3]:
                                outs.append(ps[:, 2 + slot, 0:CTX])
                                cols.append(slice(0, CTX))
                            mm = split_products(nc, outs, (wh[:, slot, kk, :], wl[:, slot, kk, :]), [[x[:, kk, n] for x in hT] for n in cols], kk == 0, kk == KD - 1)
                        mm.then_inc(group_done, 1)
                        late = window(seg, cs, c0, i)
                        if late and late[1] == 1 and j == 2:
                            pe.wait_ge(late_step, LATE0 + LATE * late[0] + LATE)
                            for n in range(LW // 512):
                                mm = nc.tensor.matmul(ps[0:1, 4 + n, :], k.c["ones"][:, 0:1], acc[:, n * 512:(n + 1) * 512], start=True, stop=True)
                            mm.then_inc(late_summed, 1)

                walk(pe, products)

            @block.scalar
            def _(act):
                act.wait_ge(small_in, 32)
                nc.scalar.activation(wbah[:, :, :], wba[:, :, :], ACT.Copy).then_inc(ba_high, 1)

                def high(c, j):
                    act.wait_ge(w_in[j // 2], 16 * c + 16)
                    nc.scalar.activation(wh[:, j % 2], raw[:, j // 2, :, (j % 2) * P:(j % 2 + 1) * P], ACT.Copy).then_inc(high_done, 1)

                high(0, 0)
                high(0, 1)
                act.wait_ge(pads_zero, 2)

                def evacuate(seg, c, cs, b, c0, i):
                    func = {"copy": ACT.Copy, "silu": ACT.Silu, "sigmoid": ACT.Sigmoid, "conv": ACT.Copy}[seg[4]]
                    for j in range(GC):
                        g0 = GC * c0 + j
                        slot = g0 % 2
                        act.wait_ge(group_done, GC * c + j + 1)
                        cc = conv_index(seg, cs, j) if seg[4] == "conv" else None
                        if seg[4] == "conv":
                            if seg[3]:
                                nc.scalar.activation(pad[:, slot, 2:2 + CTX], ps[:, 2 + slot, 0:CTX], func)
                            nc.scalar.activation(pad[:, slot, L0 + 2:L0 + 2 + LAT], ps[:, slot, :], func).then_inc(evac_done, 1)
                        if seg[4] != "conv" and g0 >= 2:
                            act.wait_ge(out_st[slot], 16 * ((g0 // 2)) + (c - c0) * 16 * GC // 2)
                        if seg[4] != "conv":
                            if seg[3]:
                                nc.scalar.activation(stage[:, slot, 0:CTX], ps[:, 2 + slot, 0:CTX], func)
                            nc.scalar.activation(stage[:, slot, CTX:T], ps[:, slot, :], func).then_inc(evac_done, 1)
                        if j < 2:
                            high(c, j + 2)
                        elif not (isinstance(c, int) and c == CHUNKS - 1):
                            high(c + 1, j - 2)
                        if seg[4] == "conv":
                            act.wait_ge(conv_done, cc + 1)
                            if g0 >= 2:
                                act.wait_ge(out_st[slot], 16 * ((g0 // 2)) + (c - c0) * 16 * GC // 2)
                            if seg[3]:
                                nc.scalar.activation(stage[:, slot, 0:CTX], y[:, slot, 0:CTX], ACT.Silu)
                            nc.scalar.activation(stage[:, slot, CTX:T], y[:, slot, L0:L0 + LAT], ACT.Silu).then_inc(conv_staged, 1)
                            act.wait_ge(conv_staged, cc + 1)
                        else:
                            act.wait_ge(evac_done, GC * c + j + 1)
                        lo = 0 if seg[3] else CTX
                        g = seg[1] + j + GC * cs
                        act.dma_start(k.feat_d[ds(g, 1), :, lo:T].rearrange("a p t -> (a p) t"), stage[:, slot, lo:T]).then_inc(out_st[slot], 16)
                        late = window(seg, cs, c0, i)
                        if late and late[1] == 1 and j == 3:
                            act.wait_ge(late_row, late[0] + 1)
                            act.dma_start(k.mod_d[0:1, ds(2 * D + late[0] * LW, LW)], acc[0:1, :]).then_inc(late_out, 16)

                walk(act, evacuate, peel=True)
                for b in range(2):
                    act.wait_ge(out_st[b], 16 * GC // 2 * CHUNKS)
                act.wait_ge(late_out, 16 + 16 * WINDOWS)

            @block.vector
            def _(dve):
                dve.sem_inc(late_step, LATE0)
                dve.sem_inc(late_out, 16)
                for b in range(2):
                    nc.vector.memset(pad[:, b, :], 0.0).then_inc(pads_zero, 1)
                dve.wait_ge(taps_turned, 2)
                nc.vector.tensor_copy(taps[:, :], ps[:, 4, 0:CONV * 24]).then_inc(taps_done, 1)
                nc.vector.tensor_copy(ba[:, :, :], ps[:, 5, 0:32 * NT].rearrange("p (t n) -> p t n", n=32)).then_inc(ba_done, 1)
                dve.wait_ge(taps_done, 1)

                first_conv = GC * sum(x[2] for x in segments[:2])

                def modulate(u, w):
                    if w == 0:
                        hold(k, dve, late_out, 16 * u + 16)
                        nc.vector.memset(acc[:, :], 0.0).then_inc(late_step, 1)
                        dve.wait_ge(bias_in, 16 * u + 16)
                    for n in range(3 * w, min(3 * w + 3, KD)):
                        dve.wait_ge(late_in[n % 4], 16 * (KD // 4) * u + 16 * (n // 4) + 16)
                        dve.wait_ge(late_step, LATE0 + LATE * u + n + 1)
                        nc.vector.scalar_tensor_tensor(out=acc[:, :], in0=aw[:, n % 4, :], scalar=sc[:, n, 0:1], in1=acc[:, :], op0=ALU.mult, op1=ALU.add).then_inc(late_step, 1)
                    if w == 7:
                        dve.wait_ge(late_summed, u + 1)
                        nc.vector.tensor_copy(acc[0:1, :], ps[0:1, 4:6, :].rearrange("p b n -> p (b n)")).then_inc(late_row, 1)

                def convolve(seg, c, cs, b, c0, i):
                    late = window(seg, cs, c0, i)
                    lo = 0 if seg[3] else L0
                    for j in range(GC):
                        g0 = GC * c0 + j
                        slot = g0 % 2
                        if late:
                            modulate(late[0], GC * late[1] + j)
                        if seg[4] != "conv":
                            continue
                        dve.wait_ge(evac_done, GC * c + j + 1)
                        if conv_index(seg, 0, j) >= 2 or c0 * GC > first_conv:
                            dve.wait_ge(conv_staged, conv_index(seg, cs, j) - 1)
                        out = y[:, slot, lo:PADW - 4]
                        for tap in range(CONV):
                            src = pad[:, slot, lo + tap:PADW - 4 + tap]
                            wt = taps[:, ds(tap * 24 + seg[1] - G_DQ + j + GC * cs, 1)]
                            if tap == 0:
                                ins = nc.vector.tensor_scalar(out, src, wt, None, ALU.mult)
                            else:
                                ins = nc.vector.scalar_tensor_tensor(out=out, in0=src, scalar=wt, in1=out, op0=ALU.mult, op1=ALU.add)
                            if tap < CONV - 1:
                                ins.then_inc(step, 1)
                                dve.wait_ge(step, conv_index(seg, cs, j) * (CONV - 1) + tap + 1)
                            else:
                                ins.then_inc(conv_done, 1)

                walk(dve, convolve)

            @block.gpsimd
            def _(pool):
                pool.wait_ge(ba_high, 1)
                nc.gpsimd.tensor_tensor(wbal[:, :, :], wba[:, :, :], exact(wbah[:, :, :]), ALU.subtract).then_inc(ba_split, 1)

                def low(seg, c, cs, b, c0, i):
                    for j in range(GC):
                        pool.wait_ge(high_done, GC * c + j + 1)
                        nc.gpsimd.tensor_tensor(wl[:, j % 2], raw[:, j // 2, :, (j % 2) * P:(j % 2 + 1) * P], exact(wh[:, j % 2]), ALU.subtract).then_inc(low_done, 1)

                walk(pool, low)


def attention(k, oT, masks):
    nc, ps = k.nc, k.psum
    NH = QH + KVH
    with ExitStack() as s:
        qk = sbuf(k, s, "qk_raw", [P, NH, T])
        vT = sbuf(k, s, "v_raw", [P, KVH, T])
        vt = sbuf(k, s, "v_tokens", [P, KVH, NT, HD])
        nw = sbuf(k, s, "qk_norm_cols", [P, 2])
        ms = sbuf(k, s, "qk_means", [NH, T])
        tmp = sbuf(k, s, "qk_roots", [NH, T])
        rr = sbuf(k, s, "qk_rsqrt", [NH, T])
        side = sbuf(k, s, "rope_cos_part", [P, 2, LAT])
        pr = sbuf(k, s, "probs", [P, 3, T])
        sq = pr[:, 0:2, :]
        pT = sbuf(k, s, "probs_turned", [P, 2, NT, LAT])
        small = sbuf(k, s, "softmax_cols", [P, 4, 4])
        tables = const_tables(k, s, "attention_tables", ATTENTION_ONLY)
        names = ["masks_in", "qkv_in", "squared", "summed", "means_done", "roots_done", "attn_dve_step", "rsqrt_done", "spread", "normed",
                 "rotated", "cos_done", "rope_done", "v_turned", "v_copied", "scores_done", "shift_done", "exp_done",
                 "recip_done", "probs_done", "probs_turned_done", "probs_copied", "o_done", "o_high", "o_copied", "sin_done"]
        S = {n: k.sem("at_" + n) for n in names}
        with nc.Block() as block:

            @block.sync
            def _(sp):
                for src, dst in (
                    (k.feat_d[G_AQ:G_AQ + QH, :, CTX:T], qk[:, 0:QH, CTX:T]),
                    (k.feat_d[G_AK:G_AK + KVH, :, :], qk[:, QH:NH, :]),
                    (k.feat_d[G_AV:G_AV + KVH, :, :], vT[:, :, :]),
                ):
                    sp.dma_start(dst, src.rearrange("g p t -> p g t")).then_inc(S["qkv_in"], 16)
                sp.dma_start(tables[:, :], k.consts[:, ATTENTION_AT:CONST_ALL]).then_inc(S["qkv_in"], 16)
                sp.dma_start(nw[:, 0:1], k.inp["attn_q_norm"].rearrange("a d -> d a")).then_inc(S["qkv_in"], 16)
                sp.dma_start(nw[:, 1:2], k.inp["attn_k_norm"].rearrange("a d -> d a")).then_inc(S["qkv_in"], 16)
                sp.dma_start(masks[:, :], k.consts[:, MASKS_AT:ATTENTION_AT]).then_inc(S["masks_in"], 16)
                sp.wait_ge(S["masks_in"], 16)

            def columns(h):
                return (CTX, T) if h < QH else (0, T)

            STEPS = QH * LT
            both = lambda x: x.rearrange("p a n -> p (a n)")[:, 0:T]

            @block.tensor
            def _(pe):
                pe.wait_ge(S["qkv_in"], 96)
                for h in range(NH):
                    pe.wait_ge(S["squared"], h + 1)
                    pick = k.c["pick"][:, 9 - h:19 - h]
                    mm = nc.tensor.matmul(ps[0:NH, 0, :], pick, sq[:, h % 2, CTX:T], start=h == 0, stop=h == NH - 1)
                    if h >= QH:
                        mm = nc.tensor.matmul(ps[0:NH, 1, 0:CTX], pick, sq[:, h % 2, 0:CTX], start=h == QH, stop=h == NH - 1)
                    mm.then_inc(S["summed"], 1)
                for kv in range(KVH):
                    for t in range(NT):
                        tr = nc.tensor.transpose(ps[:, 2 + 2 * kv + t // 4, (t % 4) * P:(t % 4 + 1) * P], vT[:, kv, t * P:(t + 1) * P], k.c["ident"])
                    tr.then_inc(S["v_turned"], 1)
                pe.wait_ge(S["rsqrt_done"], 1)
                pe.wait_ge(S["v_copied"], KVH)
                for h in range(NH):
                    if h >= 1:
                        pe.wait_ge(S["normed"], h)
                    spread = k.c["rows"][0:NH, h * P:(h + 1) * P]
                    mm = nc.tensor.matmul(ps[:, 2, :], spread, rr[:, CTX:T], start=True, stop=True)
                    if h >= QH:
                        mm = nc.tensor.matmul(ps[:, 3, 0:CTX], spread, rr[:, 0:CTX], start=True, stop=True)
                    mm.then_inc(S["spread"], 1)
                    pe.wait_ge(S["normed"], h + 1)
                    if h >= 2:
                        pe.wait_ge(S["sin_done"], h - 1)
                    nc.tensor.matmul(ps[:, 4 + h % 2, :], k.c["rot"], qk[:, h, CTX:T], start=True, stop=True).then_inc(S["rotated"], 1)
                pe.wait_ge(S["rope_done"], NH)

                def scores(n):
                    h, t = n // LT, n % LT
                    if n >= 2:
                        pe.wait_ge(S["exp_done"], n - 1)
                    lhs = qk[:, h, CTX + t * P:CTX + (t + 1) * P]
                    keys = QH + h // QGROUP
                    nc.tensor.matmul(ps[:, 2 * (n % 2), :], lhs, qk[:, keys, 0:512], start=True, stop=True)
                    nc.tensor.matmul(ps[:, 2 * (n % 2) + 1, 0:T - 512], lhs, qk[:, keys, 512:T], start=True, stop=True).then_inc(S["scores_done"], 1)

                def turn_probs(n):
                    pe.wait_ge(S["probs_done"], n + 1)
                    if n >= 1:
                        pe.wait_ge(S["probs_copied"], n)
                    for j in range(NT):
                        tr = nc.tensor.transpose(ps[:, 4 + j // 4, (j % 4) * P:(j % 4 + 1) * P], pr[:, n % 3, j * P:(j + 1) * P], k.c["ident"])
                    tr.then_inc(S["probs_turned_done"], 1)

                def values(h):
                    pe.wait_ge(S["probs_copied"], LT * (h + 1))
                    if h >= 2:
                        pe.wait_ge(S["o_copied"], h - 1)
                    for j in range(NT):
                        mm = nc.tensor.matmul(ps[:, 6 + h % 2, :], vt[:, h // QGROUP, j, :], pT[:, h % 2, j, :], start=j == 0, stop=j == NT - 1)
                    mm.then_inc(S["o_done"], 1)

                scores(0)
                scores(1)
                for n in range(STEPS):
                    if n + 2 < STEPS:
                        scores(n + 2)
                    turn_probs(n)
                    if n % LT == 1 and n > LT:
                        values(n // LT - 1)
                values(QH - 1)

            @block.scalar
            def _(act):
                act.wait_ge(S["qkv_in"], 96)
                for h in range(NH):
                    if h >= 2:
                        act.wait_ge(S["summed"], h - 1)
                    a, b = columns(h)
                    nc.scalar.activation(sq[:, h % 2, a:b], qk[:, h, a:b], ACT.Square).then_inc(S["squared"], 1)
                rsqrt_steps(k, None, act, ms[:, :], tmp[:, :], None, (S["means_done"], 2), (S["roots_done"], 1), None, None)
                for kv in range(KVH):
                    act.wait_ge(S["v_turned"], kv + 1)
                    src = ps[:, 2 + 2 * kv:4 + 2 * kv, :].rearrange("p a n -> p (a n)")[:, 0:T]
                    nc.scalar.activation(vt[:, kv].rearrange("p t d -> p (t d)"), src, ACT.Copy).then_inc(S["v_copied"], 1)

                def exp(n):
                    act.wait_ge(S["shift_done"], n + 1)
                    if n >= 3:
                        act.wait_ge(S["probs_turned_done"], n - 2)
                    b = 2 * (n % 2)
                    nc.scalar.activation(pr[:, n % 3, :], both(ps[:, b:b + 2, :]), ACT.Exp, bias=small[:, n % 4, 1:2], scale=float(HD) ** -0.5,
                                         accum_out=small[:, n % 4, 2:3]).then_inc(S["exp_done"], 1)

                exp(0)
                exp(1)
                for n in range(STEPS):
                    h, t = n // LT, n % LT
                    act.wait_ge(S["probs_turned_done"], n + 1)
                    if t == 0 and h >= 2:
                        act.wait_ge(S["o_done"], h - 1)
                    nc.scalar.activation(pT[:, h % 2, :, t * P:(t + 1) * P], both(ps[:, 4:6, :]).rearrange("p (j q) -> p j q", q=P), ACT.Copy).then_inc(S["probs_copied"], 1)
                    if n + 2 < STEPS:
                        exp(n + 2)

            @block.vector
            def _(dve):
                st = Count()
                dve.wait_ge(S["qkv_in"], 96)
                dve.wait_ge(S["summed"], NH)
                nc.vector.tensor_scalar(ms[:, CTX:T], ps[0:NH, 0, :], 1.0 / HD, EPS, ALU.mult, ALU.add).then_inc(S["means_done"], 1)
                nc.vector.tensor_scalar(ms[:, 0:CTX], ps[0:NH, 1, 0:CTX], 1.0 / HD, EPS, ALU.mult, ALU.add).then_inc(S["means_done"], 1)
                rsqrt_steps(k, dve, None, ms[:, :], tmp[:, :], rr[:, :], None, (S["roots_done"], 1), S["attn_dve_step"], st)
                dve.sem_inc(S["rsqrt_done"], 1)

                def rope_end(h):
                    dve.wait_ge(S["cos_done"], h + 1)
                    dve.wait_ge(S["sin_done"], h + 1)
                    nc.vector.tensor_tensor(qk[:, h, CTX:T], side[:, h % 2, :], qk[:, h, CTX:T], ALU.add).then_inc(S["rope_done"], 1)

                for h in range(NH):
                    dve.wait_ge(S["spread"], h + 1)
                    w = nw[:, 0:1] if h < QH else nw[:, 1:2]
                    if h >= QH:
                        nc.vector.scalar_tensor_tensor(out=qk[:, h, 0:CTX], in0=qk[:, h, 0:CTX], scalar=w, in1=ps[:, 3, 0:CTX], op0=ALU.mult, op1=ALU.mult)
                    nc.vector.scalar_tensor_tensor(out=qk[:, h, CTX:T], in0=qk[:, h, CTX:T], scalar=w, in1=ps[:, 2, :], op0=ALU.mult, op1=ALU.mult).then_inc(S["normed"], 1)
                    dve.wait_ge(S["rotated"], h + 1)
                    dve.wait_ge(S["cos_done"], h + 1)
                    nc.vector.tensor_tensor(qk[:, h, CTX:T], ps[:, 4 + h % 2, :], k.c["sin"], ALU.mult).then_inc(S["sin_done"], 1)
                    rope_end(h)

                def shift(n):
                    col = small[:, n % 4]
                    b = 2 * (n % 2)
                    dve.wait_ge(S["scores_done"], n + 1)
                    nc.vector.tensor_reduce(col[:, 0:1], both(ps[:, b:b + 2, :]), AX_X, ALU.max).then_inc(S["attn_dve_step"], 1)
                    dve.wait_ge(S["attn_dve_step"], st.up())
                    nc.vector.tensor_scalar(col[:, 1:2], col[:, 0:1], -float(HD) ** -0.5, None, ALU.mult).then_inc(S["shift_done"], 1)

                def take_o(h):
                    dve.wait_ge(S["o_done"], h + 1)
                    nc.vector.tensor_copy(oT[0][:, h, :], ps[:, 6 + h % 2, :]).then_inc(S["o_high"], 1)
                    dve.wait_ge(S["o_high"], h + 1)
                    nc.vector.tensor_tensor(oT[1][:, h, :], ps[:, 6 + h % 2, :], exact(oT[0][:, h, :]), ALU.subtract).then_inc(S["o_copied"], 1)

                shift(0)
                shift(1)
                for n in range(STEPS):
                    dve.wait_ge(S["exp_done"], n + 1)
                    nc.vector.reciprocal(small[:, n % 4, 3:4], small[:, n % 4, 2:3]).then_inc(S["recip_done"], 1)
                    if n + 2 < STEPS:
                        shift(n + 2)
                    if n % LT == LT - 1 and n > LT:
                        take_o(n // LT - 1)
                take_o(QH - 1)

            @block.gpsimd
            def _(pool):
                pool.wait_ge(S["qkv_in"], 96)
                for h in range(NH):
                    pool.wait_ge(S["normed"], h + 1)
                    if h >= 2:
                        pool.wait_ge(S["rope_done"], h - 1)
                    nc.gpsimd.tensor_tensor(side[:, h % 2, :], qk[:, h, CTX:T], k.c["cos"], ALU.mult).then_inc(S["cos_done"], 1)
                for n in range(STEPS):
                    pool.wait_ge(S["recip_done"], n + 1)
                    nc.gpsimd.tensor_tensor(pr[:, n % 3, :], pr[:, n % 3, :], small[:, n % 4, 3:4].to_broadcast([P, T]), ALU.mult).then_inc(S["probs_done"], 1)


def decay_columns(k, ba, cols):
    nc, ps = k.nc, k.psum
    W = 2 * DH * NT
    with ExitStack() as s:
        rates = sbuf(k, s, "rates", [P, 2, 2 * DH])
        a = sbuf(k, s, "decay_work", [P, 4, NT, 2 * DH])
        rates_in, act_step, dve_step, sums_done = k.sem("rates_in"), k.sem("decay_act"), k.sem("decay_dve"), k.sem("decay_sums")
        by_tile = lambda x: x.rearrange("p (t n) -> p t n", n=2 * DH)
        kind = lambda j: cols[:, :, j, :, :].rearrange("p h d t -> p t d h")
        split = lambda x: x.rearrange("p t (d h) -> p t d h", d=2)
        with nc.Block() as block:

            @block.sync
            def _(sp):
                for j, name in enumerate(("dn_a_log", "dn_dt_bias")):
                    sp.dma_start(rates[:, j, :], k.inp[name].rearrange("a d h -> a (d h)").to_broadcast([P, 2 * DH])).then_inc(rates_in, 16)

            @block.scalar
            def _(act):
                act.wait_ge(rates_in, 32)
                nc.scalar.activation(rates[:, 0, :], rates[:, 0, :], ACT.Exp).then_inc(act_step, 1)
                act.wait_ge(dve_step, 1)
                nc.scalar.activation(a[:, 1], a[:, 0], ACT.Abs).then_inc(act_step, 1)
                act.wait_ge(act_step, 2)
                nc.scalar.activation(a[:, 1], a[:, 1], ACT.Exp, scale=-1.0).then_inc(act_step, 1)
                act.wait_ge(act_step, 3)
                nc.scalar.activation(a[:, 1], a[:, 1], ACT.Ln, bias=1.0).then_inc(act_step, 1)
                nc.scalar.activation(a[:, 2], ba[:, :, 0:2 * DH], ACT.Sigmoid).then_inc(act_step, 1)
                act.wait_ge(dve_step, 6)
                nc.scalar.activation(kind(3), split(a[:, 0]), ACT.Exp).then_inc(act_step, 1)
                nc.scalar.activation(kind(4), split(a[:, 3]), ACT.Exp).then_inc(act_step, 1)
                for half in range(2):
                    nc.scalar.activation(kind(6 + half), split(by_tile(ps[:, 2 + half, 0:W])), ACT.Exp).then_inc(act_step, 1)

            @block.vector
            def _(dve):
                dve.wait_ge(rates_in, 32)
                nc.vector.tensor_tensor(a[:, 0], ba[:, :, 2 * DH:4 * DH], rates[:, 1:2, :].to_broadcast([P, NT, 2 * DH]), ALU.add).then_inc(dve_step, 1)
                dve.wait_ge(act_step, 5)
                nc.vector.scalar_tensor_tensor(out=a[:, 1], in0=a[:, 0], scalar=0.0, in1=a[:, 1], op0=ALU.max, op1=ALU.add).then_inc(dve_step, 1)
                dve.wait_ge(dve_step, 2)
                nc.vector.scalar_tensor_tensor(out=a[:, 1], in0=a[:, 1], scalar=-1.0, in1=rates[:, 0:1, :].to_broadcast([P, NT, 2 * DH]), op0=ALU.mult, op1=ALU.mult).then_inc(dve_step, 1)
                dve.wait_ge(sums_done, 1)
                nc.vector.tensor_copy(a[:, 0].rearrange("p t (d h) -> p d t h", d=2), ps[:, 0, 0:W].rearrange("p (d t h) -> p d t h", d=2, t=NT)).then_inc(dve_step, 1)
                dve.wait_ge(dve_step, 4)
                nc.vector.tensor_tensor(a[:, 3], by_tile(ps[:, 1, 0:W]), a[:, 0], ALU.subtract).then_inc(dve_step, 1)
                nc.vector.tensor_copy(kind(0), split(a[:, 2])).then_inc(dve_step, 1)
                nc.vector.tensor_copy(kind(1), split(a[:, 0])).then_inc(dve_step, 1)
                nc.vector.tensor_copy(kind(5), split(a[:, 1])).then_inc(dve_step, 1)
                dve.wait_ge(act_step, 9)
                nc.vector.tensor_tensor(kind(2), kind(3), split(a[:, 2]), ALU.mult).then_inc(dve_step, 1)

            @block.tensor
            def _(pe):
                pe.wait_ge(dve_step, 3)
                la = a[:, 1]
                for d, mask in enumerate(("incl_f", "incl_b")):
                    dst = ps[:, 0, d * W // 2:(d + 1) * W // 2].rearrange("p (t h) -> p t h", h=DH)
                    nc.tensor.matmul(dst, k.c[mask], la[:, :, d * DH:(d + 1) * DH], start=True, stop=True)
                for bank, mask in ((1, "chunk"), (2, "half0"), (3, "half1")):
                    mm = nc.tensor.matmul(by_tile(ps[:, bank, 0:W]), k.c[mask], la, start=True, stop=True)
                mm.then_inc(sums_done, 1)


def delta(k, cols, odT):
    nc, ps = k.nc, k.psum
    M = 2 * NT
    NK = 8
    with ExitStack() as s:
        raw = sbuf(k, s, "dn_raw", [P, 3, T])
        z = sbuf(k, s, "dn_z", [P, LAT])
        kt = sbuf(k, s, "dn_tokens", [P, NT + LT, P])
        vt = sbuf(k, s, "dn_v", [P, NT, P])
        sq = sbuf(k, s, "dn_squares", [P, NT + LT, P])
        cs = sbuf(k, s, "dn_head_cols", [P, NK, M])
        nrm = sbuf(k, s, "dn_norms", [P, 3, NT + LT])
        kT = sbuf(k, s, "dn_kT", [P, T])
        qT = sbuf(k, s, "dn_qT", [P, LAT])
        dec = sbuf(k, s, "dn_decay", [P, M, P])
        fs = sbuf(k, s, "dn_decay_strict", [P, M, P])
        fi = sbuf(k, s, "dn_decay_incl", [P, 2, LT, P])
        A = sbuf(k, s, "dn_A", [P, M, P])
        rates = sbuf(k, s, "dn_rates", [P, M, P])
        QK = sbuf(k, s, "dn_QK", [P, 2, LT, P])
        R = sbuf(k, s, "dn_inverse_turned", [P, M, P])
        Ti = sbuf(k, s, "dn_inverse", [P, M, P])
        Y = sbuf(k, s, "dn_product", [P, M, P])
        kbg = sbuf(k, s, "dn_k_beta_g", [P, M, P])
        kdec = sbuf(k, s, "dn_k_decayed", [P, M, P])
        vb = sbuf(k, s, "dn_v_beta", [P, M, P])
        qg = sbuf(k, s, "dn_q_g", [P, 2, LT, P])
        qgT = sbuf(k, s, "dn_q_g_turned", [P, 2, LT, P])
        state = sbuf(k, s, "dn_state", [P, 2, P])
        W = sbuf(k, s, "dn_w_turned", [P, M, P])
        U = sbuf(k, s, "dn_u", [P, M, P])
        QKs = sbuf(k, s, "dn_QK_scan", [P, 2, LT, P])
        total = sbuf(k, s, "dn_chunk_decay", [P, 2, M])
        vn = sbuf(k, s, "dn_v_new", [P, 2, P])
        o = sbuf(k, s, "dn_o", [P, LT, P])
        onr = sbuf(k, s, "dn_o_norms", [P, 3, LT])
        nw = sbuf(k, s, "dn_norm_col", [P, 1])
        per = {
            "raw_in": 48, "z_in": 16, "raw_turned": 3, "k_tok": 1, "v_tok": 1, "q_tok": 1, "squares": 1, "norm_ms": 1, "norm_root": 1,
            "normed": 2, "turned_back": 2, "copied_back": 2, "head_cols": 1, "rates_spread": 2, "g_rows": 1, "diffs": 3, "decay_done": 2,
            "strict_done": 2, "incl_done": 2, "kk_done": 2, "a_done": 2, "qk_done": 2, "scaled": 9, "qk_copied": 1, "inv_pe": 72, "inv_dve": 102,
            "w_done": 1, "u_done": 1, "w_copied": 3, "u_copied": 3, "qg_turned": 1, "qg_copied": 1, "ws_done": 22, "kv_done": 22,
            "o_mm": 16, "vn_done": 22, "s_done": 22, "o_added": 16, "o_squares": 1, "o_ms": 1, "o_root": 1, "o_normed": 1,
            "o_turned": 1, "dn_step": 5, "out_step": 7, "o_zero": 1,
        }
        S = {n: k.sem("dn_" + n) for n in per}
        head_free, nw_in = k.sem("head_free"), k.sem("nw_in")
        order = [list(range(2 * NT)), [3, 2, 1, 0] + list(range(2 * NT - 1, 3, -1))]
        GROUPS = [(d, a, a + 2) for d in range(2) for a in range(0, NT, 2)]
        flat = lambda x: x.rearrange("p a b -> p (a b)")

        def at(h, name, j):
            return h * per[name] + j + 1

        def chunk(d, i):
            c = order[d][i]
            return c // 2, d * NT + c // 2, c % 2, slice((c % 2) * CHUNK, (c % 2 + 1) * CHUNK)

        SC = slice(0, P)
        ws_at = lambda d: slice(d * P, (d + 1) * P)
        o_at = lambda d: slice((2 + d) * P, (3 + d) * P)
        STEPS = 2 * NT
        first = lambda h: isinstance(h, int) and h == 0

        def changed(x, d, n):
            x = x.rearrange("p (c two b) -> p c two b", two=2, b=1 << n)
            return x[:, :, 1 - d, :]

        with nc.Block() as block:

            @block.sync
            def _(sp):
                sp.dma_start(nw[:, :], k.inp["dn_norm_w"].rearrange("a d -> d a")).then_inc(nw_in, 16)

                def load(h):
                    row = lambda g, a: k.feat_d[ds(g + h, 1), :, a:T].rearrange("a p t -> (a p) t")
                    sp.dma_start(raw[:, 0, :], row(G_DK, 0)).then_inc(S["raw_in"], 16)
                    sp.dma_start(raw[:, 1, :], row(G_DV, 0)).then_inc(S["raw_in"], 16)
                    sp.dma_start(raw[:, 2, CTX:T], row(G_DQ, CTX)).then_inc(S["raw_in"], 16)

                def load_z(h):
                    sp.dma_start(z[:, :], k.feat_d[ds(G_Z + h, 1), :, CTX:T].rearrange("a p t -> (a p) t")).then_inc(S["z_in"], 16)

                load(0)
                load_z(0)
                sp.wait_ge(S["raw_turned"], 3)
                load(1)
                with sp.Fori(1, DH - 1) as h:
                    sp.wait_ge(S["raw_turned"], 3 * h + 3)
                    load(h + 1)
                    sp.wait_ge(head_free, h + 1)
                    load_z(h)
                sp.wait_ge(head_free, DH)
                load_z(DH - 1)

            @block.tensor
            def _(pe):
                w = lambda name, h, j: pe.wait_ge(S[name], at(h, name, j))
                ident = k.c["ident"]
                col = lambda j: slice((j % 4) * P, (j % 4 + 1) * P)

                def prepare(h):
                    pe.wait_ge(S["raw_in"], 48 * h + 48)
                    if not first(h):
                        w("qg_copied", h - 1, 0)
                    for j, (bank, lo) in enumerate(((0, 0), (2, 0), (4, CT))):
                        for t in range(lo, NT):
                            tr = nc.tensor.transpose(ps[:, bank + (t - lo) // 4, col(t - lo)], raw[:, j, t * P:(t + 1) * P], ident)
                        tr.then_inc(S["raw_turned"], 1)
                    if not first(h):
                        pe.wait_ge(head_free, h)
                    w("rates_spread", h, 1)
                    for b in range(3):
                        mm = nc.tensor.matmul(ps[:, 5 + b, :], k.c["ones"], flat(rates[:, 4 * b:4 * b + 4, :]), start=True, stop=True)
                    mm.then_inc(S["g_rows"], 1)
                    w("k_tok", h, 0)
                    w("normed", h, 0)
                    for t in range(NT):
                        tr = nc.tensor.transpose(ps[:, t // 4, col(t)], kt[:, t, :], ident)
                    tr.then_inc(S["turned_back"], 1)
                    w("q_tok", h, 0)
                    w("normed", h, 1)
                    for t in range(LT):
                        tr = nc.tensor.transpose(ps[:, 4, col(t)], kt[:, NT + t, :], ident)
                    tr.then_inc(S["turned_back"], 1)
                    w("copied_back", h, 1)
                    w("v_tok", h, 0)
                    for t in range(NT):
                        mm = nc.tensor.matmul(ps[:, 2 + t // 4, col(t)], kT[:, t * P:(t + 1) * P], kT[:, t * P:(t + 1) * P], start=True, stop=True)
                    mm.then_inc(S["kk_done"], 1)
                    for t in range(LT):
                        mm = nc.tensor.matmul(ps[:, 4, col(t)], kT[:, (CT + t) * P:(CT + t + 1) * P], qT[:, t * P:(t + 1) * P], start=True, stop=True)
                    mm.then_inc(S["kk_done"], 1)
                    w("diffs", h, 2)
                    w("qk_done", h, 1)

                def inverse_products(h, n, phase, groups):
                    for g in groups:
                        d, a, b = GROUPS[g]
                        if phase == 1:
                            w("inv_dve", h, 18 * n + g)
                        elif n == 0:
                            w("a_done", h, d)
                        else:
                            w("inv_dve", h, 18 * (n - 1) + 6 + 2 * g + 1)
                        for j in range(a, b):
                            m = d * NT + j
                            c = slice((j - a) * P, (j - a + 1) * P)
                            if phase == 0:
                                mm = nc.tensor.matmul(ps[:, g, c], A[:, m, :], ident if n == 0 else R[:, m, :], start=True, stop=True)
                                continue
                            if n < 5:
                                mm = nc.tensor.matmul(ps[:, g, c], Y[:, m, :], ident if n == 0 else Ti[:, m, :], start=True, stop=True)
                            if n > 0:
                                compact = ps[:, g, 2 * P + (j - a) * CHUNK:2 * P + (j - a + 1) * CHUNK].rearrange("p (c b) -> p c b", b=1 << n)
                                mm = nc.tensor.matmul(compact, Ti[:, m, :], changed(Y[:, m, :], d, n), start=True, stop=True)
                        mm.then_inc(S["inv_pe"], 1)

                def scan_start(h, i):
                    for d in range(2):
                        t, m, half, rows = chunk(d, i)
                        if i > 0:
                            w("s_done", h, 2 * (i - 1) + d)
                            if i > 4 and d == 0:
                                w("o_added", h, 2 * (i - 5) + 1)
                            nc.tensor.matmul(ps[rows, 6, ws_at(d)], W[:, m, rows], state[:, d, :], start=True, stop=True).then_inc(S["ws_done"], 1)

                def new_v(d, i):
                    t, m, half, rows = chunk(d, i)
                    return vn[rows, d, :] if i > 0 else U[rows, m, :]

                def scan_out(h, i):
                    for d in range(2):
                        t, m, half, rows = chunk(d, i)
                        if i > 0:
                            w("vn_done", h, 2 * (i - 1) + d)
                        if i >= 4:
                            nc.tensor.matmul(ps[rows, 6, o_at(d)], qgT[:, d, t - CT, rows], state[:, d, :], start=True, stop=False)
                            nc.tensor.matmul(ps[rows, 6, o_at(d)], QKs[rows, d, t - CT, rows], new_v(d, i), start=False, stop=True).then_inc(S["o_mm"], 1)
                    scan_add(h, i, 0)

                def scan_add(h, i, d):
                    t, m, half, rows = chunk(d, i)
                    if i < STEPS - 1:
                        if d == 1:
                            w("s_done", h, 2 * i)
                        nc.tensor.matmul(ps[:, 7, SC], kdec[rows, m, :], new_v(d, i), start=True, stop=True).then_inc(S["kv_done"], 1)

                def combine(h):
                    if not first(h):
                        w("o_added", h - 1, 15)
                    w("scaled", h, 5)
                    w("inv_dve", h, 101)
                    for m in range(M):
                        mm = nc.tensor.matmul(ps[:, m // 4, col(m)], kbg[:, m, :], R[:, m, :], start=True, stop=True)
                    mm.then_inc(S["w_done"], 1)
                    for m in range(M):
                        mm = nc.tensor.matmul(ps[:, 3 + m // 4, col(m)], R[:, m, :], vb[:, m, :], start=True, stop=True)
                    mm.then_inc(S["u_done"], 1)
                    w("w_copied", h, 2)
                    w("scaled", h, 8)
                    for d in range(2):
                        for t in range(LT):
                            tr = nc.tensor.transpose(ps[:, d, col(t)], qg[:, d, t, :], ident)
                    tr.then_inc(S["qg_turned"], 1)

                def turn_out(h):
                    w("o_normed", h, 0)
                    for t in range(LT):
                        tr = nc.tensor.transpose(ps[:, 6, col(t)], o[:, t, :], ident)
                    tr.then_inc(S["o_turned"], 1)

                def turn(h):
                    prepare(h)
                    for i in range(STEPS):
                        inverse_products(h, i // 2, i % 2, (0, 1))
                        if not first(h):
                            scan_start(h - 1, i)
                        inverse_products(h, i // 2, i % 2, (2, 3))
                        if not first(h):
                            scan_out(h - 1, i)
                        inverse_products(h, i // 2, i % 2, (4, 5))
                        if not first(h):
                            scan_add(h - 1, i, 1)
                    combine(h)
                    if not first(h):
                        turn_out(h - 1)
                    w("u_copied", h, 2)
                    w("qk_copied", h, 0)
                    w("qg_copied", h, 0)

                turns(pe, DH, turn)
                for i in range(STEPS):
                    scan_start(DH - 1, i)
                    scan_out(DH - 1, i)
                    scan_add(DH - 1, i, 1)
                turn_out(DH - 1)

            @block.scalar
            def _(act):
                w = lambda name, h, j: act.wait_ge(S[name], at(h, name, j))
                copy = lambda dst, src: nc.scalar.activation(dst, src, ACT.Copy)

                def turn(h):
                    w("raw_turned", h, 0)
                    copy(flat(kt[:, 0:NT, :]), flat(ps[:, 0:2, :])[:, 0:T]).then_inc(S["k_tok"], 1)
                    w("raw_turned", h, 1)
                    copy(flat(vt[:, :, :]), flat(ps[:, 2:4, :])[:, 0:T]).then_inc(S["v_tok"], 1)
                    w("raw_turned", h, 2)
                    copy(flat(kt[:, NT:NT + LT, :]), ps[:, 4, :]).then_inc(S["q_tok"], 1)
                    w("q_tok", h, 0)
                    nc.scalar.activation(sq[:, :, :], kt[:, :, :], ACT.Square).then_inc(S["squares"], 1)
                    rsqrt_steps(k, None, act, nrm[:, 0, :], nrm[:, 1, :], None, (S["norm_ms"], at(h, "norm_ms", 0)), (S["norm_root"], 1), None, None)
                    w("turned_back", h, 0)
                    copy(kT[:, :], flat(ps[:, 0:2, :])[:, 0:T]).then_inc(S["copied_back"], 1)
                    w("turned_back", h, 1)
                    copy(qT[:, :], ps[:, 4, :]).then_inc(S["copied_back"], 1)
                    w("diffs", h, 2)
                    nc.scalar.activation(dec[:, :, :], dec[:, :, :], ACT.Abs).then_inc(S["decay_done"], 1)
                    w("decay_done", h, 0)
                    nc.scalar.activation(dec[:, :, :], dec[:, :, :], ACT.Exp, scale=-1.0).then_inc(S["decay_done"], 1)
                    w("w_done", h, 0)
                    for b in range(3):
                        copy(flat(W[:, 4 * b:4 * b + 4, :]), ps[:, b, :]).then_inc(S["w_copied"], 1)
                    w("u_done", h, 0)
                    for b in range(3):
                        copy(flat(U[:, 4 * b:4 * b + 4, :]), ps[:, 3 + b, :]).then_inc(S["u_copied"], 1)
                    copy(QKs[:, :, :, :], QK[:, :, :, :]).then_inc(S["qk_copied"], 1)
                    w("qg_turned", h, 0)
                    copy(qgT[:, :, :, :].rearrange("p d t c -> p (d t c)"), flat(ps[:, 0:2, :])).then_inc(S["qg_copied"], 1)
                    if not first(h):
                        out_root(h - 1)

                def out_root(h):
                    rsqrt_steps(k, None, act, onr[:, 0, :], onr[:, 1, :], None, (S["o_ms"], at(h, "o_ms", 0)), (S["o_root"], 1), None, None)

                turns(act, DH, turn)
                out_root(DH - 1)

            @block.vector
            def _(dve):
                st, out_steps = Count(), Count()
                v = nc.vector
                w = lambda name, h, j: dve.wait_ge(S[name], at(h, name, j))
                dve.sem_inc(head_free, 1)

                def prepare(h):
                    w("squares", h, 0)
                    v.tensor_reduce(nrm[:, 0, :], sq[:, :, :], AX_X, ALU.add).then_inc(S["dn_step"], 1)
                    dve.wait_ge(S["dn_step"], st.up())
                    v.tensor_scalar(nrm[:, 0, :], nrm[:, 0, :], EPS, None, ALU.add).then_inc(S["norm_ms"], 1)
                    rsqrt_steps(k, dve, None, nrm[:, 0, :], nrm[:, 1, :], nrm[:, 2, :], None, (S["norm_root"], at(h, "norm_root", 0)), S["dn_step"], st)
                    v.tensor_tensor(kt[:, 0:NT, :], kt[:, 0:NT, :], nrm[:, 2, 0:NT, None].to_broadcast([P, NT, P]), ALU.mult).then_inc(S["normed"], 1)
                    v.scalar_tensor_tensor(out=kt[:, NT:NT + LT, :], in0=kt[:, NT:NT + LT, :], scalar=float(HD) ** -0.5,
                                           in1=nrm[:, 2, NT:NT + LT, None].to_broadcast([P, LT, P]), op0=ALU.mult, op1=ALU.mult).then_inc(S["normed"], 1)
                    w("g_rows", h, 0)
                    w("head_cols", h, 0)
                    for b in range(3):
                        v.tensor_tensor(dec[:, 4 * b:4 * b + 4, :], ps[:, 5 + b, :].rearrange("p (a c) -> p a c", c=P),
                                        cs[:, 1, 4 * b:4 * b + 4, None].to_broadcast([P, 4, P]), ALU.subtract).then_inc(S["diffs"], 1)
                    w("kk_done", h, 0)
                    for d in range(2):
                        w("strict_done", h, d)
                        for t in range(NT):
                            m = d * NT + t
                            ins = v.scalar_tensor_tensor(out=A[:, m, :], in0=ps[:, 2 + t // 4, (t % 4) * P:(t % 4 + 1) * P], scalar=cs[:, 0, m:m + 1], in1=fs[:, m, :], op0=ALU.mult, op1=ALU.mult)
                        ins.then_inc(S["a_done"], 1)
                    w("kk_done", h, 1)
                    for d in range(2):
                        w("incl_done", h, d)
                        v.tensor_tensor(QK[:, d], ps[:, 4, :].rearrange("p (a c) -> p a c", c=P), fi[:, d], ALU.mult).then_inc(S["qk_done"], 1)

                def inverse_updates(h, n, phase, groups):
                    for g in groups:
                        d, a, b = GROUPS[g]
                        ms = slice(d * NT + a, d * NT + b)
                        product = ps[:, g, 0:2 * P].rearrange("p (a c) -> p a c", c=P)
                        w("inv_pe", h, 12 * n + 6 * phase + g)
                        if phase == 0:
                            mask = k.c[f"level_{'fb'[d]}{n}"]
                            v.tensor_tensor(Y[:, ms, :], product, mask[:, None, :].to_broadcast([P, 2, P]), ALU.mult).then_inc(S["inv_dve"], 1)
                        elif n == 0:
                            one = k.c["ident"][:, None, :].to_broadcast([P, 2, P])
                            v.tensor_tensor(R[:, ms, :], one, Y[:, ms, :], ALU.subtract).then_inc(S["inv_dve"], 1)
                            v.tensor_tensor(Ti[:, ms, :], one, product, ALU.subtract).then_inc(S["inv_dve"], 1)
                        else:
                            part = changed(flat(R[:, ms, :]), d, n)
                            v.tensor_tensor(part, part, ps[:, g, 2 * P:3 * P].rearrange("p (c b) -> p c b", b=1 << n), ALU.subtract).then_inc(S["inv_dve"], 1)
                            if n < 5:
                                v.tensor_tensor(Ti[:, ms, :], Ti[:, ms, :], product, ALU.subtract).then_inc(S["inv_dve"], 1)

                def scan_start(h, i):
                    for d in range(2):
                        t, m, half, rows = chunk(d, i)
                        if i > 0:
                            w("ws_done", h, 2 * (i - 1) + d)
                            v.tensor_tensor(vn[rows, d, :], U[rows, m, :], ps[rows, 6, ws_at(d)], ALU.subtract).then_inc(S["vn_done"], 1)

                def scan_add(h, i, d):
                    t, m, half, rows = chunk(d, i)
                    if i < STEPS - 1:
                        w("kv_done", h, 2 * i + d)
                    if i == 0:
                        v.tensor_copy(state[:, d, :], ps[:, 7, SC]).then_inc(S["s_done"], 1)
                    elif i < STEPS - 1:
                        v.scalar_tensor_tensor(out=state[:, d, :], in0=state[:, d, :], scalar=total[:, half, m:m + 1], in1=ps[:, 7, SC], op0=ALU.mult, op1=ALU.add).then_inc(S["s_done"], 1)

                def scan_out(h, i):
                    scan_add(h, i, 0)
                    for d in range(2):
                        t, m, half, rows = chunk(d, i)
                        if i >= 4:
                            w("o_mm", h, 2 * (i - 4) + d)
                            if i > 4:
                                w("o_added", h, 2 * (i - 5) + 1)
                            v.tensor_tensor(o[rows, t - CT, :], o[rows, t - CT, :], ps[rows, 6, o_at(d)], ALU.add).then_inc(S["o_added"], 1)

                def finish(h):
                    w("o_squares", h, 0)
                    v.tensor_reduce(onr[:, 0, :], sq[:, 0:LT, :], AX_X, ALU.add).then_inc(S["out_step"], 1)
                    dve.wait_ge(S["out_step"], out_steps.up())
                    v.tensor_scalar(onr[:, 0, :], onr[:, 0, :], 1.0 / HD, EPS, ALU.mult, ALU.add).then_inc(S["o_ms"], 1)
                    rsqrt_steps(k, dve, None, onr[:, 0, :], onr[:, 1, :], onr[:, 2, :], None, (S["o_root"], at(h, "o_root", 0)), S["out_step"], out_steps)
                    v.tensor_tensor(o[:, :, :], o[:, :, :], onr[:, 2, :, None].to_broadcast([P, LT, P]), ALU.mult).then_inc(S["o_normed"], 1)
                    w("o_turned", h, 0)
                    dve.wait_ge(S["z_in"], 16 * h + 16)
                    dve.wait_ge(nw_in, 16)
                    v.scalar_tensor_tensor(out=z[:, :], in0=ps[:, 6, :], scalar=nw[:, 0:1], in1=z[:, :], op0=ALU.mult, op1=ALU.mult).then_inc(S["out_step"], 1)
                    dve.wait_ge(S["out_step"], out_steps.up())
                    high, low = (x[:, ds(h, 1), :].rearrange("p a t -> p (a t)") for x in odT)
                    v.tensor_copy(high, z[:, :]).then_inc(S["out_step"], 1)
                    dve.wait_ge(S["out_step"], out_steps.up())
                    v.tensor_tensor(low, z[:, :], exact(high), ALU.subtract).then_inc(head_free, 1)

                def turn(h):
                    prepare(h)
                    for i in range(STEPS):
                        inverse_updates(h, i // 2, i % 2, (0, 1))
                        if not first(h):
                            if i == 0:
                                w("o_zero", h - 1, 0)
                            scan_start(h - 1, i)
                        inverse_updates(h, i // 2, i % 2, (2, 3))
                        if not first(h):
                            scan_out(h - 1, i)
                        inverse_updates(h, i // 2, i % 2, (4, 5))
                        if not first(h):
                            scan_add(h - 1, i, 1)
                    if not first(h):
                        finish(h - 1)
                    v.memset(o[:, :, :], 0.0).then_inc(S["o_zero"], 1)

                PREP, OUT = 5, 7
                turn(0)
                with dve.Fori(1, DH) as h:
                    st.enter(h - 1, PREP)
                    out_steps.enter(h - 1, OUT)
                    turn(h)
                st.leave(DH - 1)
                out_steps.leave(DH - 1)
                w("u_copied", DH - 1, 2)
                w("o_zero", DH - 1, 0)
                for i in range(STEPS):
                    scan_start(DH - 1, i)
                    scan_out(DH - 1, i)
                    scan_add(DH - 1, i, 1)
                finish(DH - 1)

            @block.gpsimd
            def _(pool):
                g = nc.gpsimd
                w = lambda name, h, j: pool.wait_ge(S[name], at(h, name, j))
                spread = lambda x, n: x[:, :, None].to_broadcast([P, n, P])

                def turn(h):
                    if not first(h):
                        w("g_rows", h - 1, 0)
                    for d, mask in enumerate(("incl_f", "incl_b")):
                        rate = cols[:, ds(h, 1), 5, d].rearrange("p a t -> p (a t)")
                        g.tensor_tensor(rates[:, d * NT:(d + 1) * NT, :], k.c[mask][:, None, :].to_broadcast([P, NT, P]), spread(rate, NT), ALU.mult).then_inc(S["rates_spread"], 1)
                    if not first(h):
                        w("qg_turned", h - 1, 0)
                        pool.wait_ge(head_free, h)
                    g.tensor_copy(cs[:, :, :], cols[:, ds(h, 1)].rearrange("p a k d t -> p (a k) (d t)")).then_inc(S["head_cols"], 1)
                    w("head_cols", h, 0)
                    w("decay_done", h, 1)
                    for d in range(2):
                        ms = slice(d * NT, (d + 1) * NT)
                        strict = k.c[f"strict_{'fb'[d]}"]
                        g.tensor_tensor(fs[:, ms, :], dec[:, ms, :], strict[:, None, :].to_broadcast([P, NT, P]), ALU.mult).then_inc(S["strict_done"], 1)
                    for d in range(2):
                        g.tensor_tensor(fi[:, d], dec[:, d * NT + CT:(d + 1) * NT, :], k.c[f"incl_{'fb'[d]}"][:, None, :].to_broadcast([P, LT, P]), ALU.mult).then_inc(S["incl_done"], 1)
                    w("normed", h, 1)
                    w("v_tok", h, 0)
                    for d in range(2):
                        ms = slice(d * NT, (d + 1) * NT)
                        g.tensor_tensor(kbg[:, ms, :], kt[:, 0:NT, :], spread(cs[:, 2, ms], NT), ALU.mult).then_inc(S["scaled"], 1)
                        g.tensor_tensor(vb[:, ms, :], vt[:, :, :], spread(cs[:, 0, ms], NT), ALU.mult).then_inc(S["scaled"], 1)
                        g.tensor_tensor(qg[:, d], kt[:, NT:NT + LT, :], spread(cs[:, 3, d * NT + CT:(d + 1) * NT], LT), ALU.mult).then_inc(S["scaled"], 1)
                    if not first(h):
                        w("kv_done", h - 1, 21)
                        w("s_done", h - 1, 21)
                    for d in range(2):
                        ms = slice(d * NT, (d + 1) * NT)
                        g.tensor_tensor(kdec[:, ms, :], kt[:, 0:NT, :], spread(cs[:, 4, ms], NT), ALU.mult).then_inc(S["scaled"], 1)
                    g.tensor_copy(total[:, :, :], cs[:, 6:8, :]).then_inc(S["scaled"], 1)
                    if not first(h):
                        out_squares(h - 1)

                def out_squares(h):
                    w("o_added", h, 15)
                    g.tensor_tensor(sq[:, 0:LT, :], o[:, :, :], o[:, :, :], ALU.mult).then_inc(S["o_squares"], 1)

                turns(pool, DH, turn)
                out_squares(DH - 1)


def merge(k, oT, odT, yT, x1):
    nc, ps = k.nc, k.psum
    HALF, GROUPS = 2 * P, D // P
    with ExitStack() as s:
        raw = x1[:, :, :].rearrange("p a n -> p (a n)").rearrange("p (b k n) -> p b k n", b=2, k=2 * QH)
        wh = sbuf(k, s, "branch_high", [P, 2, 2 * QH, P], F32R)
        wl = sbuf(k, s, "branch_low", [P, 2, 2 * QH, P], F32R)
        gate = sbuf(k, s, "gate_rows", [P, 2, 2, LAT])
        gate_in = [k.sem("gate_in0"), k.sem("gate_in1")]
        w_in = [k.sem("branch_in0"), k.sem("branch_in1")]
        high_done, low_done = k.sem("branch_high_done"), k.sem("branch_low_done")
        products_done, step, y_done = k.sem("branch_done"), k.sem("gate_step"), k.sem("y_done")
        sources = [k.inp[n].rearrange("a (h p) n -> (a p) h n", p=P) for n in ("w_branch_attn", "w_branch_dn")]
        with nc.Block() as block:

            @block.sync
            def _(sp):
                def load(i):
                    for j in range(4):
                        g = 4 * i + j
                        if j % 2 == 0:
                            if not isinstance(i, int):
                                sp.wait_ge(low_done, g - 2)
                            for branch in range(2):
                                sp.dma_start(raw[:, j // 2, branch * QH:(branch + 1) * QH, :], sources[branch][:, :, ds((2 * i + j // 2) * HALF, HALF)]).then_inc(w_in[j // 2], 16)
                        if not (isinstance(i, int) and j < 2):
                            sp.wait_ge(y_done, g - 1)
                        for branch in range(2):
                            row = k.feat_d[ds(G_GATE + branch * GROUPS + g, 1), :, CTX:T].rearrange("a p t -> (a p) t")
                            sp.dma_start(gate[:, j % 2, branch], row).then_inc(gate_in[j % 2], 16)

                turns(sp, GROUPS // 4, load)

            @block.scalar
            def _(act):
                def high(i):
                    for j in range(4):
                        act.wait_ge(w_in[j // 2], 32 * i + 32)
                        if not (isinstance(i, int) and j < 2):
                            act.wait_ge(products_done, 4 * i + j - 1)
                        nc.scalar.activation(wh[:, j % 2], raw[:, j // 2, :, (j % 2) * P:(j % 2 + 1) * P], ACT.Copy).then_inc(high_done, 1)

                turns(act, GROUPS // 4, high)

            @block.gpsimd
            def _(pool):
                with pool.Fori(0, GROUPS // 4) as i:
                    for j in range(4):
                        pool.wait_ge(high_done, 4 * i + j + 1)
                        nc.gpsimd.tensor_tensor(wl[:, j % 2], raw[:, j // 2, :, (j % 2) * P:(j % 2 + 1) * P], exact(wh[:, j % 2]), ALU.subtract).then_inc(low_done, 1)

            @block.tensor
            def _(pe):
                def groups(i):
                    for j in range(4):
                        pe.wait_ge(low_done, 4 * i + j + 1)
                        if not (isinstance(i, int) and j < 2):
                            pe.wait_ge(y_done, 4 * i + j - 1)
                        for branch, src in enumerate((oT, odT)):
                            for h in range(QH):
                                m = branch * QH + h
                                mm = split_products(nc, ps[:, 2 * (j % 2) + branch, :], (wh[:, j % 2, m, :], wl[:, j % 2, m, :]), [x[:, h, :] for x in src], h == 0, h == QH - 1)
                        mm.then_inc(products_done, 1)

                turns(pe, GROUPS // 4, groups)

            @block.vector
            def _(dve):
                with dve.Fori(0, GROUPS // 4) as i:
                    for j in range(4):
                        g = 4 * i + j
                        dve.wait_ge(gate_in[j % 2], 64 * i + 32 * (j // 2) + 32)
                        dve.wait_ge(products_done, g + 1)
                        for branch in range(2):
                            nc.vector.tensor_tensor(gate[:, j % 2, branch, :], ps[:, 2 * (j % 2) + branch, :], gate[:, j % 2, branch, :], ALU.mult).then_inc(step, 1)
                        dve.wait_ge(step, 4 * g + 2)
                        whole = gate[:, j % 2, 0, :]
                        nc.vector.tensor_tensor(whole, whole, gate[:, j % 2, 1, :], ALU.add).then_inc(step, 1)
                        dve.wait_ge(step, 4 * g + 3)
                        high, low = (x[:, ds(g, 1), :].rearrange("p a t -> p (a t)") for x in yT)
                        nc.vector.tensor_copy(high, whole).then_inc(step, 1)
                        dve.wait_ge(step, 4 * g + 4)
                        nc.vector.tensor_tensor(low, whole, exact(high), ALU.subtract).then_inc(y_done, 1)


def residual(k, yT, x1):
    nc, ps = k.nc, k.psum
    NGR, RW = D // P, 256
    NCH = D // RW
    with ExitStack() as s:
        w = sbuf(k, s, "w_out_chunk", [P, 2, NGR, RW])
        wh = sbuf(k, s, "w_out_high", [P, 2, NGR, RW], F32R)
        wl = sbuf(k, s, "w_out_low", [P, 2, NGR, RW], F32R)
        g1 = sbuf(k, s, "g1_rows", [P, D])
        part = sbuf(k, s, "mix_part", [P, 2, RW])
        w_in = [k.sem("w_out_in0"), k.sem("w_out_in1")]
        high_done, low_done = k.sem("w_out_high_done"), k.sem("w_out_low_done")
        x_in, mix_done, gated, added = k.sem("x1_in"), k.sem("mix_done"), k.sem("mix_gated"), k.sem("mix_added")
        wo = k.inp["w_out"].rearrange("a (g p) n -> (a p) g n", p=P)
        with nc.Block() as block:

            @block.sync
            def _(sp):
                def load(c, b):
                    sp.dma_start(w[:, b], wo[:, :, ds(c * RW, RW)]).then_inc(w_in[b], 16)

                load(0, 0)
                load(1, 1)
                sp.dma_start(g1[:, :], k.mod_d[0:1, 2 * D:3 * D].to_broadcast([P, D])).then_inc(x_in, 16)
                sp.dma_start(x1[:, :, :], k.inp["x"].rearrange("a (t p) d -> (a p) t d", p=P)).then_inc(x_in, 16)
                with sp.Fori(1, NCH // 2) as i:
                    for b in range(2):
                        sp.wait_ge(low_done, 2 * i + b - 1)
                        load(2 * i + b, b)

            @block.scalar
            def _(act):
                def high(c, b):
                    act.wait_ge(w_in[b], 8 * (c - b) + 16)
                    if not (isinstance(c, int) and c < 2):
                        act.wait_ge(mix_done, LT * (c - 1))
                    nc.scalar.activation(wh[:, b], w[:, b], ACT.Copy).then_inc(high_done, 1)

                high(0, 0)
                high(1, 1)
                with act.Fori(1, NCH // 2) as i:
                    for b in range(2):
                        high(2 * i + b, b)

            @block.tensor
            def _(pe):
                def chunks(i):
                    for b in range(2):
                        c = 2 * i + b
                        pe.wait_ge(low_done, c + 1)
                        for t in range(LT):
                            if not (isinstance(c, int) and c == 0):
                                pe.wait_ge(gated, LT * c + t - 3)
                            for g in range(NGR):
                                tile = [x[:, g, t * P:(t + 1) * P] for x in yT]
                                mm = split_products(nc, ps[:, t, 0:RW], tile, (wh[:, b, g, :], wl[:, b, g, :]), g == 0, g == NGR - 1)
                            mm.then_inc(mix_done, 1)

                turns(pe, NCH // 2, chunks)

            @block.vector
            def _(dve):
                def low(c, b):
                    dve.wait_ge(high_done, c + 1)
                    nc.vector.tensor_tensor(wl[:, b], w[:, b], exact(wh[:, b]), ALU.subtract).then_inc(low_done, 1)

                def gate(c):
                    for t in range(LT):
                        n = LT * c + t
                        dve.wait_ge(mix_done, n + 1)
                        if not (isinstance(n, int) and n < 2):
                            dve.wait_ge(added, n - 1)
                        nc.vector.tensor_tensor(part[:, t % 2, :], ps[:, t, 0:RW], g1[:, ds(c * RW, RW)], ALU.mult).then_inc(gated, 1)
                        dve.wait_ge(gated, n + 1)
                        xs = x1[:, t, ds(c * RW, RW)]
                        nc.vector.tensor_tensor(xs, xs, part[:, t % 2, :], ALU.add).then_inc(added, 1)

                low(0, 0)
                low(1, 1)
                dve.wait_ge(x_in, 32)
                gate(0)
                with dve.Fori(0, NCH // 2 - 1) as i:
                    low(2 * i + 2, 0)
                    gate(2 * i + 1)
                    low(2 * i + 3, 1)
                    gate(2 * i + 2)
                gate(NCH - 1)


def second_norm(k, x1, h2T):
    nc, ps = k.nc, k.psum
    with ExitStack() as s:
        h2 = sbuf(k, s, "h2", [P, LT, D])
        rows = sbuf(k, s, "norm2_rows", [P, 3, D])
        h2_out = k.sem("h2_out")
        ss = sbuf(k, s, "norm2_sums", [P, 3, LT])
        rows_in, sums, ms_done, root_done, step = k.sem("norm2_rows_in"), k.sem("norm2_sums_done"), k.sem("norm2_ms"), k.sem("norm2_root"), k.sem("norm2_step")
        h2_done, turned, high_done, low_done = k.sem("h2_done"), k.sem("h2_turned"), k.sem("h2_high_done"), k.sem("h2_low_done")
        with nc.Block() as block:

            @block.sync
            def _(sp):
                sp.dma_start(rows[:, 0, :], k.inp["norm2_w"].to_broadcast([P, D])).then_inc(rows_in, 16)
                sp.dma_start(rows[:, 1, :], k.mod_d[0:1, 4 * D:5 * D].to_broadcast([P, D])).then_inc(rows_in, 16)
                sp.dma_start(rows[:, 2, :], k.mod_d[0:1, 3 * D:4 * D].to_broadcast([P, D])).then_inc(rows_in, 16)
                for t in range(LT):
                    sp.wait_ge(h2_done, t + 1)
                    sp.dma_start(k.h2_d[t], h2[:, t, :]).then_inc(h2_out, 16)
                sp.wait_ge(h2_out, 16 * LT)

            @block.scalar
            def _(act):
                for t in range(LT):
                    nc.scalar.activation(h2[:, t, :], x1[:, t, :], ACT.Square, accum_out=ss[:, 0, t:t + 1]).then_inc(sums, 1)
                rsqrt_steps(k, None, act, ss[:, 0, :], ss[:, 1, :], None, (ms_done, 1), (root_done, 1), None, None)
                for kk in range(KD):
                    act.wait_ge(turned, kk + 1)
                    nc.scalar.activation(h2T[0][:, kk, :], ps[:, kk % 8, :], ACT.Copy).then_inc(high_done, 1)

            @block.vector
            def _(dve):
                st = Count()
                dve.wait_ge(rows_in, 48)
                nc.vector.scalar_tensor_tensor(out=rows[:, 0, :], in0=rows[:, 1, :], scalar=1.0, in1=rows[:, 0, :], op0=ALU.add, op1=ALU.mult).then_inc(step, 1)
                st.up()
                dve.wait_ge(sums, LT)
                nc.vector.tensor_scalar(ss[:, 0, :], ss[:, 0, :], 1.0 / D, EPS, ALU.mult, ALU.add).then_inc(ms_done, 1)
                rsqrt_steps(k, dve, None, ss[:, 0, :], ss[:, 1, :], ss[:, 2, :], None, (root_done, 1), step, st)
                for t in range(LT):
                    nc.vector.scalar_tensor_tensor(out=h2[:, t, :], in0=x1[:, t, :], scalar=ss[:, 2, t:t + 1], in1=rows[:, 0, :], op0=ALU.mult, op1=ALU.mult).then_inc(step, 1)
                    dve.wait_ge(step, st.up())
                    nc.vector.tensor_tensor(h2[:, t, :], h2[:, t, :], rows[:, 2, :], ALU.add).then_inc(h2_done, 1)
                for kk in range(KD):
                    dve.wait_ge(high_done, kk + 1)
                    nc.vector.tensor_tensor(h2T[1][:, kk, :], ps[:, kk % 8, :], exact(h2T[0][:, kk, :]), ALU.subtract).then_inc(low_done, 1)

            @block.tensor
            def _(pe):
                pe.wait_ge(h2_done, LT)
                for kk in range(KD):
                    if kk >= 8:
                        pe.wait_ge(low_done, kk - 7)
                    for t in range(LT):
                        tr = nc.tensor.transpose(ps[:, kk % 8, t * P:(t + 1) * P], h2[:, t, kk:D:KD], k.c["ident"])
                    tr.then_inc(turned, 1)


def routes(k, h2T, experts, weights):
    nc, ps = k.nc, k.psum
    NF = 2 * PH
    K2 = TOPK * TOPK
    with ExitStack() as s:
        raw = sbuf(k, s, "w_q_raw", [P, 2, KD, P])
        wh = sbuf(k, s, "w_q_high", [P, 2, KD, P], F32R)
        wl = sbuf(k, s, "w_q_low", [P, 2, KD, P], F32R)
        qT = sbuf(k, s, "queries", [P, 2, LAT])
        sk = sbuf(k, s, "sub_keys", [P, NF, P])
        skT = sbuf(k, s, "sub_keys_turned", [P, NF, P])
        sc = sbuf(k, s, "key_scores", [P, 4, LT, NKEYS])
        top = sbuf(k, s, "top_scores", [P, LT, 2, TOPK])
        topi = sbuf(k, s, "top_index", [P, LT, 2, TOPK], U32)
        topf = sbuf(k, s, "top_index_f", [P, LT, 2, TOPK])
        cand = sbuf(k, s, "candidates", [P, LT, K2])
        best = sbuf(k, s, "best_scores", [P, LT, PH, TOPK])
        best1 = sbuf(k, s, "best_of_head", [P, LT, TOPK])
        pos = sbuf(k, s, "best_places", [P, LT, TOPK], U32)
        half = sbuf(k, s, "best_halves", [P, 2, LT, TOPK], U32)
        halff = sbuf(k, s, "best_halves_f", [P, 2, LT, TOPK])
        hit = sbuf(k, s, "place_hits", [P, LT, TOPK, TOPK])
        keyf = sbuf(k, s, "best_keys", [P, 2, LT, TOPK])
        sums = sbuf(k, s, "weight_sums", [P, 2, LT, PH])
        w_in = [k.sem("w_q_in0"), k.sem("w_q_in1")]
        sk_in, sk_turned, sk_taken, q_done, q_taken = k.sem("sk_in"), k.sem("sk_turned"), k.sem("sk_taken"), k.sem("q_done"), k.sem("q_taken")
        high_done, low_done = k.sem("w_q_high_done"), k.sem("w_q_low_done")
        scores, scores_taken, step, shifted, exps, ranked = k.sem("key_scores_done"), k.sem("key_scores_taken"), k.sem("route_step"), k.sem("shifted"), k.sem("route_exp"), k.sem("head_ranked")
        wq = k.inp["peer_w_q"].rearrange("a (p k) n -> (a p) k n", k=KD)
        LOW = -3.0e38
        TURNS = NF // 4
        with nc.Block() as block:

            @block.sync
            def _(sp):
                def load(g, b):
                    sp.dma_start(raw[:, b], wq[:, :, ds(g * P, P)]).then_inc(w_in[b], 16)

                load(0, 0)
                load(1, 1)
                sp.dma_start(sk[:, :, :], k.inp["peer_sub_keys"].rearrange("a h c k d -> k (a h c) d")).then_inc(sk_in, 16)
                with sp.Fori(1, NF // 2) as i:
                    for b in range(2):
                        sp.wait_ge(low_done, 2 * i + b - 1)
                        load(2 * i + b, b)

            @block.gpsimd
            def _(pool):
                with pool.Fori(0, NF // 2) as i:
                    for b in range(2):
                        pool.wait_ge(high_done, 2 * i + b + 1)
                        nc.gpsimd.tensor_tensor(wl[:, b], raw[:, b], exact(wh[:, b]), ALU.subtract).then_inc(low_done, 1)

            @block.tensor
            def _(pe):
                pe.wait_ge(sk_in, 16)
                for f in range(NF):
                    tr = nc.tensor.transpose(ps[:, 4 + f // 4, (f % 4) * P:(f % 4 + 1) * P], sk[:, f, :], k.c["ident"])
                tr.then_inc(sk_turned, 1)

                def queries(g, b):
                    pe.wait_ge(low_done, g + 1)
                    if not (isinstance(g, int) and g < 2):
                        pe.wait_ge(q_taken, g - 1)
                    for kk in range(KD):
                        mm = split_products(nc, ps[:, b, :], (wh[:, b, kk, :], wl[:, b, kk, :]), [x[:, kk, :] for x in h2T], kk == 0, kk == KD - 1)
                    mm.then_inc(q_done, 1)

                def key_scores(g, b):
                    pe.wait_ge(q_taken, g + 1)
                    if not (isinstance(g, int) and g < 2):
                        pe.wait_ge(scores_taken, g - 1)
                    for t in range(LT):
                        mm = nc.tensor.matmul(ps[:, 2 + b, t * P:(t + 1) * P], qT[:, b, t * P:(t + 1) * P], skT[:, ds(g, 1), :].rearrange("p a n -> p (a n)"), start=True, stop=True)
                    mm.then_inc(scores, 1)

                queries(0, 0)
                queries(1, 1)
                pe.wait_ge(sk_taken, 1)
                key_scores(0, 0)
                with pe.Fori(1, NF // 2) as i:
                    queries(2 * i, 0)
                    key_scores(2 * i - 1, 1)
                    queries(2 * i + 1, 1)
                    key_scores(2 * i, 0)
                key_scores(NF - 1, 1)

            @block.scalar
            def _(act):
                def high(g, b):
                    act.wait_ge(w_in[b], 8 * (g - b) + 16)
                    nc.scalar.activation(wh[:, b], raw[:, b], ACT.Copy).then_inc(high_done, 1)

                def take_queries(g, b):
                    act.wait_ge(q_done, g + 1)
                    if not (isinstance(g, int) and g < 2):
                        act.wait_ge(scores, g - 1)
                    nc.scalar.activation(qT[:, b, :], ps[:, b, :], ACT.Copy).then_inc(q_taken, 1)

                def take_scores(i, place):
                    g = 4 * i + place
                    act.wait_ge(scores, g + 1)
                    if not (isinstance(g, int) and g < 4):
                        act.wait_ge(ranked, 2 * i + place // 2 - 1)
                    nc.scalar.activation(sc[:, place].rearrange("p t n -> p (t n)"), ps[:, 2 + place % 2, :], ACT.Copy).then_inc(scores_taken, 1)

                high(0, 0)
                high(1, 1)
                act.wait_ge(sk_turned, 1)
                nc.scalar.activation(skT[:, :, :].rearrange("p f n -> p (f n)"), ps[:, 4:8, :].rearrange("p b n -> p (b n)"), ACT.Copy).then_inc(sk_taken, 1)

                def groups(i):
                    last = isinstance(i, int) and i == TURNS - 1
                    for j in range(4):
                        g = 4 * i + j
                        take_queries(g, j % 2)
                        if not (last and j >= 2):
                            high(g + 2, j % 2)
                        if j:
                            take_scores(i, j - 1)
                        elif not (isinstance(i, int) and i == 0):
                            take_scores(i - 1, 3)

                groups(0)
                with act.Fori(1, TURNS - 1) as i:
                    groups(i)
                groups(TURNS - 1)
                take_scores(TURNS - 1, 3)
                act.wait_ge(shifted, 1)
                nc.scalar.activation(best[:, :, :, :], best[:, :, :, :], ACT.Exp).then_inc(exps, 1)

            @block.vector
            def _(dve):
                st = Count()
                v = nc.vector

                def top16(lists):
                    def step_all(op):
                        for values, places, data in lists:
                            op(values, places, data).then_inc(step, 1)
                        return st.up(len(lists))

                    hold(k, dve, step, step_all(lambda values, places, data: v.max(values[:, 0:8], data)))
                    step_all(lambda values, places, data: v.max_index(places[:, 0:8], values[:, 0:8], data))
                    hold(k, dve, step, step_all(lambda values, places, data: v.match_replace(data, values[:, 0:8], data, LOW)))
                    hold(k, dve, step, step_all(lambda values, places, data: v.max(values[:, 8:16], data)))
                    step_all(lambda values, places, data: v.max_index(places[:, 8:16], values[:, 8:16], data))

                with dve.Fori(0, TURNS) as i:
                    st.enter(i, 2 * 72)
                    for b in range(2):
                        h = 2 * i + b
                        for c in range(2):
                            hold(k, dve, scores_taken, 4 * i + 2 * b + c + 1)
                            top16([(top[:, t, c], topi[:, t, c], sc[:, 2 * b + c, t]) for t in range(LT)])
                        dve.wait_ge(step, st.up(0))
                        v.tensor_copy(topf[:, :, :, :], topi[:, :, :, :]).then_inc(ranked, 1)
                        square = [P, LT, TOPK, TOPK]
                        v.tensor_tensor(cand[:, :, :].rearrange("p t (a b) -> p t a b", b=TOPK), top[:, :, 0, :, None].to_broadcast(square),
                                        top[:, :, 1, None, :].to_broadcast(square), ALU.add).then_inc(step, 1)
                        hold(k, dve, step, st.up())
                        top16([(best1[:, t], pos[:, t], cand[:, t]) for t in range(LT)])
                        dve.wait_ge(step, st.up(0))
                        v.tensor_single_scalar(half[:, 0], pos[:, :, :], 4, ALU.logical_shift_right).then_inc(step, 1)
                        v.tensor_single_scalar(half[:, 1], pos[:, :, :], TOPK - 1, ALU.bitwise_and).then_inc(step, 1)
                        v.tensor_copy(best[:, :, ds(h, 1), :].rearrange("p t a n -> p t (a n)"), best1[:, :, :]).then_inc(step, 1)
                        dve.wait_ge(step, st.up(3))
                        v.tensor_copy(halff[:, :, :, :], half[:, :, :, :]).then_inc(step, 1)
                        dve.wait_ge(step, st.up())
                        for c in range(2):
                            v.tensor_tensor(hit[:, :, :, :], halff[:, c, :, :, None].to_broadcast(square), k.c["iota16"][:, None, None, :].to_broadcast(square), ALU.is_equal).then_inc(step, 1)
                            dve.wait_ge(step, st.up())
                            v.tensor_tensor(hit[:, :, :, :], hit[:, :, :, :], topf[:, :, c, None, :].to_broadcast(square), ALU.mult).then_inc(step, 1)
                            dve.wait_ge(step, st.up())
                            v.tensor_reduce(keyf[:, c], hit[:, :, :, :], AX_X, ALU.add).then_inc(step, 1)
                            dve.wait_ge(step, st.up())
                        v.scalar_tensor_tensor(out=experts[:, :, ds(h * TOPK, TOPK)], in0=keyf[:, 0], scalar=float(NKEYS), in1=keyf[:, 1], op0=ALU.mult, op1=ALU.add).then_inc(step, 1)
                        dve.wait_ge(step, st.up())
                st.leave(TURNS)
                flat = lambda x: x.rearrange("p t h n -> p (t h) n")
                v.tensor_copy(sums[:, 0], best[:, :, :, 0]).then_inc(step, 1)
                dve.wait_ge(step, st.up())
                v.tensor_tensor(flat(best[:, :, :, :]), flat(best[:, :, :, :]), sums[:, 0].rearrange("p t h -> p (t h)")[:, :, None].to_broadcast([P, LT * PH, TOPK]), ALU.subtract).then_inc(shifted, 1)
                dve.wait_ge(exps, 1)
                v.tensor_reduce(sums[:, 0].rearrange("p t h -> p (t h)"), flat(best[:, :, :, :]), AX_X, ALU.add).then_inc(step, 1)
                dve.wait_ge(step, st.up())
                v.reciprocal(sums[:, 1], sums[:, 0]).then_inc(step, 1)
                dve.wait_ge(step, st.up())
                v.tensor_tensor(weights[:, :, :].rearrange("p t (h n) -> p (t h) n", n=TOPK), flat(best[:, :, :, :]),
                                sums[:, 1].rearrange("p t h -> p (t h)")[:, :, None].to_broadcast([P, LT * PH, TOPK]), ALU.mult).then_inc(step, 1)


def expert_layer(k, x1, experts, weights):
    nc = k.nc
    RING, TURN = 8, 16
    PER = PH * TOPK
    with ExitStack() as s:
        ring = sbuf(k, s, "expert_rows", [P, RING, D])
        idx = sbuf(k, s, "gather_index", [P, 2, RING], I32)
        h2s = sbuf(k, s, "h2_tile", [P, D])
        y = sbuf(k, s, "expert_sum", [P, D])
        rows = sbuf(k, s, "final_rows", [P, 2, D])
        hid16 = sbuf(k, s, "hidden_turn", [P, TURN])
        hid = sbuf(k, s, "hidden", [P, PER])
        acts = sbuf(k, s, "expert_acts", [P, PER])
        ss = sbuf(k, s, "final_sums", [P, 4])
        rows_in, used, h2_in = k.sem("final_rows_in"), k.sem("rows_used"), k.sem("h2_tile_in")
        row_in = [k.sem(f"row_in{b}") for b in range(RING)]
        idx_ready, hid_done, gelu_done, step = k.sem("idx_ready"), k.sem("hidden_done"), k.sem("gelu_done"), k.sem("expert_step")
        x2_done, sq_done, ms_done, root_done, out_done, y_free = k.sem("x2_done"), k.sem("x2_squares"), k.sem("x2_ms"), k.sem("x2_root"), k.sem("out_done"), k.sem("y_free")
        tables = [k.inp[n].rearrange("a e d -> (a e) d") for n in ("peer_u", "peer_v")]
        HALF = PER // TURN

        def number(t, phase, i, b):
            return t * 2 * PER + phase * PER + i * TURN + b

        with nc.Block() as block:

            @block.sync
            def _(sp):
                sp.dma_start(rows[:, 0, :], k.mod_d[0:1, 5 * D:6 * D].to_broadcast([P, D])).then_inc(rows_in, 16)
                sp.dma_start(rows[:, 1, :], k.inp["final_norm_w"][None, :].to_broadcast([P, D])).then_inc(rows_in, 16)

                def load_h2(t):
                    sp.dma_start(h2s[:, :], k.h2_d[ds(t, 1)].rearrange("a p d -> (a p) d")).then_inc(h2_in, 16)

                def store(t):
                    sp.wait_ge(out_done, t + 1)
                    sp.dma_start(k.out[:, ds(t * P, P), :].rearrange("a p d -> (a p) d"), y[:, :]).then_inc(y_free, 16)

                load_h2(0)
                with sp.Fori(1, LT) as t:
                    sp.wait_ge(hid_done, t * HALF)
                    load_h2(t)
                    store(t - 1)
                store(LT - 1)
                sp.wait_ge(y_free, 16 * LT + 16)

            @block.gpsimd
            def _(pool):
                with pool.Fori(0, LT) as t:
                    for phase in range(2):
                        with pool.Fori(0, HALF) as i:
                            for b in range(TURN):
                                slot, bank = b % RING, b // RING
                                hold(k, pool, used, number(t, phase, i, b) + 1)
                                if slot == 0:
                                    src = experts[:, ds(t, 1), ds(i * TURN + b, RING)].rearrange("p a n -> p (a n)")
                                    nc.gpsimd.tensor_copy(idx[:, bank, :], src).then_inc(idx_ready, 1)
                                    hold(k, pool, idx_ready, (t * 2 + phase) * (2 * HALF) + 2 * i + bank + 1)
                                nc.gpsimd.indirect_dma_start(out=ring[:, slot, :], out_offset=None, in_=tables[phase],
                                                             in_offset=bass.IndirectOffsetOnAxis(ap=idx[:, bank, slot:slot + 1], axis=0)).then_inc(row_in[slot], 16)

            @block.scalar
            def _(act):
                with act.Fori(0, LT) as t:
                    act.wait_ge(hid_done, (t + 1) * HALF)
                    nc.scalar.activation(acts[:, :], hid[:, :], ACT.Gelu).then_inc(gelu_done, 1)
                    act.wait_ge(x2_done, t + 1)
                    nc.scalar.activation(y[:, :], x1[:, ds(t, 1), :].rearrange("p a d -> p (a d)"), ACT.Square, accum_out=ss[:, 0:1]).then_inc(sq_done, 1)
                    rsqrt_steps(k, None, act, ss[:, 1:2], ss[:, 2:3], None, (ms_done, t + 1), (root_done, 1), None, None)

            @block.vector
            def _(dve):
                st = Count()
                v = nc.vector
                dve.sem_inc(used, RING)
                dve.sem_inc(y_free, 16)
                dve.wait_ge(rows_in, 32)
                with dve.Fori(0, LT) as t:
                    st.enter(t, 7)
                    xt = x1[:, ds(t, 1), :].rearrange("p a d -> p (a d)")
                    hold(k, dve, h2_in, 16 * t + 16)
                    with dve.Fori(0, HALF) as i:
                        for b in range(TURN):
                            n = number(t, 0, i, b)
                            dve.wait_ge(row_in[b % RING], 16 * ((t * 2 * HALF + i) * (TURN // RING) + b // RING + 1))
                            v.tensor_tensor_reduce(ring[:, b % RING, :], ring[:, b % RING, :], h2s[:, :], 1.0, 0.0, ALU.mult, ALU.add, hid16[:, b:b + 1]).then_inc(used, 1)
                        dve.wait_ge(used, RING + number(t, 0, i, TURN))
                        v.tensor_copy(hid[:, ds(i * TURN, TURN)], hid16[:, :]).then_inc(hid_done, 1)
                        hold(k, dve, hid_done, t * HALF + i + 1)
                    dve.wait_ge(y_free, 16 * t + 16)
                    v.memset(y[:, :], 0.0).then_inc(step, 1)
                    st.up()
                    dve.wait_ge(gelu_done, t + 1)
                    v.tensor_tensor(acts[:, :], acts[:, :], weights[:, ds(t, 1), :].rearrange("p a n -> p (a n)"), ALU.mult).then_inc(step, 1)
                    hold(k, dve, step, st.up())
                    with dve.Fori(0, HALF) as i:
                        for b in range(TURN):
                            n = number(t, 1, i, b)
                            dve.wait_ge(row_in[b % RING], 16 * ((t * 2 * HALF + HALF + i) * (TURN // RING) + b // RING + 1))
                            dve.wait_ge(used, RING + n)
                            v.scalar_tensor_tensor(out=y[:, :], in0=ring[:, b % RING, :], scalar=acts[:, ds(i * TURN + b, 1)], in1=y[:, :], op0=ALU.mult, op1=ALU.add).then_inc(used, 1)
                    dve.wait_ge(used, RING + number(t, 1, HALF, 0))
                    v.tensor_tensor(y[:, :], y[:, :], rows[:, 0, :], ALU.mult).then_inc(step, 1)
                    dve.wait_ge(step, st.up())
                    v.tensor_tensor(xt, xt, y[:, :], ALU.add).then_inc(x2_done, 1)
                    dve.wait_ge(sq_done, t + 1)
                    v.tensor_scalar(ss[:, 1:2], ss[:, 0:1], 1.0 / D, EPS, ALU.mult, ALU.add).then_inc(ms_done, 1)
                    rsqrt_steps(k, dve, None, ss[:, 1:2], ss[:, 2:3], ss[:, 3:4], None, (root_done, t + 1), step, st)
                    v.scalar_tensor_tensor(out=y[:, :], in0=xt, scalar=ss[:, 3:4], in1=rows[:, 1, :], op0=ALU.mult, op1=ALU.mult).then_inc(out_done, 1)
                st.leave(LT)


def pair(k, stack, name, shape, side="left"):
    return [sbuf(k, stack, name + part, shape, F32R, side) for part in ("_high", "_low")]


def build(nc, inputs, consts, out):
    with ExitStack() as stack:
        k = Kernel(nc, stack, inputs, consts, out)
        k.const_sb = const_tables(k, stack, "const_sb", ALWAYS)
        ba = sbuf(k, stack, "beta_decay_cols", [P, NT, 4 * DH])
        with ExitStack() as s:
            sc = sbuf(k, s, "cond_silu", [P, KD, 2])
            hT = pair(k, s, "hT", [P, KD, T])
            with ExitStack() as s2:
                xn = sbuf(k, s2, "xn", [P, NT, D])
                modulation(k, xn, sc)
                turn(k, xn, hT)
            project(k, hT, ba, sc)
        k.give_back_semaphores()
        with ExitStack() as outputs:
            oT = pair(k, outputs, "attn_out_turned", [P, QH, LAT])
            odT = pair(k, outputs, "delta_out_turned", [P, DH, LAT])
            with ExitStack() as mixers:
                masks = const_tables(k, mixers, "mask_tables", MASKS)
                attention(k, oT, masks)
                cols = sbuf(k, mixers, "decay_cols", [P, DH, 8, 2, NT])
                decay_columns(k, ba, cols)
                delta(k, cols, odT)
            k.give_back_semaphores()
            x1 = sbuf(k, stack, "x1", [P, LT, D], side="right")
            mixed = stack.enter_context(ExitStack())
            yT = pair(k, mixed, "yT", [P, D // P, LAT], side="right")
            merge(k, oT, odT, yT, x1)
        residual(k, yT, x1)
        mixed.close()
        experts = sbuf(k, stack, "experts", [P, LT, PH * TOPK], I32, side="right")
        weights = sbuf(k, stack, "expert_weights", [P, LT, PH * TOPK], side="right")
        with ExitStack() as s:
            h2T = pair(k, s, "h2T", [P, KD, LAT])
            second_norm(k, x1, h2T)
            routes(k, h2T, experts, weights)
        k.give_back_semaphores()
        expert_layer(k, x1, experts, weights)


_INS = ["x", "c", "ctx", "c_ctx", "ada_w", "ada_b", "norm1_w", "norm2_w", "w_in", "attn_q_norm", "attn_k_norm",
        "dn_conv_w", "dn_a_log", "dn_dt_bias", "dn_norm_w", "w_branch_attn", "w_branch_dn", "w_out", "peer_w_q",
        "peer_sub_keys", "peer_u", "peer_v", "final_norm_w"]


def kernel(**inputs):
    import concourse.bacc as bacc
    from concourse.bass_utils import run_bass_kernel_spmd

    nc = bacc.Bacc("TRN2", target_bir_lowering=False, num_devices=1)
    arrays, aps = {}, {}
    for name in _INS:
        a = np.ascontiguousarray(inputs[name])
        arrays[f"in_{name}"] = a
        aps[name] = nc.dram_tensor(f"in_{name}", a.shape, F32, kind="ExternalInput").ap()
    tables = constants()
    table = np.concatenate([tables[name] for name in CONST_AT], axis=1)
    arrays["shape_tables"] = table
    consts = nc.dram_tensor("shape_tables", table.shape, F32, kind="ExternalInput").ap()
    out = nc.dram_tensor("out", (1, LAT, D), F32, kind="ExternalOutput").ap()
    build(nc, aps, consts, out)
    r = run_bass_kernel_spmd(nc, [arrays], core_ids=[0])
    return r.results[0]["out"]
```
